# Optimizing a Trainium2 kernel written in Bass

```python
import jax, jax.numpy as jnp
from jax import lax
import numpy as np

D_MODEL = 1024
BATCH = 1
SEQ = 512
DEPTH = 2

GRID_W = 64
CTX_LEN = 256
EPS = 1e-6
N_MOD = 6

N_BRANCH = 4
BRANCH_W = 512

N_HEADS = 8
Q_LORA = 256
KV_LORA = 128
NOPE_DIM = 64
ROPE_DIM = 32
V_DIM = BRANCH_W // N_HEADS
QK_DIM = NOPE_DIM + ROPE_DIM
ROPE_HALF = ROPE_DIM // 2
AXIS_PAIRS = ROPE_DIM // 4
ROPE_THETA = 10000.0
Q_BLOCK = 128
ATTN_SCALE = QK_DIM ** -0.5

CONV_W = BRANCH_W
CONV_K = 3

POOL_WINDOWS = (2, 4, 8, 16)
N_POOL_G = len(POOL_WINDOWS)
POOL_GC = BRANCH_W // N_POOL_G
POOL_W = BRANCH_W

SGU_CHUNK = 128
SGU_G = 4
SGU_GC = BRANCH_W // SGU_G
SGU_W = BRANCH_W

KV_OFF = 0
KR_OFF = KV_OFF + KV_LORA
Q_OFF = KR_OFF + ROPE_DIM
CONV_OFF = Q_OFF + Q_LORA
POOL_OFF = CONV_OFF + 3 * CONV_W
SGU_OFF = POOL_OFF + POOL_W
GATE_OFF = SGU_OFF + 2 * SGU_W
N_IN = GATE_OFF + N_BRANCH * D_MODEL

N_EXPERTS = 16
N_EXPERT_GROUPS = 4
EXPERTS_PER_GROUP = N_EXPERTS // N_EXPERT_GROUPS
GROUP_SCORE_TOPK = 2
TOP_K = 2
EXPERT_FF = 256

kernel_name = "hybrid_parallel_mixer_moe_diffusion_trunk"

def rms_norm(x, g):
    xf = x.astype(jnp.float32)
    y = xf * lax.rsqrt(jnp.mean(xf * xf, axis=-1, keepdims=True) + EPS)
    return (y * g.astype(jnp.float32)).astype(x.dtype)

def modulate(xn, shift, scale):
    return xn * (1.0 + scale) + shift

def axial_rope(length):
    rows = length // GRID_W
    grid = jnp.stack(jnp.meshgrid(jnp.arange(rows), jnp.arange(GRID_W), indexing='ij'), -1)
    grid = grid.reshape(rows * GRID_W, 2).astype(jnp.float32)
    inv_freq = ROPE_THETA ** (-jnp.arange(AXIS_PAIRS, dtype=jnp.float32) / AXIS_PAIRS)
    ang = jnp.concatenate([grid[:, :1] * inv_freq, grid[:, 1:] * inv_freq], -1)
    return jnp.cos(ang), jnp.sin(ang)

def apply_rope(t, cos, sin):
    nope, r = t[..., :NOPE_DIM], t[..., NOPE_DIM:]
    r1, r2 = r[..., :ROPE_HALF], r[..., ROPE_HALF:]
    cs = cos[None, :, None, :].astype(t.dtype)
    sn = sin[None, :, None, :].astype(t.dtype)
    return jnp.concatenate([nope, r1 * cs - r2 * sn, r1 * sn + r2 * cs], -1)

def mla_keys_values(p, kv_a_norm_g, w_ukv, k_norm_g, rope):
    ckv = rms_norm(p[..., KV_OFF:KR_OFF], kv_a_norm_g)
    kv = jnp.einsum('blr,rhe->blhe', ckv, w_ukv)
    k_nope, v = kv[..., :NOPE_DIM], kv[..., NOPE_DIM:]
    k_rope = jnp.broadcast_to(p[..., None, KR_OFF:Q_OFF], k_nope.shape[:-1] + (ROPE_DIM,))
    k = rms_norm(jnp.concatenate([k_nope, k_rope], -1), k_norm_g)
    if rope is not None:
        k = apply_rope(k, *rope)
    return k.transpose(0, 2, 1, 3), v.transpose(0, 2, 1, 3)

def mla_queries(p, q_a_norm_g, w_uq, q_norm_g, rope):
    cq = rms_norm(p[..., Q_OFF:CONV_OFF], q_a_norm_g)
    q = rms_norm(jnp.einsum('blr,rhe->blhe', cq, w_uq), q_norm_g)
    if rope is not None:
        q = apply_rope(q, *rope)
    return q.transpose(0, 2, 1, 3)

def block_attention(q, k, v):
    nb_b, n_h, length, _ = q.shape
    nb = length // Q_BLOCK
    qb = jnp.moveaxis(q.reshape(nb_b, n_h, nb, Q_BLOCK, QK_DIM), 2, 0)

    def one_block(qi):
        s = jnp.einsum('bhqd,bhkd->bhqk', qi, k, preferred_element_type=jnp.float32) * ATTN_SCALE
        pr = jax.nn.softmax(s, axis=-1).astype(v.dtype)
        return jnp.einsum('bhqk,bhkd->bhqd', pr, v)

    o = lax.map(one_block, qb)
    return jnp.moveaxis(o, 0, 2).reshape(nb_b, n_h, length, V_DIM)

def short_conv(u, w):
    return lax.conv_general_dilated(
        u, w[:, None, :].astype(u.dtype), window_strides=(1,), padding=((CONV_K // 2, CONV_K // 2),),
        dimension_numbers=('NWC', 'WIO', 'NWC'), feature_group_count=u.shape[-1])

def pool_branch(p, pool_w, pool_scale):
    nb_b, length, _ = p.shape
    pf = p.astype(jnp.float32)
    cs = jnp.pad(jnp.cumsum(pf, axis=1), ((0, 0), (1, 0), (0, 0)))
    t = jnp.arange(length)
    means = []
    for g, w in enumerate(POOL_WINDOWS):
        lo = jnp.clip(t - w // 2, 0, length)
        hi = jnp.clip(t - w // 2 + w, 0, length)
        csg = cs[..., g * POOL_GC:(g + 1) * POOL_GC]
        cnt = (hi - lo).astype(jnp.float32)[None, :, None]
        means.append((csg[:, hi] - csg[:, lo]) / cnt)
    pooled = (jnp.concatenate(means, -1) - pf).astype(p.dtype)
    mixed = jnp.einsum('blgc,gcd->blgd', pooled.reshape(nb_b, length, N_POOL_G, POOL_GC), pool_w)
    return mixed.reshape(nb_b, length, POOL_W) * pool_scale

def sgu_branch(z, sgu_norm_g, sgu_w, sgu_b):
    z = jax.nn.gelu(z)
    u, v = z[..., :SGU_W], z[..., SGU_W:]
    v = rms_norm(v, sgu_norm_g)
    nb_b, length, _ = v.shape
    vc = v.reshape(nb_b, length // SGU_CHUNK, SGU_CHUNK, SGU_G, SGU_GC)
    mixed = jnp.einsum('gpq,bnqgc->bnpgc', sgu_w, vc) + sgu_b.T[None, None, :, :, None]
    return u * mixed.reshape(nb_b, length, SGU_W)

def branch_merge(p, k_all, v_all, rope, q_a_norm_g, w_uq, q_norm_g, conv_w, pool_w, pool_scale,
                 sgu_norm_g, sgu_w, sgu_b, w_branch, w_o):
    nb_b, length, _ = p.shape
    q = mla_queries(p, q_a_norm_g, w_uq, q_norm_g, rope)
    o = block_attention(q, k_all, v_all)
    br_attn = o.transpose(0, 2, 1, 3).reshape(nb_b, length, BRANCH_W)
    gb, gc, u = jnp.split(p[..., CONV_OFF:POOL_OFF], 3, axis=-1)
    br_conv = gb * short_conv(gc * u, conv_w)
    br_pool = pool_branch(p[..., POOL_OFF:SGU_OFF], pool_w, pool_scale)
    br_sgu = sgu_branch(p[..., SGU_OFF:GATE_OFF], sgu_norm_g, sgu_w, sgu_b)
    gates = jax.nn.sigmoid(p[..., GATE_OFF:].reshape(nb_b, length, N_BRANCH, D_MODEL))
    br = jnp.stack([br_attn, br_conv, br_pool, br_sgu], axis=2)
    merged = jnp.sum(gates * jnp.einsum('blnc,ncd->blnd', br, w_branch), axis=2)
    return merged @ w_o

def grouped_moe(h, router_w, router_b, w1, w3, w2):
    logits = jnp.einsum('bld,de->ble', h, router_w, preferred_element_type=jnp.float32)
    s = jax.nn.sigmoid(logits)
    sb = s + router_b.astype(jnp.float32)
    grp = sb.reshape(sb.shape[:-1] + (N_EXPERT_GROUPS, EXPERTS_PER_GROUP))
    gscore = jnp.sum(lax.top_k(grp, GROUP_SCORE_TOPK)[0], axis=-1)
    gsel = jnp.argmax(gscore, axis=-1)
    in_group = (jnp.arange(N_EXPERTS) // EXPERTS_PER_GROUP) == gsel[..., None]
    _, idx = lax.top_k(jnp.where(in_group, sb, -jnp.inf), TOP_K)
    w = jnp.take_along_axis(s, idx, axis=-1)
    w = w / jnp.sum(w, axis=-1, keepdims=True)
    combine = jnp.sum(jax.nn.one_hot(idx, N_EXPERTS, dtype=jnp.float32) * w[..., None], axis=-2)
    combine = combine.astype(h.dtype)
    y = jnp.zeros_like(h)
    for e in range(N_EXPERTS):
        a = jax.nn.silu(h @ w1[e]) * (h @ w3[e])
        y = y + combine[..., e:e + 1] * (a @ w2[e])
    return y

def setup_inputs(seed: int = 0) -> dict:
    key = jax.random.key(seed)
    ks = iter(jax.random.split(key, 32))
    f32 = jnp.float32

    def nrm(shape, scale):
        return jax.random.normal(next(ks), shape, f32) * scale

    def gain(shape):
        return 1.0 + nrm(shape, 0.05)

    return {
        "x": nrm((BATCH, SEQ, D_MODEL), 1.0),
        "c": nrm((BATCH, D_MODEL), 1.0),
        "ctx": nrm((BATCH, CTX_LEN, D_MODEL), 1.0),
        "c_ctx": nrm((D_MODEL,), 1.0),
        "mod_w": nrm((DEPTH, D_MODEL, N_MOD * D_MODEL), 0.5 * D_MODEL ** -0.5),
        "mod_b": nrm((DEPTH, N_MOD * D_MODEL), 0.01),
        "norm1_g": gain((DEPTH, D_MODEL)),
        "norm2_g": gain((DEPTH, D_MODEL)),
        "w_in": nrm((DEPTH, D_MODEL, N_IN), D_MODEL ** -0.5),
        "kv_a_norm_g": gain((DEPTH, KV_LORA)),
        "w_ukv": nrm((DEPTH, KV_LORA, N_HEADS, NOPE_DIM + V_DIM), KV_LORA ** -0.5),
        "k_norm_g": gain((DEPTH, QK_DIM)),
        "q_a_norm_g": gain((DEPTH, Q_LORA)),
        "w_uq": nrm((DEPTH, Q_LORA, N_HEADS, QK_DIM), Q_LORA ** -0.5),
        "q_norm_g": gain((DEPTH, QK_DIM)),
        "conv_w": nrm((DEPTH, CONV_K, CONV_W), CONV_K ** -0.5),
        "pool_w": nrm((DEPTH, N_POOL_G, POOL_GC, POOL_GC), POOL_GC ** -0.5),
        "pool_scale": gain((DEPTH, POOL_W)),
        "sgu_norm_g": gain((DEPTH, SGU_W)),
        "sgu_w": nrm((DEPTH, SGU_G, SGU_CHUNK, SGU_CHUNK), SGU_CHUNK ** -0.5),
        "sgu_b": gain((DEPTH, SGU_G, SGU_CHUNK)),
        "w_branch": nrm((DEPTH, N_BRANCH, BRANCH_W, D_MODEL), BRANCH_W ** -0.5),
        "w_o": nrm((DEPTH, D_MODEL, D_MODEL), D_MODEL ** -0.5),
        "router_w": nrm((D_MODEL, N_EXPERTS), D_MODEL ** -0.5),
        "router_b": nrm((N_EXPERTS,), 0.01),
        "moe_w1": nrm((DEPTH, N_EXPERTS, D_MODEL, EXPERT_FF), D_MODEL ** -0.5),
        "moe_w3": nrm((DEPTH, N_EXPERTS, D_MODEL, EXPERT_FF), D_MODEL ** -0.5),
        "moe_w2": nrm((DEPTH, N_EXPERTS, EXPERT_FF, D_MODEL), EXPERT_FF ** -0.5),
    }

def reference(x, c, ctx, c_ctx, mod_w, mod_b, norm1_g, norm2_g, w_in, kv_a_norm_g, w_ukv, k_norm_g,
              q_a_norm_g, w_uq, q_norm_g, conv_w, pool_w, pool_scale, sgu_norm_g, sgu_w, sgu_b,
              w_branch, w_o, router_w, router_b, moe_w1, moe_w3, moe_w2):
    nb_b, length, d = x.shape
    rope = axial_rope(length)
    sc = jax.nn.silu(c)
    scc = jax.nn.silu(c_ctx)
    xc = ctx
    for i in range(DEPTH):
        update_ctx = i < DEPTH - 1
        m = (sc @ mod_w[i] + mod_b[i]).reshape(nb_b, N_MOD, 1, d)
        mc = (scc @ mod_w[i] + mod_b[i]).reshape(N_MOD, d)
        h = modulate(rms_norm(x, norm1_g[i]), m[:, 0], m[:, 1])
        hc = modulate(rms_norm(xc, norm1_g[i]), mc[0], mc[1])
        p = h @ w_in[i]
        pc = hc @ (w_in[i] if update_ctx else w_in[i][:, :Q_OFF])
        k_c, v_c = mla_keys_values(pc, kv_a_norm_g[i], w_ukv[i], k_norm_g[i], None)
        k_l, v_l = mla_keys_values(p, kv_a_norm_g[i], w_ukv[i], k_norm_g[i], rope)
        k_all = jnp.concatenate([k_c, k_l], axis=2)
        v_all = jnp.concatenate([v_c, v_l], axis=2)
        mix = branch_merge(p, k_all, v_all, rope, q_a_norm_g[i], w_uq[i], q_norm_g[i], conv_w[i],
                           pool_w[i], pool_scale[i], sgu_norm_g[i], sgu_w[i], sgu_b[i],
                           w_branch[i], w_o[i])
        x = x + m[:, 2] * mix
        h2 = modulate(rms_norm(x, norm2_g[i]), m[:, 3], m[:, 4])
        x = x + m[:, 5] * grouped_moe(h2, router_w, router_b, moe_w1[i], moe_w3[i], moe_w2[i])
        if update_ctx:
            mix_c = branch_merge(pc, k_c, v_c, None, q_a_norm_g[i], w_uq[i], q_norm_g[i], conv_w[i],
                                 pool_w[i], pool_scale[i], sgu_norm_g[i], sgu_w[i], sgu_b[i],
                                 w_branch[i], w_o[i])
            xc = xc + mc[2] * mix_c
            hc2 = modulate(rms_norm(xc, norm2_g[i]), mc[3], mc[4])
            xc = xc + mc[5] * grouped_moe(hc2, router_w, router_b, moe_w1[i], moe_w3[i], moe_w2[i])
    return x


_drawn_inputs = setup_inputs


def setup_inputs(seed=0):
    import zlib

    import numpy as np

    out = dict(_drawn_inputs(seed))
    spreads = {}
    factors = {'kv_a_norm_g': 6.014,
     'k_norm_g': 5.859,
     'q_a_norm_g': 5.861,
     'q_norm_g': 6.291,
     'sgu_norm_g': 3.102,
     'sgu_b': 2.715}
    for name, (base, spread) in spreads.items():
        noise = np.random.default_rng([zlib.crc32(name.encode()), seed]).standard_normal(out[name].shape)
        drawn = base * np.exp(spread * noise) if base else spread * noise
        out[name] = __import__('jax').numpy.asarray(drawn.astype(out[name].dtype))
    for name, factor in factors.items():
        out[name] = (out[name] * factor).astype(out[name].dtype)
    return out
```

```python
from contextlib import ExitStack

import numpy as np
import concourse.bass as bass
from concourse import mybir

F32 = mybir.dt.float32
I32 = mybir.dt.int32
ALU = mybir.AluOpType
ACT = mybir.ActivationFunctionType
AX = mybir.AxisListType

P = 128
D = 1024
KD = D // P
DEPTH = 2
SEQ = 512
CTX = 256
TOK = SEQ + CTX
LT = SEQ // P
AT = TOK // P
N_MOD = 6
MC = N_MOD * KD
EPS = 1e-6
GRID_W = 64

BW = 512
BC = BW // P
H = 8
NOPE, ROPE, VD = 64, 32, 64
QK = NOPE + ROPE
HALF = ROPE // 2
AXIS_PAIRS = ROPE // 4
KV_LORA, Q_LORA = 128, 256
SCALE = QK ** -0.5

KR_OFF = KV_LORA
Q_OFF = KR_OFF + ROPE
CONV_OFF = Q_OFF + Q_LORA
POOL_OFF = CONV_OFF + 3 * BW
SGU_OFF = POOL_OFF + BW
GATE_OFF = SGU_OFF + 2 * BW
WINDOWS = (2, 4, 8, 16)

NE, NG = 16, 4
EG = NE // NG
FF = 256
BIG = 1.0e30

SLOTS = 6
SLAB = 2048
MAXB = (2 * TOK + NE * (P - 1)) // P

CVL, CVC, CVW = 1, 1 + SEQ + 2, SEQ + CTX + 4
PP = 8
PLL, PLC, PLW = PP, PP + SEQ + 2 * PP, SEQ + CTX + 4 * PP


def expert_blocks(tokens):
    return (2 * tokens + NE * (P - 1)) // P


def signals(name):
    steps, blocks = H * AT, expert_blocks(TOK)
    rounds = H * ((2 * AT + 3) // 4)
    once = "eid n1_eps n1_rt n2_eps n2_rt po_pad r_oh r_s rank_ps slots tab_i tab_ps wT wT_tr"
    by_tile = ("cn cnT cn_tr h2T h2_tok h2_tr hT_tile h_tok h_tr lg_ps n1_sq n2_sq raw sgv sgv_stat t_eps t_hrt t_qk "
               "t_rn t_rt t_sq t_sqd t_ss tproj up w_ps w_x x_new yg_free")
    by_chunk = "at_br cv_br cv_cu o_tr po_br po_mix po_pl po_pp po_ps sgu_mix sgu_out sgu_ps sgu_u"
    by_step = "negmax o_ps o_sb prT_d pr_tr probs s_ps"
    by_block = "aT_ps aT_sb a_sb h_ps sil y_ps y_sb"
    counts = {
        **dict.fromkeys(once.split(), 1), **dict.fromkeys(by_tile.split(), AT), **dict.fromkeys(by_chunk.split(), BC),
        **dict.fromkeys(by_step.split(), steps), "prT_a": H * LT, **dict.fromkeys(by_block.split(), blocks),
        **dict.fromkeys(("b_ps", "g_prod", "g_ps", "g_sig"), 4 * KD), **dict.fromkeys(("qkT", "qk_tr"), rounds),
        **dict.fromkeys(("idx", "xT_ps", "xgT"), blocks + 1),
        "cv_evac": 2 * BC, "cv_ps": 3 * BC,
        "h2_st0": 16 * (AT // 2), "h2_st1": 16 * (AT // 2), "par_b": 16 * 7, "par_g": 32, "par_n1": 48, "par_n2": 48,
        "par_p": 16, "par_sb": 16, "tab_ld": 16, "tab_st": 16 * 2 * AT, "x_back": 16 * AT,
        "xg0": 16 * (blocks // 2 + 1), "xg1": 16 * ((blocks + 1) // 2),
        "y_st0": 16 * ((blocks + 1) // 2), "y_st1": 16 * (blocks // 2), "yg0": 16 * AT, "yg1": 16 * AT,
    }
    return counts[name]


def latent_steps(n, nt):
    return n // nt * LT + min(n % nt, LT)


def rope_tables():
    t = np.arange(SEQ)
    grid = np.stack([t // GRID_W, t % GRID_W], -1).astype(np.float32)
    inv = (np.float32(10000.0) ** (-np.arange(AXIS_PAIRS, dtype=np.float32) / np.float32(AXIS_PAIRS))).astype(np.float32)
    ang = np.concatenate([grid[:, :1] * inv, grid[:, 1:] * inv], -1).astype(np.float32).astype(np.float64)
    tabs = [np.concatenate([f(ang), f(ang)], -1).astype(np.float32) for f in (np.cos, np.sin)]
    return np.ascontiguousarray(np.stack([x.reshape(LT, P, ROPE).transpose(1, 0, 2) for x in tabs], 1))


def pool_edges():
    rows = []
    for w in WINDOWS:
        first = [w / (min(j + w - w // 2, w)) for j in range(PP)]
        last = [w / (min(PP - j, w - w // 2) + w // 2) for j in range(PP)]
        rows.append(first + last)
    return np.asarray(rows, np.float32)


def trunk(nc, A, out):
    mod_rows = nc.dram_tensor("mod_rows", [DEPTH, 2, N_MOD * D], F32, kind="Internal").ap()
    x_spill = nc.dram_tensor("x_spill", [TOK, D], F32, kind="Internal").ap()
    h2_rows = nc.dram_tensor("h2_rows", [TOK, D], F32, kind="Internal").ap()
    token_of = [nc.dram_tensor(f"token_of_{l}", [(MAXB + 1) * P, 1], F32, kind="Internal").ap() for l in range(DEPTH)]
    y_rows = [nc.dram_tensor(f"y_rows_{l}", [expert_blocks(SEQ if l else TOK) * P, D], F32, kind="Internal").ap()
              for l in range(DEPTH)]

    with ExitStack() as ctx:
        def sb(name, width, parts=P, dt=F32):
            return ctx.enter_context(nc.sbuf_tensor(name, [parts, width], dt))

        X = sb("X", AT * D)
        HT = sb("HT", KD * TOK)
        BRA = sb("BRA", BC * TOK)
        BRB = sb("BRB", BC * TOK)
        MG = sb("MG", KD * TOK)
        QKB = sb("QKB", AT * 2 * H * QK)
        VB = sb("VB", AT * BW)
        RING = sb("RING", SLOTS * SLAB)
        T = sb("T", 2304)
        PW = sb("PW", BC * P)
        ident = sb("ident", P)
        cw = sb("cw", 16)
        edge = sb("edge", 4 * 2 * PP)
        st = sb("st", 3 * AT)
        rst = sb("rst", 3 * AT)
        srt = sb("srt", 3 * AT)
        scT = sb("scT", 2 * KD)
        ps = ctx.enter_context(nc.psum_tensor("ps", [P, 4, 1024], F32))

        def W(l):
            return TOK if l < DEPTH - 1 else SEQ

        def tiles(l):
            return W(l) // P

        x_t = X[:, :].rearrange("p (t d) -> p t d", t=AT)
        hT = HT[:, :].rearrange("p (k t) -> p k t", k=KD)
        brA = BRA[:, :].rearrange("p (c t) -> p c t", c=BC)
        brB = BRB[:, :].rearrange("p (c t) -> p c t", c=BC)
        sgv = BRA[:, :].rearrange("p (t c) -> p t c", t=AT)
        merged = MG[:, :].rearrange("p (k t) -> p k t", k=KD)
        qk = QKB[:, :].rearrange("p (t s h e) -> p t s h e", t=AT, s=2, h=H)
        vb = VB[:, :].rearrange("p (t c) -> p t c", t=AT)
        poolw = PW[:, :].rearrange("p (g d) -> p g d", g=BC)

        def slot(s):
            return RING[:, s * SLAB:(s + 1) * SLAB]

        def slot3(s, a):
            return slot(s).rearrange("p (a n) -> p a n", a=a)

        def psb(i):
            return ps[:, i, :]

        def shift1(v):
            return MG[:, v * 2 * D:v * 2 * D + D]

        def scale1(v):
            return MG[:, v * 2 * D + D:(v + 1) * 2 * D]

        gain1 = MG[:, 4 * D:5 * D]
        sgub = MG[:, 5 * D:5 * D + BW]
        sguwT = MG[:, 5 * D + BW:6 * D].rearrange("p (g q) -> p g q", g=BC)
        htok = [BRA[:, j * D:(j + 1) * D] for j in range(2)]
        g_kva = BRB[:, 0:128]
        g_qa = BRB[:, 128:384]
        g_qk = BRB[:, 384:384 + 2 * QK].rearrange("p (s e) -> p s e", s=2)
        g_sgu = BRB[:, 576:576 + BW]
        sguw = BRB[:, 1088:1088 + BW].rearrange("p (g q) -> p g q", g=BC)
        crow = BRB[0:16, 1600:1728]
        cn = [T[:, j * 384:(j + 1) * 384] for j in range(2)]
        cnT = [T[:, 768 + j * 384:768 + (j + 1) * 384] for j in range(2)]
        cosv = T[:, 1536:1536 + LT * ROPE].rearrange("p (t e) -> p t e", t=LT)
        sinv = T[:, 1664:1664 + LT * ROPE].rearrange("p (t e) -> p t e", t=LT)
        ssq = [T[:, 1792 + j * 16:1808 + j * 16] for j in range(2)]
        rsq = [T[:, 1824 + j * 16:1840 + j * 16] for j in range(2)]
        raw = [X[:, j * 1536:(j + 1) * 1536].rearrange("p (s h e) -> p s h e", s=2, h=H) for j in range(2)]
        sqb = [X[:, 3072 + j * 1536:3072 + (j + 1) * 1536] for j in range(2)]
        uT = [X[:, j * TOK:(j + 1) * TOK] for j in range(2)]
        umix = X[:, 2 * TOK:3 * TOK]
        gcs = [X[:, j * TOK:(j + 1) * TOK] for j in range(2)]
        gbs = [X[:, (2 + j) * TOK:(3 + j) * TOK] for j in range(2)]
        cup = [X[:, 4 * TOK + j * CVW:4 * TOK + (j + 1) * CVW] for j in range(2)]
        cvy = X[:, 4 * TOK + 2 * CVW:4 * TOK + 3 * CVW]
        pp = [X[:, j * PLW:(j + 1) * PLW] for j in range(2)]
        pacc = [X[:, (2 + j) * PLW:(3 + j) * PLW] for j in range(2)]
        pooled = [X[:, 4 * PLW + j * TOK:4 * PLW + (j + 1) * TOK] for j in range(2)]
        obuf = X[:, 0:AT * BW].rearrange("p (t c) -> p t c", t=AT)
        qkT = [X[:, 3072 + j * 1536:3072 + (j + 1) * 1536] for j in range(2)]
        probs = [BRB[:, j * TOK:(j + 1) * TOK] for j in range(2)]
        prT = [BRB[:, (2 + j) * TOK:(3 + j) * TOK] for j in range(2)]
        negm = T[:, 0:H * AT]
        rsum = T[:, 64:64 + H * AT]
        rinv = T[:, 128:128 + H * AT]
        sig = [T[:, j * TOK:(j + 1) * TOK] for j in range(2)]
        prod = T[:, 2 * TOK:3 * TOK]
        mrow = QKB[:, 0:2 * 4 * D].rearrange("p (v m d) -> p v m d", v=2, m=4)
        gain2 = QKB[:, 8 * D:9 * D]
        wtmp = T[:, 0:D]
        h2tok = htok
        h2T = [HT[:, j * D:(j + 1) * D].rearrange("p (k t) -> p k t", k=KD) for j in range(2)]
        junk = BRB[:, 0:D]
        xg = htok
        xgT = h2T
        sil = [HT[:, 2 * D + j * FF:2 * D + (j + 1) * FF] for j in range(2)]
        act_a = [HT[:, 2 * D + (2 + j) * FF:2 * D + (3 + j) * FF] for j in range(2)]
        act_T = [HT[:, 3 * D + j * FF:3 * D + (j + 1) * FF].rearrange("p (k t) -> p k t", k=2) for j in range(2)]
        ysb = [MG[:, j * D:(j + 1) * D] for j in range(2)]
        yg = [[MG[:, (2 * j + k) * D:(2 * j + k + 1) * D] for k in range(2)] for j in range(2)]
        ytmp = HT[:, 4 * D:5 * D]
        cursor = [D]

        def rt(*shape):
            n = int(np.prod(shape))
            a = BRB[:, cursor[0]:cursor[0] + n]
            cursor[0] += n
            if len(shape) == 1:
                return a
            names = "abcd"[:len(shape)]
            return a.rearrange(f"p ({' '.join(names)}) -> p {' '.join(names)}",
                               **{n_: s for n_, s in zip(names[:-1], shape[:-1])})

        r_s, r_sb, r_m, r_sc = rt(AT, NE), rt(AT, NE), rt(AT, NE), rt(AT, NE)
        r_oh = [rt(AT, NE), rt(AT, NE)]
        r_pair = rt(AT * NG, 6)
        r_gs, r_gq, r_gm = rt(AT, NG), rt(AT, NG), rt(AT, NG)
        r_mx = rt(AT)
        r_w = [rt(AT), rt(AT)]
        r_den = rt(AT)
        r_cnt = rt(NE, 6)
        r_nb, r_end, r_base = rt(NE), rt(NE), rt(NE)
        r_slot = rt(2, AT)
        r_blk = rt(MAXB, NE)
        r_eid = rt(MAXB)
        assert cursor[0] <= BC * TOK
        slot_i = sb("slot_i", 2 * AT, dt=I32)
        eid_i = sb("eid_i", MAXB + 1, dt=I32)
        tab_i = sb("tab_i", MAXB + 1, dt=I32)
        idx_i = [sb(f"idx_i{j}", 1, dt=I32) for j in range(2)]
        tabr = T[0:MAXB + 1, 0:P]
        gw = [r_w[0], r_w[1]]
        rw = sb("rw", KD * NE)
        rwv = rw[:, :].rearrange("p (k e) -> p k e", k=KD)
        rbias = sb("rbias", NE)
        ones = sb("ones", P)
        tri = sb("tri", P)
        w4 = sb("w4", NG)
        w16 = sb("w16", NE)
        steps6 = sb("steps6", 6)
        blkno = sb("blkno", MAXB)
        tokf = sb("tokf", AT)
        zrow = sb("zrow", MAXB + 1)
        iint = sb("iint", 64, dt=I32)

        sems = {}

        def S(name):
            if name not in sems:
                sems[name] = ctx.enter_context(nc.semaphore(name))
            return sems[name]

        def at(name, l, n):
            return n + (signals(name) if l else 0)

        slab_full = [S(f"slab_full{s}") for s in range(SLOTS)]
        slab_used = S("slab_used")

        def cols(w, c0, n):
            return w[:, c0:c0 + n].rearrange("(k p) n -> p k n", p=P)

        def win(l, c0, n=256):
            return (KD, n, cols(A["w_in"][l], c0, n))

        def gate_slabs(l, n):
            g = GATE_OFF + n * D
            wb = A["w_branch"][l, n]
            half = [(BC, 512, wb[:, j * 512:(j + 1) * 512].rearrange("(k p) n -> p k n", p=P)) for j in range(2)]
            return [win(l, g), half[0], win(l, g + 256), win(l, g + 512), half[1], win(l, g + 768)]

        def token_slabs(l):
            r = [win(l, 0), win(l, 256, CONV_OFF - 256), win(l, SGU_OFF + BW), win(l, SGU_OFF + BW + 256)]
            r.append((1, D, A["w_ukv"][l].rearrange("p (a h) e -> p a (h e)", a=1)))
            r.append((2, H * QK, A["w_uq"][l].rearrange("(k p) h e -> p k (h e)", p=P)))
            return r

        def straight_slabs(l):
            r = token_slabs(l)
            r += [win(l, SGU_OFF), win(l, SGU_OFF + 256)]
            r += gate_slabs(l, 3)
            for j in range(2):
                for part in (1, 0, 2):
                    r.append(win(l, CONV_OFF + part * BW + j * 256))
            r += gate_slabs(l, 1)
            r += [win(l, POOL_OFF), win(l, POOL_OFF + 256)]
            r += gate_slabs(l, 2)
            r += gate_slabs(l, 0)
            r += [(KD, 256, cols(A["w_o"][l], j * 256, 256)) for j in range(4)]
            return r

        block = ctx.enter_context(nc.Block())

        @block.sync
        def _(sp):
            issued = [0]

            def load(shape, src, before=None, at=None):
                n = issued[0] if at is None else at
                if n >= SLOTS or before is not None:
                    need = n - SLOTS + 1
                    sp.wait_ge(slab_used, need if before is None else before + need)
                a, m = shape
                sp.dma_start(slot(n % SLOTS)[:, 0:a * m].rearrange("p (a m) -> p a m", a=a), src)\
                    .then_inc(slab_full[n % SLOTS], 16)
                if at is None:
                    issued[0] += 1

            def mod_cols(l, c0):
                return A["mod_w"][l][:, c0].rearrange("(k p) n -> p k n", p=P)

            for j in range(SLOTS):
                load((KD, 256), mod_cols(0, slice(j * 256, (j + 1) * 256)))
            for l in range(DEPTH):
                start = 1 if l == 0 else 0
                turn0 = l * MC // 2
                with sp.Fori(start, MC // (2 * SLOTS)) as i:
                    for j in range(SLOTS):
                        load((KD, 256), mod_cols(l, bass.ds(i * (256 * SLOTS) + j * 256, 256)), i * SLOTS, turn0 + j)
                issued[0] = (l + 1) * MC // 2

            for l in range(DEPTH):
                for a, m, src in straight_slabs(l):
                    load((a, m), src)
                nb = expert_blocks(W(l))
                w1, w3, w2 = A["moe_w1"][l], A["moe_w3"][l], A["moe_w2"][l]
                sp.wait_ge(S("eid"), at("eid", l, 1))

                def up(b, n, before=None):
                    e = sp.value_load(eid_i[0:1, b] if before is None else eid_i[0:1, bass.ds(b, 1)],
                                      min_val=0, max_val=NE - 1)
                    for w in (w1, w3):
                        load((KD, FF), w[bass.ds(e, 1)].rearrange("e (k p) n -> p (e k) n", p=P), before, n)
                        n = None if n is None else n + 1

                def down(b, n, before=None):
                    e = sp.value_load(eid_i[0:1, b] if before is None else eid_i[0:1, bass.ds(b, 1)],
                                      min_val=0, max_val=NE - 1)
                    load((2, D), w2[bass.ds(e, 1)].rearrange("e (k p) n -> p (e k) n", p=P), before, n)

                up(slice(0, 1), None)
                for b in (1, 2):
                    up(slice(b, b + 1), None)
                    down(slice(b - 1, b), None)
                n0 = issued[0]
                with sp.Fori(0, (nb - 3) // 2) as i:
                    for j in range(2):
                        up(i * 2 + (3 + j), n0 + 3 * j, i * SLOTS)
                        down(i * 2 + (2 + j), n0 + 3 * j + 2, i * SLOTS)
                issued[0] += 3 * (nb - 3)
                down(slice(nb - 1, nb), None)
            sp.wait_ge(S("x_stored"), 16 * LT)

        @block.tensor
        def _(pe):
            used = [0]
            owed = [0]
            mm = pe.matmul

            def pays(ins):
                if owed[0]:
                    ins.then_inc(slab_used, owed[0])
                    owed[0] = 0

            def arrived():
                n = used[0]
                pe.wait_ge(slab_full[n % SLOTS], 16 * (n // SLOTS + 1))
                used[0] += 1
                return n % SLOTS

            def chunk(l, wcols, bank):
                last = None
                for k in range(KD):
                    last = mm(psb(bank)[:, 0:SEQ], wcols[:, k, :], hT[:, k, 0:SEQ], start=(k == 0), stop=(k == KD - 1))
                    if k == 0:
                        pays(last)
                    if W(l) > SEQ:
                        last = mm(psb(bank)[:, SEQ:TOK], wcols[:, k, :], hT[:, k, SEQ:TOK],
                                  start=(k == 0), stop=(k == KD - 1))
                return last

            pe.wait_ge(S("const"), 2)
            pe.wait_ge(S("c_silu"), 1)
            pe.transpose(psb(3)[:, 0:2 * KD], T[0:2 * KD, 0:P], ident[0:2 * KD, 0:2 * KD]).then_inc(S("c_tr"), 1)
            pe.wait_ge(S("c_col"), 1)
            for l in range(DEPTH):
                n0 = used[0]
                with pe.Fori(0, MC // (2 * SLOTS)) as i:
                    for j in range(SLOTS):
                        s = (n0 + j) % SLOTS
                        pe.wait_ge(slab_full[s], i * 16 + 16 * ((n0 + j) // SLOTS + 1))
                        for c in range(2):
                            o = psb(l)[:, 0:2 * MC].rearrange("p (v c) -> p v c", v=2)[:, :, bass.ds(i * (2 * SLOTS) + (2 * j + c), 1)]
                            for k in range(KD):
                                last = mm(o, slot3(s, KD)[:, k, c * P:(c + 1) * P],
                                          scT[:, :].rearrange("p (v k) -> p v k", v=2)[:, :, k],
                                          start=(k == 0), stop=(k == KD - 1))
                        last.then_inc(slab_used, 1)
                used[0] += MC // 2
                pe.wait_ge(S("mod_sb"), l + 1)
                pe.transpose(psb(2)[0:2 * MC, l * 512:l * 512 + P], HT[:, l * 2 * MC:(l + 1) * 2 * MC], ident[:, :])\
                    .then_inc(S("mod_tr"), 1)

            for l in range(DEPTH):
                NT = tiles(l)
                for t in range(AT):
                    pe.wait_ge(S("h_tok"), at("h_tok", l, t + 1))
                    if t >= 2:
                        pe.wait_ge(S("hT_tile"), at("hT_tile", l, t - 1))
                    for k in range(KD):
                        last = pe.transpose(psb(t % 2)[:, k * P:(k + 1) * P], htok[t % 2][:, k * P:(k + 1) * P], ident[:, :])
                        if k == 0:
                            pays(last)
                    last.then_inc(S("h_tr"), 1)

                pe.wait_ge(S("hT_tile"), at("hT_tile", l, AT))
                tslot = [arrived() for _ in range(6)]
                wkv, wq, wv0, wv1 = (slot3(s, KD) for s in tslot[:4])
                wq = slot(tslot[1])[:, 0:KD * 160].rearrange("p (k n) -> p k n", k=KD)
                wukv = slot(tslot[4])[:, 0:D]
                wuq = slot(tslot[5])[:, 0:2 * H * QK].rearrange("p (k n) -> p k n", k=2)

                def project(t):
                    if t >= 2:
                        pe.wait_ge(S("cnT"), at("cnT", l, t - 1))
                        if t - 2 < NT:
                            pe.wait_ge(S("sgv_stat"), at("sgv_stat", l, t - 1))
                    b = psb(t % 2)
                    full = t < NT
                    parts = [(wkv, 0, 256 if full else Q_OFF, 0)]
                    if full:
                        parts += [(wq, 0, 160, 256), (wv0, 0, 256, 512), (wv1, 0, 256, 768)]
                    for w, _, n, o in parts:
                        for k in range(KD):
                            last = mm(b[:, o:o + n], hT[:, k, t * P:(t + 1) * P], w[:, k, 0:n],
                                      start=(k == 0), stop=(k == KD - 1))
                    last.then_inc(S("tproj"), 1)

                def low_rank(t):
                    full = t < NT
                    b = psb(t % 2)
                    pe.wait_ge(S("cn"), at("cn", l, t + 1))
                    for j in range(3 if full else 1):
                        last = pe.transpose(b[:, j * P:(j + 1) * P], cn[t % 2][:, j * P:(j + 1) * P], ident[:, :])
                    last.then_inc(S("cn_tr"), 1)
                    pe.wait_ge(S("cnT"), at("cnT", l, t + 1))
                    if t >= 1:
                        pe.wait_ge(S("raw"), at("raw", l, t))
                    for j in range(2):
                        last = mm(psb(2)[:, j * 512:(j + 1) * 512], cnT[t % 2][:, 0:P], wukv[:, j * 512:(j + 1) * 512],
                                  start=True, stop=True)
                    if full:
                        for j in range(2):
                            for k in range(2):
                                last = mm(psb(3)[:, j * 512:j * 512 + 384], cnT[t % 2][:, (1 + k) * P:(2 + k) * P],
                                          wuq[:, k, j * 384:(j + 1) * 384], start=(k == 0), stop=(k == 1))
                    last.then_inc(S("up"), 1)

                for t in range(AT + 1):
                    if t < AT:
                        project(t)
                    if t >= 1:
                        low_rank(t - 1)
                owed[0] += 6
                pe.wait_ge(S("raw"), at("raw", l, AT))
                pe.wait_ge(S("par_b"), at("par_b", l, 16 * 7))
                for g in range(BC):
                    pays(pe.transpose(psb(2)[:, g * P:(g + 1) * P], sguw[:, g, :], ident[:, :]))
                pe.transpose(psb(2)[:, 512:528], crow, ident[0:16, 0:16]).then_inc(S("wT_tr"), 1)

                pe.wait_ge(S("cnT"), at("cnT", l, AT))
                pe.wait_ge(S("sgv_stat"), at("sgv_stat", l, NT))
                us = [arrived(), arrived()]
                for g in range(BC):
                    if g >= 2:
                        pe.wait_ge(S("sgu_u"), at("sgu_u", l, g - 1))
                    last = chunk(l, slot3(us[g // 2], KD)[:, :, (g % 2) * P:(g % 2 + 1) * P], g % 2)
                    last.then_inc(S("sgu_ps"), 1)
                    owed[0] += g % 2
                    if g == 0:
                        pe.wait_ge(S("sgv"), at("sgv", l, NT))
                        pe.wait_ge(S("wT"), at("wT", l, 1))
                    if g % 2 == 0:
                        continue
                    for gg in (g - 1, g):
                        if gg >= 2:
                            pe.wait_ge(S("sgu_out"), at("sgu_out", l, gg - 1))
                        for t in range(NT):
                            last = mm(psb(2 + gg % 2)[:, t * P:(t + 1) * P], sgv[:, t, gg * P:(gg + 1) * P], sguwT[:, gg, :],
                                      start=True, stop=True)
                            if t == 0:
                                pays(last)
                        last.then_inc(S("sgu_mix"), 1)

                def gated(q, br):
                    slabs = {}
                    for d in range(KD):
                        u = q * KD + d
                        if d % 2 == 0:
                            slabs["g"] = arrived()
                            if d % 4 == 0:
                                slabs["b"] = arrived()
                        if d >= 2:
                            pe.wait_ge(S("g_sig"), at("g_sig", l, u - 1))
                        last = chunk(l, slot3(slabs["g"], KD)[:, :, (d % 2) * P:(d % 2 + 1) * P], u % 2)
                        last.then_inc(S("g_ps"), 1)
                        if d >= 2:
                            pe.wait_ge(S("g_prod"), at("g_prod", l, u - 1))
                        wb = slot3(slabs["b"], BC)[:, :, (d % 4) * P:(d % 4 + 1) * P]
                        for k in range(BC):
                            last = mm(psb(2 + u % 2)[:, 0:SEQ], wb[:, k, :], br[:, k, 0:SEQ], start=(k == 0), stop=(k == BC - 1))
                            if W(l) > SEQ:
                                last = mm(psb(2 + u % 2)[:, SEQ:TOK], wb[:, k, :], br[:, k, SEQ:TOK],
                                          start=(k == 0), stop=(k == BC - 1))
                        last.then_inc(S("b_ps"), 1)
                        if d % 4 == 1:
                            owed[0] += 1
                        elif d % 4 == 3:
                            owed[0] += 2

                pe.wait_ge(S("sgu_u"), at("sgu_u", l, BC))
                pe.wait_ge(S("sgu_out"), at("sgu_out", l, BC))
                gated(0, brB)

                pe.wait_ge(S("g_sig"), at("g_sig", l, KD))
                pe.wait_ge(S("g_prod"), at("g_prod", l, KD))
                for c in range(BC):
                    if c % 2 == 0:
                        cs = [arrived() for _ in range(3)]
                    for j in range(3):
                        w = 3 * c + j
                        if w >= 4:
                            pc, pj = divmod(w - 4, 3)
                            if pj < 2:
                                pe.wait_ge(S("cv_evac"), at("cv_evac", l, 2 * pc + pj + 1))
                            else:
                                pe.wait_ge(S("cv_cu"), at("cv_cu", l, pc + 1))
                        chunk(l, slot3(cs[j], KD)[:, :, (c % 2) * P:(c % 2 + 1) * P], w % 4).then_inc(S("cv_ps"), 1)
                    owed[0] += 3 * (c % 2)
                pe.wait_ge(S("cv_evac"), at("cv_evac", l, 2 * BC))
                pe.wait_ge(S("cv_br"), at("cv_br", l, BC))
                gated(1, brA)

                pe.wait_ge(S("g_sig"), at("g_sig", l, 2 * KD))
                pe.wait_ge(S("g_prod"), at("g_prod", l, 2 * KD))
                pe.wait_ge(S("par_p"), at("par_p", l, 16))
                for g in range(BC + 1):
                    if g < BC:
                        if g % 2 == 0:
                            s = arrived()
                        if g >= 2:
                            pe.wait_ge(S("po_pp"), at("po_pp", l, g - 1))
                        last = chunk(l, slot3(s, KD)[:, :, (g % 2) * P:(g % 2 + 1) * P], g % 2)
                        last.then_inc(S("po_ps"), 1)
                        owed[0] += g % 2
                    if g >= 1:
                        h = g - 1
                        pe.wait_ge(S("po_pl"), at("po_pl", l, h + 1))
                        if h >= 2:
                            pe.wait_ge(S("po_br"), at("po_br", l, h - 1))
                        last = mm(psb(2 + h % 2)[:, 0:SEQ], poolw[:, h, :], pooled[h % 2][:, 0:SEQ], start=True, stop=True)
                        if W(l) > SEQ:
                            last = mm(psb(2 + h % 2)[:, SEQ:TOK], poolw[:, h, :], pooled[h % 2][:, SEQ:TOK], start=True, stop=True)
                        last.then_inc(S("po_mix"), 1)
                pe.wait_ge(S("po_br"), at("po_br", l, BC))
                gated(2, brB)

                pe.wait_ge(S("g_sig"), at("g_sig", l, 3 * KD))
                pe.wait_ge(S("g_prod"), at("g_prod", l, 3 * KD))
                pe.wait_ge(S("t_qk"), at("t_qk", l, AT))
                steps = [(h, t) for h in range(H) for t in range(NT)]
                rounds = (AT + NT + 3) // 4

                def transposes(h, r):
                    n = h * rounds + r
                    if n >= 1:
                        pe.wait_ge(S("qkT"), at("qkT", l, n))
                    for i in range(4 * r, min(4 * r + 4, AT + NT)):
                        src = qk[:, i, 0, h, :] if i < AT else qk[:, i - AT, 1, h, :]
                        last = pe.transpose(psb(3)[0:QK, 512 + (i % 4) * P:512 + (i % 4 + 1) * P], src, ident[:, :])
                    last.then_inc(S("qk_tr"), 1)

                def key_tiles(t):
                    return range(0, AT) if t < LT else range(LT, AT)

                for r in range(rounds):
                    transposes(0, r)
                for n in range(len(steps) + 2):
                    if n < len(steps):
                        h, t = steps[n]
                        if t == 0:
                            pe.wait_ge(S("qkT"), at("qkT", l, (h + 1) * rounds))
                        if n >= 2:
                            pe.wait_ge(S("probs"), at("probs", l, n - 1))
                        q = qkT[h % 2][0:QK, (AT + t) * P:(AT + t + 1) * P]
                        if t < LT:
                            mm(psb(n % 2)[:, 0:SEQ], q, qkT[h % 2][0:QK, 0:SEQ], start=True, stop=True)
                        mm(psb(n % 2)[:, SEQ:TOK], q, qkT[h % 2][0:QK, SEQ:TOK], start=True, stop=True)\
                            .then_inc(S("s_ps"), 1)
                        if h + 1 < H and t < rounds:
                            transposes(h + 1, t)
                    if 1 <= n <= len(steps):
                        m = n - 1
                        h, t = steps[m]
                        pe.wait_ge(S("probs"), at("probs", l, m + 1))
                        if m >= 1:
                            pe.wait_ge(S("prT_a"), at("prT_a", l, latent_steps(m, NT)))
                            pe.wait_ge(S("prT_d"), at("prT_d", l, m))
                        for kt in key_tiles(t):
                            last = pe.transpose(psb(2)[:, kt * P:(kt + 1) * P], probs[m % 2][:, kt * P:(kt + 1) * P], ident[:, :])
                        last.then_inc(S("pr_tr"), 1)
                    if n >= 2:
                        m = n - 2
                        h, t = steps[m]
                        pe.wait_ge(S("prT_a"), at("prT_a", l, latent_steps(m + 1, NT)))
                        pe.wait_ge(S("prT_d"), at("prT_d", l, m + 1))
                        if m >= 1:
                            pe.wait_ge(S("o_sb"), at("o_sb", l, m))
                        ks = list(key_tiles(t))
                        for kt in ks:
                            last = mm(psb(3)[:, (m % 2) * VD:(m % 2 + 1) * VD], prT[m % 2][:, kt * P:(kt + 1) * P],
                                      vb[:, kt, h * VD:(h + 1) * VD], start=(kt == ks[0]), stop=(kt == ks[-1]))
                        last.then_inc(S("o_ps"), 1)
                pe.wait_ge(S("o_sb"), at("o_sb", l, len(steps)))
                for c in range(BC):
                    if c >= 2:
                        pe.wait_ge(S("at_br"), at("at_br", l, c - 1))
                    for t in range(NT):
                        last = pe.transpose(psb(c % 2)[:, t * P:(t + 1) * P], obuf[:, t, c * P:(c + 1) * P], ident[:, :])
                    last.then_inc(S("o_tr"), 1)
                pe.wait_ge(S("at_br"), at("at_br", l, BC))
                gated(3, brA)

                pe.wait_ge(S("g_sig"), at("g_sig", l, 4 * KD))
                pe.wait_ge(S("g_prod"), at("g_prod", l, 4 * KD))
                ws = [arrived() for _ in range(4)]
                for t in range(NT):
                    if t >= 4:
                        pe.wait_ge(S("w_x"), at("w_x", l, t - 3))
                    for j in range(4):
                        for k in range(KD):
                            last = mm(psb(t % 4)[:, j * 256:(j + 1) * 256], merged[:, k, t * P:(t + 1) * P],
                                      slot3(ws[j], KD)[:, k, :], start=(k == 0), stop=(k == KD - 1))
                    last.then_inc(S("w_ps"), 1)
                owed[0] += 4

                pe.wait_ge(S("const_dma"), 48)
                for t in range(NT + 1):
                    if t < NT:
                        pe.wait_ge(S("h2_tok"), at("h2_tok", l, t + 1))
                        if t == 0:
                            pe.wait_ge(S("w_x"), at("w_x", l, NT))
                        if t >= 2:
                            pe.wait_ge(S("h2T"), at("h2T", l, t - 1))
                        for k in range(KD):
                            last = pe.transpose(psb(t % 2)[:, k * P:(k + 1) * P], h2tok[t % 2][:, k * P:(k + 1) * P], ident[:, :])
                            if k == 0:
                                pays(last)
                        last.then_inc(S("h2_tr"), 1)
                    if t >= 1:
                        u = t - 1
                        pe.wait_ge(S("h2T"), at("h2T", l, u + 1))
                        for k in range(KD):
                            last = mm(psb(3)[:, u * NE:(u + 1) * NE], h2T[u % 2][:, k, :], rwv[:, k, :],
                                      start=(k == 0), stop=(k == KD - 1))
                        last.then_inc(S("lg_ps"), 1)

                pe.wait_ge(S("r_oh"), at("r_oh", l, 1))
                for t in range(NT + 1):
                    o = psb(2)[:, t * NE:(t + 1) * NE]
                    prev = list(range(t))
                    for i, u in enumerate(prev):
                        for k in range(2):
                            last = mm(o, ones[:, :], r_oh[k][:, u, :], start=(i == 0 and k == 0),
                                      stop=(t == NT and i == len(prev) - 1 and k == 1))
                    if t < NT:
                        for k in range(2):
                            last = mm(o, tri[:, :], r_oh[k][:, t, :], start=(t == 0 and k == 0), stop=(k == 1))
                last.then_inc(S("rank_ps"), 1)
                nb = expert_blocks(W(l))
                pe.wait_ge(S("tab_ld"), at("tab_ld", l, 16))
                pe.transpose(psb(3)[:, 0:MAXB + 1], tabr, ident[0:MAXB + 1, 0:MAXB + 1]).then_inc(S("tab_ps"), 1)

                def gather_T(b, j, first=False):
                    pe.wait_ge(S(f"xg{j}"), at(f"xg{j}", l, (b // 2 + 1) * 16 if isinstance(b, int) else b))
                    for k in range(KD):
                        last = pe.transpose(psb(0)[:, k * P:(k + 1) * P], xg[j][:, k * P:(k + 1) * P], ident[:, :])
                        if k == 0:
                            pays(last)
                    last.then_inc(S("xT_ps"), 1)

                def hidden(j, s1, s3):
                    for s, o in ((s1, 0), (s3, FF)):
                        for k in range(KD):
                            last = mm(psb(1)[:, o:o + FF], xgT[j][:, k, :], slot3(s, KD)[:, k, :],
                                      start=(k == 0), stop=(k == KD - 1))
                        last.then_inc(slab_used if s == s1 else S("h_ps"), 1)
                    owed[0] += 1

                def down(j, s2):
                    w = slot3(s2, 2)
                    for n in range(2):
                        for k in range(2):
                            last = mm(psb(2 + j)[:, n * 512:(n + 1) * 512], act_T[j][:, k, :], w[:, k, n * 512:(n + 1) * 512],
                                      start=(k == 0), stop=(k == 1))
                    last.then_inc(S("y_ps"), 1)
                    owed[0] += 1

                def act_transpose(j):
                    for k in range(2):
                        last = pe.transpose(psb(1)[:, 512 + k * P:512 + (k + 1) * P], act_a[j][:, k * P:(k + 1) * P], ident[:, :])
                        if k == 0:
                            pays(last)
                    last.then_inc(S("aT_ps"), 1)

                pe.wait_ge(S("tab_i"), at("tab_i", l, 1))
                gather_T(0, 0)
                for b in range(3):
                    pe.wait_ge(S("xgT"), at("xgT", l, b + 1))
                    if b:
                        pe.wait_ge(S("a_sb"), at("a_sb", l, b))
                    hidden(b % 2, arrived(), arrived())
                    gather_T(b + 1, (b + 1) % 2)
                    if b:
                        pe.wait_ge(S("aT_sb"), at("aT_sb", l, b))
                        down((b - 1) % 2, arrived())
                    pe.wait_ge(S("a_sb"), at("a_sb", l, b + 1))
                    act_transpose(b % 2)
                n0 = used[0]
                with pe.Fori(0, (nb - 3) // 2) as i:
                    for j in range(2):
                        par = (3 + j) % 2
                        sl = [(n0 + 3 * j + c) % SLOTS for c in range(3)]
                        turn = [16 * ((n0 + 3 * j + c) // SLOTS + 1) for c in range(3)]
                        b = i * 2 + (3 + j)
                        pe.wait_ge(S("xgT"), at("xgT", l, b + 1))
                        pe.wait_ge(S("a_sb"), at("a_sb", l, b))
                        pe.wait_ge(slab_full[sl[0]], i * 16 + turn[0])
                        pe.wait_ge(slab_full[sl[1]], i * 16 + turn[1])
                        hidden(par, sl[0], sl[1])
                        gather_T(i * 16 + ((4 + j) // 2 + 1) * 16, 1 - par)
                        pe.wait_ge(S("aT_sb"), at("aT_sb", l, b))
                        pe.wait_ge(S("y_sb"), at("y_sb", l, b - 2))
                        pe.wait_ge(slab_full[sl[2]], i * 16 + turn[2])
                        down(1 - par, sl[2])
                        pe.wait_ge(S("a_sb"), at("a_sb", l, b + 1))
                        act_transpose(par)
                used[0] += 3 * (nb - 3)
                pe.wait_ge(S("aT_sb"), at("aT_sb", l, nb))
                pe.wait_ge(S("y_sb"), at("y_sb", l, nb - 2))
                down((nb - 1) % 2, arrived())

        @block.scalar
        def _(act):
            act_f = act.activation
            chain = [0]

            def link(ins):
                chain[0] += 1
                ins.then_inc(S("act_chain"), 1)
                act.wait_ge(S("act_chain"), chain[0])

            for t in range(AT):
                src = A["x"][0, t * P:(t + 1) * P, :] if t < LT else A["ctx"][0, (t - LT) * P:(t - LT + 1) * P, :]
                act.dma_start(x_t[:, t, :], src).then_inc(S("x_in"), 16)
            act.wait_ge(S("c_rows"), 32)
            act_f(T[0:2 * KD, 0:P], T[0:2 * KD, P:2 * P], ACT.Silu).then_inc(S("c_silu"), 1)
            act.wait_ge(S("c_tr"), 1)
            act_f(scT[:, :], psb(3)[:, 0:2 * KD], ACT.Copy).then_inc(S("c_col"), 1)
            for l in range(DEPTH):
                act.wait_ge(slab_used, (l + 1) * MC // 2)
                act_f(HT[:, l * 2 * MC:(l + 1) * 2 * MC], psb(l)[:, 0:2 * MC], ACT.Copy).then_inc(S("mod_sb"), 1)

            for l in range(DEPTH):
                NT = tiles(l)
                if l == 0:
                    act.wait_ge(S("x_in"), 16 * AT)
                for t in range(AT):
                    if l > 0:
                        act.wait_ge(S("x_new"), at("x_new", l - 1, t + 1))
                    if t:
                        act.wait_ge(S("n1_sq"), at("n1_sq", l, t))
                    act_f(psb(3), x_t[:, t, :], ACT.Square, scale=D ** -0.5, accum_out=st[:, t:t + 1]).then_inc(S("n1_sq"), 1)
                act.wait_ge(S("n1_eps"), at("n1_eps", l, 1))
                act_f(srt[:, 0:AT], rst[:, 0:AT], ACT.Sqrt).then_inc(S("n1_rt"), 1)
                for t in range(AT):
                    act.wait_ge(S("h_tr"), at("h_tr", l, t + 1))
                    act_f(hT[:, :, t * P:(t + 1) * P], psb(t % 2).rearrange("p (k t) -> p k t", k=KD), ACT.Copy)\
                        .then_inc(S("hT_tile"), 1)

                def stats(t):
                    full = t < NT
                    b = psb(t % 2)
                    act.wait_ge(S("tproj"), at("tproj", l, t + 1))
                    if full:
                        link(act_f(sgv[:, t, :], b[:, 512:1024], ACT.Gelu_apprx_tanh))
                        act_f(cnT[t % 2][:, 0:Q_LORA], b[:, Q_OFF:CONV_OFF], ACT.Square, scale=Q_LORA ** -0.5,
                              accum_out=st[:, 3 * t + 1:3 * t + 2])
                        act_f(psb(t % 2)[:, 512:1024], sgv[:, t, :], ACT.Square, scale=BW ** -0.5,
                              accum_out=st[:, 3 * t + 2:3 * t + 3]).then_inc(S("sgv_stat"), 1)
                    act_f(cnT[t % 2][:, 256:384], b[:, 0:KV_LORA], ACT.Square, scale=KV_LORA ** -0.5,
                          accum_out=st[:, 3 * t:3 * t + 1]).then_inc(S("t_sq"), 1)
                    act.wait_ge(S("t_eps"), at("t_eps", l, t + 1))
                    n = 3 if full else 1
                    act_f(srt[:, 3 * t:3 * t + n], rst[:, 3 * t:3 * t + n], ACT.Sqrt).then_inc(S("t_rt"), 1)

                def evacuate(t):
                    full = t < NT
                    act.wait_ge(S("cn_tr"), at("cn_tr", l, t + 1))
                    n = 384 if full else P
                    act_f(cnT[t % 2][:, 0:n], psb(t % 2)[:, 0:n], ACT.Copy).then_inc(S("cnT"), 1)
                    act.wait_ge(S("up"), at("up", l, t + 1))
                    if t >= 2:
                        act.wait_ge(S("t_qk"), at("t_qk", l, t - 1))
                    kv = psb(2).rearrange("p (h e) -> p h e", h=H)
                    act_f(raw[t % 2][:, 0, :, 0:NOPE], kv[:, :, 0:NOPE], ACT.Copy)
                    if full:
                        for j in range(2):
                            act_f(raw[t % 2][:, 1, 4 * j:4 * j + 4, :],
                                  psb(3)[:, j * 512:j * 512 + 384].rearrange("p (h e) -> p h e", h=4), ACT.Copy)
                    act_f(vb[:, t, :].rearrange("p (h e) -> p h e", h=H), kv[:, :, NOPE:P], ACT.Copy).then_inc(S("raw"), 1)

                def head_roots(t):
                    n = 2 * H if t < NT else H
                    act.wait_ge(S("t_ss"), at("t_ss", l, t + 1))
                    act_f(rsq[t % 2][:, 0:n], ssq[t % 2][:, 0:n], ACT.Sqrt).then_inc(S("t_hrt"), 1)

                if l > 0:
                    act.wait_ge(S("x_spilled"), 16 * AT)
                for t in range(AT + 2):
                    if t >= 2:
                        head_roots(t - 2)
                    if t < AT:
                        stats(t)
                    if 1 <= t <= AT:
                        evacuate(t - 1)

                act.wait_ge(S("wT_tr"), at("wT_tr", l, 1))
                act_f(sguwT, psb(2)[:, 0:512].rearrange("p (g q) -> p g q", g=BC), ACT.Copy)
                act_f(cw[:, :], psb(2)[:, 512:528], ACT.Copy).then_inc(S("wT"), 1)
                act.wait_ge(S("t_qk"), at("t_qk", l, AT))
                for g in range(BC):
                    act.wait_ge(S("sgu_ps"), at("sgu_ps", l, g + 1))
                    if g >= 2:
                        act.wait_ge(S("sgu_out"), at("sgu_out", l, g - 1))
                    act_f(uT[g % 2][:, 0:W(l)], psb(g % 2)[:, 0:W(l)], ACT.Gelu_apprx_tanh).then_inc(S("sgu_u"), 1)

                def gated(q):
                    for d in range(KD):
                        u = q * KD + d
                        act.wait_ge(S("g_ps"), at("g_ps", l, u + 1))
                        if u >= 2:
                            act.wait_ge(S("g_prod"), at("g_prod", l, u - 1))
                        act_f(sig[u % 2][:, 0:W(l)], psb(u % 2)[:, 0:W(l)], ACT.Sigmoid).then_inc(S("g_sig"), 1)

                gated(0)
                act.wait_ge(S("sgu_out"), at("sgu_out", l, BC))
                for c in range(BC):
                    for j in range(2):
                        w = 3 * c + j
                        act.wait_ge(S("cv_ps"), at("cv_ps", l, w + 1))
                        if c >= 2:
                            act.wait_ge(S("cv_br"), at("cv_br", l, c - 1))
                        act_f((gcs, gbs)[j][c % 2][:, 0:W(l)], psb(w % 4)[:, 0:W(l)], ACT.Copy).then_inc(S("cv_evac"), 1)
                gated(1)
                act.wait_ge(S("po_pad"), at("po_pad", l, 1))
                for g in range(BC + 1):
                    if g < BC:
                        act.wait_ge(S("po_ps"), at("po_ps", l, g + 1))
                        if g >= 2:
                            act.wait_ge(S("po_pl"), at("po_pl", l, g - 1))
                        last = act_f(pp[g % 2][:, PLL:PLL + SEQ], psb(g % 2)[:, 0:SEQ], ACT.Copy)
                        if W(l) > SEQ:
                            last = act_f(pp[g % 2][:, PLC:PLC + CTX], psb(g % 2)[:, SEQ:TOK], ACT.Copy)
                        last.then_inc(S("po_pp"), 1)
                    if g >= 1:
                        h = g - 1
                        act.wait_ge(S("po_mix"), at("po_mix", l, h + 1))
                        act_f(brB[:, h, 0:W(l)], psb(2 + h % 2)[:, 0:W(l)], ACT.Copy, scale=cw[:, 12 + h:13 + h])\
                            .then_inc(S("po_br"), 1)
                gated(2)
                steps = [(h, t) for h in range(H) for t in range(NT)]
                rounds = (AT + NT + 3) // 4
                act.wait_ge(S("g_prod"), at("g_prod", l, 3 * KD))

                def head_T(h, r):
                    act.wait_ge(S("qk_tr"), at("qk_tr", l, h * rounds + r + 1))
                    if h >= 2 and r == 0:
                        act.wait_ge(S("s_ps"), at("s_ps", l, (h - 1) * NT))
                    n = min(4, AT + NT - 4 * r) * P
                    act_f(qkT[h % 2][0:QK, r * 512:r * 512 + n], psb(3)[0:QK, 512:512 + n], ACT.Copy).then_inc(S("qkT"), 1)

                for r in range(rounds):
                    head_T(0, r)
                for n in range(len(steps) + 1):
                    if n < len(steps):
                        h, t = steps[n]
                        lo = 0 if t < LT else SEQ
                        act.wait_ge(S("negmax"), at("negmax", l, n + 1))
                        if n >= 2:
                            act.wait_ge(S("pr_tr"), at("pr_tr", l, n - 1))
                        act_f(probs[n % 2][:, lo:TOK], psb(n % 2)[:, lo:TOK], ACT.Exp, bias=negm[:, n:n + 1],
                              accum_out=rsum[:, n:n + 1]).then_inc(S("probs"), 1)
                        if h + 1 < H and t < rounds:
                            head_T(h + 1, t)
                    if n >= 1 and steps[n - 1][1] < LT:
                        m = n - 1
                        act.wait_ge(S("pr_tr"), at("pr_tr", l, m + 1))
                        if m >= 2:
                            act.wait_ge(S("o_ps"), at("o_ps", l, m - 1))
                        act_f(prT[m % 2][:, 0:SEQ], psb(2)[:, 0:SEQ], ACT.Copy).then_inc(S("prT_a"), 1)
                for c in range(BC):
                    act.wait_ge(S("o_tr"), at("o_tr", l, c + 1))
                    act_f(brA[:, c, 0:W(l)], psb(c % 2)[:, 0:W(l)], ACT.Copy).then_inc(S("at_br"), 1)
                act.wait_ge(S("o_tr"), at("o_tr", l, BC))
                for t in range(NT):
                    if l == 0:
                        src = A["x"][0, t * P:(t + 1) * P, :] if t < LT else A["ctx"][0, (t - LT) * P:(t - LT + 1) * P, :]
                    else:
                        src = x_spill[t * P:(t + 1) * P, :]
                    act.dma_start(x_t[:, t, :], src).then_inc(S("x_back"), 16)
                gated(3)
                for t in range(NT):
                    act.wait_ge(S("w_x"), at("w_x", l, t + 1))
                    if t:
                        act.wait_ge(S("n2_sq"), at("n2_sq", l, t))
                    act_f(junk, x_t[:, t, :], ACT.Square, scale=D ** -0.5, accum_out=st[:, t:t + 1]).then_inc(S("n2_sq"), 1)
                act.wait_ge(S("n2_eps"), at("n2_eps", l, 1))
                act_f(srt[:, 0:NT], rst[:, 0:NT], ACT.Sqrt).then_inc(S("n2_rt"), 1)
                for t in range(NT):
                    act.wait_ge(S("h2_tok"), at("h2_tok", l, t + 1))
                    act.dma_start(h2_rows[t * P:(t + 1) * P, :], h2tok[t % 2]).then_inc(S(f"h2_st{t % 2}"), 16)
                    act.wait_ge(S("h2_tr"), at("h2_tr", l, t + 1))
                    if t >= 2:
                        act.wait_ge(S("lg_ps"), at("lg_ps", l, t - 1))
                    act_f(h2T[t % 2], psb(t % 2).rearrange("p (k t) -> p k t", k=KD), ACT.Copy).then_inc(S("h2T"), 1)
                act.wait_ge(S("lg_ps"), at("lg_ps", l, NT))
                act_f(r_s[:, 0:NT, :], psb(3)[:, 0:NT * NE].rearrange("p (t e) -> p t e", t=NT), ACT.Sigmoid)\
                    .then_inc(S("r_s"), 1)

                nb = expert_blocks(W(l))

                def silu(b, j, first=False):
                    act.wait_ge(S("h_ps"), at("h_ps", l, b + 1))
                    if not first:
                        act.wait_ge(S("a_sb"), at("a_sb", l, b - 1))
                    act_f(sil[j], psb(1)[:, 0:FF], ACT.Silu).then_inc(S("sil"), 1)

                def rows_T(b, j):
                    act.wait_ge(S("xT_ps"), at("xT_ps", l, b + 1))
                    act_f(xgT[j], psb(0).rearrange("p (k t) -> p k t", k=KD), ACT.Copy).then_inc(S("xgT"), 1)

                def hidden_T(b, j):
                    act.wait_ge(S("aT_ps"), at("aT_ps", l, b + 1))
                    act_f(act_T[j], psb(1)[:, 512:768].rearrange("p (k t) -> p k t", k=2), ACT.Copy).then_inc(S("aT_sb"), 1)

                def store(b, j, dyn=False):
                    act.wait_ge(S("y_sb"), at("y_sb", l, b + 1))
                    dst = y_rows[l][bass.ds(b * P, P), :] if dyn else y_rows[l][b * P:(b + 1) * P, :]
                    act.dma_start(dst, ysb[j]).then_inc(S(f"y_st{j}"), 16)

                rows_T(0, 0)
                for b in range(3):
                    silu(b, b % 2, b < 2)
                    rows_T(b + 1, (b + 1) % 2)
                    hidden_T(b, b % 2)
                    if b >= 2:
                        store(b - 2, b % 2)
                with act.Fori(0, (nb - 3) // 2) as i:
                    for j in range(2):
                        par = (3 + j) % 2
                        b = i * 2 + (3 + j)
                        silu(b, par)
                        rows_T(b + 1, 1 - par)
                        hidden_T(b, par)
                        store(b - 2, par, True)
                for b in (nb - 2, nb - 1):
                    store(b, b % 2)
                if l == DEPTH - 1:
                    for t in range(LT):
                        act.wait_ge(S("x_new"), at("x_new", l, t + 1))
                        act.dma_start(out[0, t * P:(t + 1) * P, :], x_t[:, t, :]).then_inc(S("x_stored"), 16)
                else:
                    for t in range(AT):
                        act.wait_ge(S("x_new"), at("x_new", l, t + 1))
                        act.dma_start(x_spill[t * P:(t + 1) * P, :], x_t[:, t, :]).then_inc(S("x_spilled"), 16)

        @block.vector
        def _(dve):
            chain = [0]

            def link(ins):
                chain[0] += 1
                ins.then_inc(S("dve_chain"), 1)
                dve.wait_ge(S("dve_chain"), chain[0])

            tt, ts, stt, cp = dve.tensor_tensor, dve.tensor_scalar, dve.scalar_tensor_tensor, dve.tensor_copy

            dve.wait_ge(S("mod_b"), 16 * 2 * DEPTH)
            for l in range(DEPTH):
                dve.wait_ge(S("mod_tr"), l + 1)
                tt(MG[0:2 * MC, l * P:(l + 1) * P], psb(2)[0:2 * MC, l * 512:l * 512 + P], MG[0:2 * MC, (2 + l) * P:(3 + l) * P], ALU.add)\
                    .then_inc(S("mod_out"), 1)

            for l in range(DEPTH):
                NT = tiles(l)
                dve.wait_ge(S("par_n1"), at("par_n1", l, 16 * 3))
                for v in range(2):
                    last = stt(scale1(v), scale1(v), 1.0, gain1, ALU.add, ALU.mult)
                dve.wait_ge(S("n1_sq"), at("n1_sq", l, AT))
                ts(rst[:, 0:AT], st[:, 0:AT], EPS, None, ALU.add).then_inc(S("n1_eps"), 1)
                dve.wait_ge(S("n1_rt"), at("n1_rt", l, 1))
                link(dve.reciprocal(rst[:, 0:AT], srt[:, 0:AT]))
                for t in range(AT):
                    v = 0 if t < LT else 1
                    if t >= 2:
                        dve.wait_ge(S("h_tr"), at("h_tr", l, t - 1))
                    link(stt(htok[t % 2], x_t[:, t, :], rst[:, t:t + 1], scale1(v), ALU.mult, ALU.mult))
                    tt(htok[t % 2], htok[t % 2], shift1(v), ALU.add).then_inc(S("h_tok"), 1)

                def small_norms(t):
                    full = t < NT
                    b = psb(t % 2)
                    n = 3 if full else 1
                    dve.wait_ge(S("t_sq"), at("t_sq", l, t + 1))
                    ts(rst[:, 3 * t:3 * t + n], st[:, 3 * t:3 * t + n], EPS, None, ALU.add).then_inc(S("t_eps"), 1)
                    dve.wait_ge(S("t_rt"), at("t_rt", l, t + 1))
                    link(dve.reciprocal(rst[:, 3 * t:3 * t + n], srt[:, 3 * t:3 * t + n]))
                    if t >= 2:
                        dve.wait_ge(S("t_qk"), at("t_qk", l, t - 1))
                    cp(raw[t % 2][:, 0, :, NOPE:QK], b[:, None, KR_OFF:Q_OFF].to_broadcast([P, H, ROPE]))
                    last = stt(cn[t % 2][:, 0:P], b[:, 0:KV_LORA], rst[:, 3 * t:3 * t + 1], g_kva, ALU.mult, ALU.mult)
                    if full:
                        last = stt(cn[t % 2][:, P:384], b[:, Q_OFF:CONV_OFF], rst[:, 3 * t + 1:3 * t + 2], g_qa, ALU.mult, ALU.mult)
                    last.then_inc(S("cn"), 1)
                    if full:
                        stt(sgv[:, t, :], sgv[:, t, :], rst[:, 3 * t + 2:3 * t + 3], g_sgu, ALU.mult, ALU.mult)\
                            .then_inc(S("sgv"), 1)

                def head_squares(t):
                    n = 2 * H if t < NT else H
                    dve.wait_ge(S("t_sqd"), at("t_sqd", l, t + 1))
                    link(dve.tensor_reduce(ssq[t % 2][:, 0:n], sqb[t % 2][:, 0:n * QK].rearrange("p (h e) -> p h e", e=QK),
                                           AX.X, ALU.add))
                    ts(ssq[t % 2][:, 0:n], ssq[t % 2][:, 0:n], 1.0 / QK, EPS, ALU.mult, ALU.add).then_inc(S("t_ss"), 1)

                def head_norms(t):
                    n = 2 * H if t < NT else H
                    dve.wait_ge(S("t_hrt"), at("t_hrt", l, t + 1))
                    link(dve.reciprocal(rsq[t % 2][:, 0:n], rsq[t % 2][:, 0:n]))
                    r = raw[t % 2].rearrange("p s h e -> p (s h) e")[:, 0:n, :]
                    tt(r, r, rsq[t % 2][:, 0:n, None].to_broadcast([P, n, QK]), ALU.mult).then_inc(S("t_rn"), 1)

                if l > 0:
                    dve.wait_ge(S("x_spilled"), 16 * AT)
                dve.wait_ge(S("par_b"), at("par_b", l, 16 * 7))
                dve.wait_ge(S("h_tr"), at("h_tr", l, AT))
                for t in range(AT + 2):
                    if t >= 2:
                        head_norms(t - 2)
                    if t < AT:
                        small_norms(t)
                    if 1 <= t <= AT:
                        head_squares(t - 1)

                dve.wait_ge(S("par_sb"), at("par_sb", l, 16))
                dve.wait_ge(S("t_qk"), at("t_qk", l, AT))
                for g in range(BC):
                    dve.wait_ge(S("sgu_mix"), at("sgu_mix", l, g + 1))
                    if g:
                        dve.wait_ge(S("sgu_out"), at("sgu_out", l, g))
                    m3 = psb(2 + g % 2)[:, 0:W(l)].rearrange("p (t q) -> p t q", q=P)
                    link(tt(umix[:, 0:W(l)].rearrange("p (t q) -> p t q", q=P), m3,
                            sgub[:, None, g * P:(g + 1) * P].to_broadcast([P, NT, P]), ALU.add))
                    dve.wait_ge(S("sgu_u"), at("sgu_u", l, g + 1))
                    tt(brB[:, g, 0:W(l)], umix[:, 0:W(l)], uT[g % 2][:, 0:W(l)], ALU.mult).then_inc(S("sgu_out"), 1)

                def gated(q):
                    for d in range(KD):
                        u = q * KD + d
                        dve.wait_ge(S("b_ps"), at("b_ps", l, u + 1))
                        dve.wait_ge(S("g_sig"), at("g_sig", l, u + 1))
                        o = merged[:, d, 0:W(l)]
                        if q == 0:
                            tt(o, sig[u % 2][:, 0:W(l)], psb(2 + u % 2)[:, 0:W(l)], ALU.mult).then_inc(S("g_prod"), 1)
                        else:
                            dve.wait_ge(S("g_prod"), at("g_prod", l, u))
                            link(tt(prod[:, 0:W(l)], sig[u % 2][:, 0:W(l)], psb(2 + u % 2)[:, 0:W(l)], ALU.mult))
                            tt(o, o, prod[:, 0:W(l)], ALU.add).then_inc(S("g_prod"), 1)

                gated(0)
                dve.memset(cup[0], 0.0)
                link(dve.memset(cup[1], 0.0))
                streams = [(0, SEQ, CVL)] + ([(SEQ, TOK, CVC)] if W(l) > SEQ else [])
                hi = CVC + CTX if W(l) > SEQ else CVL + SEQ
                for c in range(BC):
                    w = 3 * c + 2
                    dve.wait_ge(S("cv_ps"), at("cv_ps", l, w + 1))
                    dve.wait_ge(S("cv_evac"), at("cv_evac", l, 2 * c + 2))
                    cu = cup[c % 2]
                    for a, b, o in streams:
                        last = tt(cu[:, o:o + b - a], gcs[c % 2][:, a:b], psb(w % 4)[:, a:b], ALU.mult)
                    last.then_inc(S("cv_cu"), 1)
                    dve.wait_ge(S("cv_cu"), at("cv_cu", l, c + 1))
                    if c:
                        dve.wait_ge(S("cv_br"), at("cv_br", l, c))
                    y = cvy[:, 1:hi]
                    link(ts(y, cu[:, 1:hi], cw[:, 4 + c:5 + c], None, ALU.mult))
                    link(stt(y, cu[:, 0:hi - 1], cw[:, c:c + 1], y, ALU.mult, ALU.add))
                    link(stt(y, cu[:, 2:hi + 1], cw[:, 8 + c:9 + c], y, ALU.mult, ALU.add))
                    for a, b, o in streams:
                        last = tt(brA[:, c, a:b], cvy[:, o:o + b - a], gbs[c % 2][:, a:b], ALU.mult)
                    last.then_inc(S("cv_br"), 1)
                gated(1)
                dve.wait_ge(S("const_dma"), 48)
                for j in range(2):
                    last = dve.memset(pp[j], 0.0)
                last.then_inc(S("po_pad"), 1)
                streams = [(0, SEQ, PLL)] + ([(SEQ, TOK, PLC)] if W(l) > SEQ else [])
                for g, win_ in enumerate(WINDOWS):
                    dve.wait_ge(S("po_pp"), at("po_pp", l, g + 1))
                    if g:
                        dve.wait_ge(S("po_pl"), at("po_pl", l, g))
                    src, lo, k = pp[g % 2], 1, 1
                    link(tt(pacc[0][:, 1:PLW], src[:, 0:PLW - 1], src[:, 1:PLW], ALU.add))
                    cur, lo, hi = 0, 1, PLW
                    while 2 * k < win_:
                        link(tt(pacc[1 - cur][:, lo + k:hi - k], pacc[cur][:, lo:hi - 2 * k], pacc[cur][:, lo + 2 * k:hi], ALU.add))
                        cur, lo, hi, k = 1 - cur, lo + k, hi - k, 2 * k
                    s = pacc[cur]
                    e = edge[:, g * 2 * PP:(g + 1) * 2 * PP]
                    for a, b, o in streams:
                        n = b - a
                        tt(s[:, o:o + PP], s[:, o:o + PP], e[:, 0:PP], ALU.mult)
                        last = tt(s[:, o + n - PP:o + n], s[:, o + n - PP:o + n], e[:, PP:2 * PP], ALU.mult)
                    link(last)
                    if g >= 2:
                        dve.wait_ge(S("po_mix"), at("po_mix", l, g - 1))
                    for a, b, o in streams:
                        last = stt(pooled[g % 2][:, a:b], s[:, o:o + b - a], 1.0 / win_, src[:, o:o + b - a], ALU.mult, ALU.subtract)
                    last.then_inc(S("po_pl"), 1)
                gated(2)
                dve.wait_ge(S("po_br"), at("po_br", l, BC))
                steps = [(h, t) for h in range(H) for t in range(NT)]
                for n in range(len(steps) + 2):
                    if n < len(steps):
                        h, t = steps[n]
                        lo = 0 if t < LT else SEQ
                        dve.wait_ge(S("s_ps"), at("s_ps", l, n + 1))
                        dve.tensor_reduce(negm[:, n:n + 1], psb(n % 2)[:, lo:TOK], AX.X, ALU.max, negate=True)\
                            .then_inc(S("negmax"), 1)
                    if 1 <= n <= len(steps):
                        m = n - 1
                        h, t = steps[m]
                        dve.wait_ge(S("pr_tr"), at("pr_tr", l, m + 1))
                        if m >= 2:
                            dve.wait_ge(S("o_ps"), at("o_ps", l, m - 1))
                        cp(prT[m % 2][:, SEQ:TOK], psb(2)[:, SEQ:TOK]).then_inc(S("prT_d"), 1)
                    if n >= 2:
                        m = n - 2
                        h, t = steps[m]
                        dve.wait_ge(S("o_ps"), at("o_ps", l, m + 1))
                        link(dve.reciprocal(rinv[:, m:m + 1], rsum[:, m:m + 1]))
                        ts(obuf[:, t, h * VD:(h + 1) * VD], psb(3)[:, (m % 2) * VD:(m % 2 + 1) * VD], rinv[:, m:m + 1], None,
                           ALU.mult).then_inc(S("o_sb"), 1)
                gated(3)
                dve.wait_ge(S("par_n2"), at("par_n2", l, 16 * 3))
                dve.wait_ge(S("x_back"), at("x_back", l, 16 * NT))
                for t in range(NT):
                    v = 0 if t < LT else 1
                    dve.wait_ge(S("w_ps"), at("w_ps", l, t + 1))
                    if t:
                        dve.wait_ge(S("w_x"), at("w_x", l, t))
                    link(tt(wtmp, psb(t % 4), mrow[:, v, 0, :], ALU.mult))
                    tt(x_t[:, t, :], x_t[:, t, :], wtmp, ALU.add).then_inc(S("w_x"), 1)
                for v in range(2):
                    last = stt(mrow[:, v, 2, :], mrow[:, v, 2, :], 1.0, gain2, ALU.add, ALU.mult)
                dve.wait_ge(S("n2_sq"), at("n2_sq", l, NT))
                ts(rst[:, 0:NT], st[:, 0:NT], EPS, None, ALU.add).then_inc(S("n2_eps"), 1)
                dve.wait_ge(S("n2_rt"), at("n2_rt", l, 1))
                link(dve.reciprocal(rst[:, 0:NT], srt[:, 0:NT]))
                for t in range(NT):
                    v = 0 if t < LT else 1
                    if t >= 2:
                        dve.wait_ge(S("h2_tr"), at("h2_tr", l, t - 1))
                        dve.wait_ge(S(f"h2_st{t % 2}"), at(f"h2_st{t % 2}", l, 16 * (t // 2)))
                    link(stt(h2tok[t % 2], x_t[:, t, :], rst[:, t:t + 1], mrow[:, v, 2, :], ALU.mult, ALU.mult))
                    tt(h2tok[t % 2], h2tok[t % 2], mrow[:, v, 1, :], ALU.add).then_inc(S("h2_tok"), 1)

                s, sbv, m_, sc = (a[:, 0:NT, :] for a in (r_s, r_sb, r_m, r_sc))
                oh = [a[:, 0:NT, :] for a in r_oh]

                def bc(a, n):
                    return a[:, :, None].to_broadcast([P, a.shape[1], n])

                dve.wait_ge(S("r_s"), at("r_s", l, 1))
                dve.wait_ge(S("const"), 8)
                link(tt(sbv, s, rbias[:, None, :].to_broadcast([P, NT, NE]), ALU.add))
                g3 = sbv.rearrange("p t (g e) -> p (t g) e", g=NG)
                pr = r_pair[:, 0:NT * NG, :]
                tt(pr[:, :, 0:3], g3[:, :, 0:3], g3[:, :, 1:4], ALU.add)
                tt(pr[:, :, 3:5], g3[:, :, 0:2], g3[:, :, 2:4], ALU.add)
                link(tt(pr[:, :, 5:6], g3[:, :, 0:1], g3[:, :, 3:4], ALU.add))
                gs, gq, gm = (a[:, 0:NT, :] for a in (r_gs, r_gq, r_gm))
                mx = r_mx[:, 0:NT]
                link(dve.tensor_reduce(gs.rearrange("p t g -> p (t g)"), pr, AX.X, ALU.max))

                def first_max(dst, src, weights, tmp, n):
                    link(dve.tensor_reduce(mx, src, AX.X, ALU.max))
                    link(tt(tmp, src, bc(mx, n), ALU.is_ge))
                    link(tt(tmp, tmp, weights[:, None, :].to_broadcast([P, NT, n]), ALU.mult))
                    link(dve.tensor_reduce(mx, tmp, AX.X, ALU.max))
                    link(tt(dst, tmp, bc(mx, n), ALU.is_equal))

                first_max(gm, gs, w4, gq, NG)
                link(ts(gq, gm, BIG, -BIG, ALU.mult, ALU.add))
                m3 = m_.rearrange("p t (g e) -> p (t g) e", g=NG)
                link(tt(m3, g3, bc(gm.rearrange("p t g -> p (t g)"), EG), ALU.mult))
                link(tt(m3, m3, bc(gq.rearrange("p t g -> p (t g)"), EG), ALU.add))
                first_max(oh[0], m_, w16, sc, NE)
                link(stt(m_, oh[0], -3.0e38, m_, ALU.mult, ALU.add))
                first_max(oh[1], m_, w16, sc, NE)
                cp(r_den[:, 0:1], oh[1][:, 0, 0:1]).then_inc(S("r_oh"), 1)
                for k in range(2):
                    link(tt(sc, oh[k], s, ALU.mult))
                    link(dve.tensor_reduce(gw[k][:, 0:NT], sc, AX.X, ALU.add))
                link(tt(r_den[:, 0:NT], gw[0][:, 0:NT], gw[1][:, 0:NT], ALU.add))
                link(dve.reciprocal(r_den[:, 0:NT], r_den[:, 0:NT]))
                for k in range(2):
                    tt(gw[k][:, 0:NT], gw[k][:, 0:NT], r_den[:, 0:NT], ALU.mult)
                nb = expert_blocks(W(l))
                dve.wait_ge(S("rank_ps"), at("rank_ps", l, 1))
                cnt = psb(2)[:, NT * NE:(NT + 1) * NE]
                link(tt(r_cnt, cnt[:, :, None].to_broadcast([P, NE, 6]), steps6[:, None, :].to_broadcast([P, NE, 6]), ALU.is_gt))
                link(dve.tensor_reduce(r_nb, r_cnt, AX.X, ALU.add))
                link(dve.tensor_tensor_scan(r_end, ones[:, 0:NE], r_nb, 0.0, ALU.mult, ALU.add))
                link(tt(r_base, r_end, r_nb, ALU.subtract))
                link(ts(r_base, r_base, float(P), None, ALU.mult))
                link(tt(m_, psb(2)[:, 0:NT * NE].rearrange("p (t e) -> p t e", t=NT), r_base[:, None, :].to_broadcast([P, NT, NE]), ALU.add))
                for k in range(2):
                    link(tt(sc, m_, oh[k], ALU.mult))
                    link(dve.tensor_reduce(r_slot[:, k, 0:NT], sc, AX.X, ALU.add))
                cp(slot_i[:, :], r_slot.rearrange("p k t -> p (k t)")).then_inc(S("slots"), 1) if NT == AT else \
                    cp(slot_i[:, :].rearrange("p (k t) -> p k t", k=2)[:, :, 0:NT], r_slot[:, :, 0:NT]).then_inc(S("slots"), 1)
                blk = r_blk[:, 0:nb, :]
                link(tt(blk, r_end[:, None, :].to_broadcast([P, nb, NE]), blkno[:, 0:nb, None].to_broadcast([P, nb, NE]), ALU.is_le))
                link(dve.tensor_reduce(r_eid[:, 0:nb], blk, AX.X, ALU.add))
                link(ts(r_eid[:, 0:nb], r_eid[:, 0:nb], float(NE - 1), None, ALU.min))
                cp(eid_i[:, 0:nb], r_eid[:, 0:nb]).then_inc(S("eid"), 1)
                dve.wait_ge(S("tab_ps"), at("tab_ps", l, 1))
                cp(tab_i[:, :], psb(3)[:, 0:MAXB + 1]).then_inc(S("tab_i"), 1)

                def hidden(b, j, first=False):
                    dve.wait_ge(S("sil"), at("sil", l, b + 1))
                    if not first:
                        dve.wait_ge(S("aT_ps"), at("aT_ps", l, b - 1))
                    tt(act_a[j], sil[j], psb(1)[:, FF:2 * FF], ALU.mult).then_inc(S("a_sb"), 1)

                def rows_out(b, j, stored=None):
                    dve.wait_ge(S("y_ps"), at("y_ps", l, b + 1))
                    if stored is not None:
                        dve.wait_ge(S(f"y_st{j}"), at(f"y_st{j}", l, stored))
                    cp(ysb[j], psb(2 + j)).then_inc(S("y_sb"), 1)

                for b in range(3):
                    hidden(b, b % 2, b < 2)
                    if b:
                        rows_out(b - 1, (b - 1) % 2)
                with dve.Fori(0, (nb - 3) // 2) as i:
                    for j in range(2):
                        par = (3 + j) % 2
                        b = i * 2 + (3 + j)
                        hidden(b, par)
                        rows_out(b - 1, 1 - par, i * 16 + 16)
                rows_out(nb - 1, (nb - 1) % 2, 16 * ((nb - 1) // 2))

                for t in range(NT):
                    v = 0 if t < LT else 1
                    j = t % 2
                    dve.wait_ge(S(f"yg{j}"), at(f"yg{j}", l, 32 * (t // 2 + 1)))
                    if t:
                        dve.wait_ge(S("x_new"), at("x_new", l, t))
                    link(ts(ytmp, yg[j][0], gw[0][:, t:t + 1], None, ALU.mult))
                    link(stt(ytmp, yg[j][1], gw[1][:, t:t + 1], ytmp, ALU.mult, ALU.add))
                    ins = tt(ytmp, ytmp, mrow[:, v, 3, :], ALU.mult)
                    ins.then_inc(S("yg_free"), 1)
                    dve.wait_ge(S("yg_free"), at("yg_free", l, t + 1))
                    tt(x_t[:, t, :], x_t[:, t, :], ytmp, ALU.add).then_inc(S("x_new"), 1)

        @block.gpsimd
        def _(pool):
            chain = [0]

            def link(ins):
                chain[0] += 1
                ins.then_inc(S("pool_chain"), 1)
                pool.wait_ge(S("pool_chain"), chain[0])

            pool.dma_start(T[0:KD, P:2 * P], A["c"][0].rearrange("(k p) -> k p", p=P)).then_inc(S("c_rows"), 16)
            pool.dma_start(T[KD:2 * KD, P:2 * P], A["c_ctx"].rearrange("(k p) -> k p", p=P)).then_inc(S("c_rows"), 16)
            link(pool.memset(ident[:, :], 0.0))
            pool.affine_select(out=ident[:, :], in_=ident[:, :], compare_op=ALU.not_equal, fill=1.0, base=0,
                               pattern=[[-1, P]], channel_multiplier=1).then_inc(S("const"), 1)
            link(pool.memset(ones[:, :], 1.0))
            pool.affine_select(out=tri[:, :], in_=ones[:, :], compare_op=ALU.is_gt, fill=0.0, base=0,
                               pattern=[[1, P]], channel_multiplier=-1).then_inc(S("const"), 1)
            for l in range(DEPTH):
                for v in range(2):
                    pool.dma_start(MG[v * MC:(v + 1) * MC, (2 + l) * P:(3 + l) * P],
                                   A["mod_b"][l].rearrange("(c p) -> c p", p=P)).then_inc(S("mod_b"), 16)
            pool.dma_start(rwv, A["router_w"].rearrange("(k p) e -> p k e", p=P)).then_inc(S("const_dma"), 16)
            pool.dma_start(rbias[:, :], A["router_b"].rearrange("(a e) -> a e", a=1).partition_broadcast(P)).then_inc(S("const_dma"), 16)
            pool.dma_start(edge[:, :], A["edges"].rearrange("g e -> (g e)").rearrange("(a n) -> a n", a=1).partition_broadcast(P))\
                .then_inc(S("const_dma"), 16)

            def counter(dst, at_, n, base, step, channel):
                link(pool.iota(iint[:, at_:at_ + n], [[step, n]], base=base, channel_multiplier=channel))
                pool.tensor_copy(dst, iint[:, at_:at_ + n]).then_inc(S("const"), 1)

            counter(w4[:, :], 0, NG, NG, -1, 0)
            counter(w16[:, :], 4, NE, NE, -1, 0)
            counter(steps6[:, :], 20, 6, 0, P, 0)
            counter(blkno[:, :], 26, MAXB, 0, 1, 0)
            counter(tokf[:, :], 56, AT, 0, P, 1)
            pool.memset(zrow[:, :], 0.0).then_inc(S("const"), 1)
            pool.wait_ge(S("const"), 8)
            for l in range(DEPTH):
                pool.dma_start(token_of[l].rearrange("(p b) o -> p (b o)", p=P), zrow[:, :]).then_inc(S("tab_zero"), 16)
            for l in range(DEPTH):
                pool.wait_ge(S("mod_out"), l + 1)
                pool.dma_start(mod_rows[l].rearrange("v (c p) -> (v c) p", p=P), MG[0:2 * MC, l * P:(l + 1) * P])\
                    .then_inc(S("mod_st"), 16)
            pool.wait_ge(S("mod_st"), 16 * DEPTH)

            def row(a):
                return a.rearrange("(a n) -> a n", a=1).partition_broadcast(P)

            for l in range(DEPTH):
                NT = tiles(l)
                if l > 0:
                    pool.wait_ge(S("x_new"), at("x_new", l - 1, tiles(l - 1)))
                for v in range(2):
                    pool.dma_start(MG[:, v * 2 * D:(v + 1) * 2 * D], row(mod_rows[l, v, 0:2 * D])).then_inc(S("par_n1"), 16)
                pool.dma_start(gain1, row(A["norm1_g"][l])).then_inc(S("par_n1"), 16)
                for dst, src in ((g_kva, row(A["kv_a_norm_g"][l])), (g_qa, row(A["q_a_norm_g"][l])),
                                 (g_sgu, row(A["sgu_norm_g"][l])),
                                 (sguw, A["sgu_w"][l].rearrange("g p q -> p g q")),
                                 (crow[0:12, :], A["conv_w"][l].rearrange("k (c p) -> (k c) p", p=P)),
                                 (crow[12:16, :], A["pool_scale"][l].rearrange("(c p) -> c p", p=P)),
                                 (T[:, 1536:1792], A["rope"].rearrange("p s t e -> p (s t e)"))):
                    pool.dma_start(dst, src).then_inc(S("par_b"), 16)
                pool.dma_start(g_qk[:, 0, :], row(A["k_norm_g"][l])).then_inc(S("par_g"), 16)
                pool.dma_start(g_qk[:, 1, :], row(A["q_norm_g"][l])).then_inc(S("par_g"), 16)
                pool.dma_start(sgub, row(A["sgu_b"][l].rearrange("g q -> (g q)"))).then_inc(S("par_sb"), 16)
                pool.dma_start(poolw, A["pool_w"][l].rearrange("g c d -> c g d")).then_inc(S("par_p"), 16)
                pool.wait_ge(S("par_g"), at("par_g", l, 32))
                pool.wait_ge(S("par_b"), at("par_b", l, 16 * 7))
                link(pool.tensor_scalar(g_qk[:, 1, :], g_qk[:, 1, :], SCALE, None, ALU.mult))

                def squares(t):
                    n = 2 * H if t < NT else H
                    pool.wait_ge(S("raw"), at("raw", l, t + 1))
                    pool.wait_ge(S("cn"), at("cn", l, t + 1))
                    if t >= 2:
                        pool.wait_ge(S("t_ss"), at("t_ss", l, t - 1))
                    r = raw[t % 2].rearrange("p s h e -> p (s h e)")[:, 0:n * QK]
                    pool.tensor_tensor(sqb[t % 2][:, 0:n * QK], r, r, ALU.mult).then_inc(S("t_sqd"), 1)

                def rotate(t):
                    full = t < NT
                    pool.wait_ge(S("t_rn"), at("t_rn", l, t + 1))
                    for s in range(2 if full else 1):
                        ins = pool.tensor_tensor(qk[:, t, s], raw[t % 2][:, s], g_qk[:, s:s + 1, :].to_broadcast([P, H, QK]), ALU.mult)
                    if t >= LT:
                        ins.then_inc(S("t_qk"), 1)
                        return
                    link(ins)
                    n = 2 * H
                    r = qk[:, t].rearrange("p s h e -> p (s h) e")[:, :, NOPE:QK]
                    t1 = sqb[t % 2][:, 0:n * ROPE].rearrange("p (h e) -> p h e", h=n)
                    t2 = sqb[t % 2][:, n * ROPE:2 * n * ROPE].rearrange("p (h e) -> p h e", h=n)
                    pool.tensor_tensor(t1, r, cosv[:, t:t + 1, :].to_broadcast([P, n, ROPE]), ALU.mult)
                    link(pool.tensor_tensor(t2, r, sinv[:, t:t + 1, :].to_broadcast([P, n, ROPE]), ALU.mult))
                    pool.tensor_tensor(r[:, :, 0:HALF], t1[:, :, 0:HALF], t2[:, :, HALF:ROPE], ALU.subtract)
                    pool.tensor_tensor(r[:, :, HALF:ROPE], t2[:, :, 0:HALF], t1[:, :, HALF:ROPE], ALU.add).then_inc(S("t_qk"), 1)

                for t in range(AT + 1):
                    if t < AT:
                        squares(t)
                    if t >= 1:
                        rotate(t - 1)

                pool.wait_ge(S("o_tr"), at("o_tr", l, BC))
                for v in range(2):
                    pool.dma_start(QKB[:, v * 4 * D:(v + 1) * 4 * D], row(mod_rows[l, v, 2 * D:6 * D])).then_inc(S("par_n2"), 16)
                pool.dma_start(gain2, row(A["norm2_g"][l])).then_inc(S("par_n2"), 16)

                pool.wait_ge(S("tab_zero"), 16 * DEPTH)
                pool.wait_ge(S("slots"), at("slots", l, 1))
                for k in range(2):
                    for t in range(NT):
                        c = k * AT + t
                        pool.indirect_dma_start(out=token_of[l], out_offset=bass.IndirectOffsetOnAxis(slot_i[:, c:c + 1], 0),
                                                in_=tokf[:, t:t + 1], in_offset=None).then_inc(S("tab_st"), 16)
                pool.wait_ge(S("tab_st"), at("tab_st", l, 16 * 2 * NT))
                pool.dma_start(tabr, token_of[l].rearrange("(b p) o -> b (p o)", p=P)).then_inc(S("tab_ld"), 16)
                pool.wait_ge(S("tab_i"), at("tab_i", l, 1))
                for t in range(2):
                    pool.wait_ge(S(f"h2_st{t}"), at(f"h2_st{t}", l, 16 * ((NT + 1 - t) // 2)))
                pool.wait_ge(S("h2_tr"), at("h2_tr", l, NT))
                nb = expert_blocks(W(l))

                def gather(b, j, n, dyn=False):
                    src = tab_i[:, bass.ds(b, 1)] if dyn else tab_i[:, b:b + 1]
                    pool.tensor_copy(idx_i[j][:, :], src).then_inc(S("idx"), 1)
                    pool.wait_ge(S("idx"), at("idx", l, n + 1))
                    pool.sem_inc(S("idx_seen"), 1)
                    pool.indirect_dma_start(out=xg[j], out_offset=None, in_=h2_rows,
                                            in_offset=bass.IndirectOffsetOnAxis(idx_i[j][:, :], 0)).then_inc(S(f"xg{j}"), 16)

                gather(0, 0, 0)
                gather(1, 1, 1)
                with pool.Fori(0, (nb - 1) // 2) as i:
                    for j in range(2):
                        pool.wait_ge(S("xT_ps"), at("xT_ps", l, i * 2 + (1 + j)))
                        gather(i * 2 + (2 + j), j, i * 2 + (2 + j), True)
                for j in range(2):
                    pool.wait_ge(S(f"y_st{j}"), at(f"y_st{j}", l, 16 * ((nb + 1 - j) // 2)))
                for t in range(NT):
                    j = t % 2
                    if t >= 2:
                        pool.wait_ge(S("yg_free"), at("yg_free", l, t - 1))
                    for k in range(2):
                        c = k * AT + t
                        pool.indirect_dma_start(out=yg[j][k], out_offset=None, in_=y_rows[l],
                                                in_offset=bass.IndirectOffsetOnAxis(slot_i[:, c:c + 1], 0)).then_inc(S(f"yg{j}"), 16)
        return len(sems)


_INS = ["x", "c", "ctx", "c_ctx", "mod_w", "mod_b", "norm1_g", "norm2_g", "w_in", "kv_a_norm_g", "w_ukv", "k_norm_g",
        "q_a_norm_g", "w_uq", "q_norm_g", "conv_w", "pool_w", "pool_scale", "sgu_norm_g", "sgu_w", "sgu_b",
        "w_branch", "w_o", "router_w", "router_b", "moe_w1", "moe_w3", "moe_w2"]


def kernel(**inputs):
    import concourse.bacc as bacc
    from concourse.bass_utils import run_bass_kernel_spmd

    nc = bacc.Bacc("TRN2", target_bir_lowering=False, num_devices=1)
    arrays, aps = {}, {}
    tables = {"rope": rope_tables(), "edges": pool_edges()}
    for name in _INS + list(tables):
        a = np.ascontiguousarray(tables[name] if name in tables else inputs[name])
        arrays[f"in_{name}"] = a
        aps[name] = nc.dram_tensor(f"in_{name}", a.shape, mybir.dt.from_np(a.dtype), kind="ExternalInput").ap()
    out = nc.dram_tensor("out", [1, SEQ, D], F32, kind="ExternalOutput").ap()
    trunk(nc, aps, out)
    r = run_bass_kernel_spmd(nc, [arrays], core_ids=[0])
    return r.results[0]["out"]
```

```python
from contextlib import ExitStack

import numpy as np
import concourse.bass as bass
from concourse import mybir

F32 = mybir.dt.float32
F32R = mybir.dt.float32r
I32 = mybir.dt.int32
ALU = mybir.AluOpType
ACT = mybir.ActivationFunctionType
AX = mybir.AxisListType

P = 128
D = 1024
KD = D // P
DEPTH = 2
SEQ = 512
CTX = 256
TOK = SEQ + CTX
LT = SEQ // P
AT = TOK // P
N_MOD = 6
MC = N_MOD * KD
EPS = 1e-6
GRID_W = 64

BW = 512
BC = BW // P
H = 8
NOPE, ROPE, VD = 64, 32, 64
QK = NOPE + ROPE
HALF = ROPE // 2
AXIS_PAIRS = ROPE // 4
KV_LORA, Q_LORA = 128, 256
SCALE = QK ** -0.5

KR_OFF = KV_LORA
Q_OFF = KR_OFF + ROPE
CONV_OFF = Q_OFF + Q_LORA
POOL_OFF = CONV_OFF + 3 * BW
SGU_OFF = POOL_OFF + BW
GATE_OFF = SGU_OFF + 2 * BW
WINDOWS = (2, 4, 8, 16)

NE, NG = 16, 4
EG = NE // NG
FF = 256
BIG = 1.0e30

SLOTS = 6
SLAB = 2048
RAWS, RAW = 3, (KD + BC) * P
KVQ = CONV_OFF
KVQ_SPLIT = (3, 3, 2)

G_AT, S_V, S_U = 0, KD, KD + 4
G_SG = S_U + BC
S_CV = G_SG + KD
G_CV = S_CV + 3 * BC
S_PO = G_CV + KD
G_PO = S_PO + BC
S_WO = G_PO + KD
CHUNKS = S_WO + KD
SPLITS = len(KVQ_SPLIT) + CHUNKS
MAXB = (2 * TOK + NE * (P - 1)) // P

CVL, CVC, CVW = 1, 1 + SEQ + 2, SEQ + CTX + 4
PP = 8
PLL, PLC, PLW = PP, PP + SEQ + 2 * PP, SEQ + CTX + 4 * PP


def expert_blocks(tokens):
    return (2 * tokens + NE * (P - 1)) // P


def signals(name):
    steps, blocks = H * AT, expert_blocks(TOK)
    rounds = H * ((2 * AT + 3) // 4)
    once = "eid g_scaled n1_eps n1_rt n2_eps n2_rt r_oh r_s rank_ps slots sv_eps sv_rt t_sq t_eps t_rt tab_i tab_ps wT wT_tr"
    by_tile = ("cn cnT cn_tr h2T h2_tok h2_tr hT_hi hT_tile h_tok h_tr lg_ps n1_sq n2_sq sgv sv_sq t_gain t_hrt t_qk "
               "t_sqd t_ss x_new yg_free")
    by_chunk = "cv_cu o_tr po_mix po_pl po_pp sgu_mix sgu_sum sgu_u"
    by_step = "negmax o_ps o_sb prT_d pr_tr probs s_ps"
    by_block = "aT_ps aT_sb a_sb h_ps sil y_ps y_sb"
    counts = {
        **dict.fromkeys(once.split(), 1), **dict.fromkeys(by_tile.split(), AT), **dict.fromkeys(by_chunk.split(), BC),
        **dict.fromkeys(by_step.split(), steps), "prT_a": H * LT, **dict.fromkeys(by_block.split(), blocks),
        **dict.fromkeys(("g_prod", "g_ps", "g_sig"), 4 * KD), **dict.fromkeys(("qkT", "qk_tr"), rounds),
        **dict.fromkeys(("idx", "xT_ps", "xgT"), blocks + 1), **dict.fromkeys(("m_hi", "m_lo", "w_sc", "w_tr", "w_x"), KD),
        **dict.fromkeys(("up_ps", "up_sb"), 4 * AT), **dict.fromkeys(("br_hi", "br_lo"), 4 * BC),
        **dict.fromkeys(("w_hi", "w_lo"), SPLITS), "prod": CHUNKS, "tproj": 1, "cv_evac": 2 * BC, "cv_y": BC, "po_pad": 1,
        "h2_st0": 16 * (AT // 2), "h2_st1": 16 * (AT // 2), "par_b": 16 * 8, "par_g": 32, "par_n1": 48, "par_n2": 48,
        "par_p": 16, "par_sb": 16, "tab_ld": 16, "tab_st": 16 * 2 * AT, "x_back": 16 * AT,
        "xg0": 16 * (blocks // 2 + 1), "xg1": 16 * ((blocks + 1) // 2),
        "y_st0": 16 * ((blocks + 1) // 2), "y_st1": 16 * (blocks // 2), "yg0": 16 * AT, "yg1": 16 * AT,
    }
    return counts[name]


def latent_steps(n, nt):
    return n // nt * LT + min(n % nt, LT)


def rope_tables():
    t = np.arange(SEQ)
    grid = np.stack([t // GRID_W, t % GRID_W], -1).astype(np.float32)
    inv = (np.float32(10000.0) ** (-np.arange(AXIS_PAIRS, dtype=np.float32) / np.float32(AXIS_PAIRS))).astype(np.float32)
    ang = np.concatenate([grid[:, :1] * inv, grid[:, 1:] * inv], -1).astype(np.float32).astype(np.float64)
    tabs = [np.concatenate([f(ang), f(ang)], -1).astype(np.float32) for f in (np.cos, np.sin)]
    return np.ascontiguousarray(np.stack([x.reshape(LT, P, ROPE).transpose(1, 0, 2) for x in tabs], 1))


def pool_edges():
    rows = []
    for w in WINDOWS:
        first = [w / (min(j + w - w // 2, w)) for j in range(PP)]
        last = [w / (min(PP - j, w - w // 2) + w // 2) for j in range(PP)]
        rows.append(first + last)
    return np.asarray(rows, np.float32)


def trunk(nc, A, out):
    mod_rows = nc.dram_tensor("mod_rows", [DEPTH, 2, N_MOD * D], F32, kind="Internal").ap()
    x_spill = nc.dram_tensor("x_spill", [TOK, D], F32, kind="Internal").ap()
    h2_rows = nc.dram_tensor("h2_rows", [TOK, D], F32, kind="Internal").ap()
    token_of = [nc.dram_tensor(f"token_of_{l}", [(MAXB + 1) * P, 1], F32, kind="Internal").ap() for l in range(DEPTH)]
    y_rows = [nc.dram_tensor(f"y_rows_{l}", [expert_blocks(SEQ if l else TOK) * P, D], F32, kind="Internal").ap()
              for l in range(DEPTH)]

    with ExitStack() as ctx:
        free = [0]
        base = (nc.sbuf_base + 31) // 32 * 32

        def place(name, width, dt=F32, parts=P, over=None):
            at_ = free[0] if over is None else over
            if over is None:
                free[0] += (width + 7) // 8 * 8
            return nc.alloc_sbuf_tensor_at(name, [parts, width], dt, offset=base + 4 * at_)

        X = place("X", AT * D)
        HTF = place("HTF", 2 * KD * TOK)
        HTH = place("HTH", KD * TOK, F32R, over=AT * D)
        HTL = place("HTL", KD * TOK, F32R, over=2 * AT * D)
        br0 = free[0]
        BR = place("BR", 2 * BC * TOK)
        BRH = place("BRH", BC * TOK, F32R, over=br0)
        BRL = place("BRL", BC * TOK, F32R, over=br0 + BC * TOK)
        mg0 = free[0]
        MGZ = place("MGZ", 2 * KD * TOK)
        MGL = place("MGL", KD * TOK, F32R, over=mg0)
        MGH = place("MGH", KD * TOK, F32R, over=mg0 + KD * TOK)
        ring0 = free[0]
        RAWB = place("RAWB", RAWS * RAW)
        WS = place("WS", 2 * KD * KVQ, F32R)
        RING = place("RING", (SLOTS - 1) * SLAB, over=ring0)
        assert (SLOTS - 1) * SLAB <= free[0] - ring0 and 4 * RAW <= 2 * KD * KVQ
        t0 = free[0]
        T = place("T", 2304)
        SG = place("SG", 3 * BW)
        ident = place("ident", P)
        cw = place("cw", 16 + 2 * KD)
        edge = place("edge", 4 * 2 * PP)
        st = place("st", 2 * AT)
        rst = place("rst", 2 * AT)
        srt = place("srt", 2 * AT)
        scT = place("scT", 2 * KD)
        ps = ctx.enter_context(nc.psum_tensor("ps", [P, 4, 1024], F32))

        def W(l):
            return TOK if l < DEPTH - 1 else SEQ

        def tiles(l):
            return W(l) // P

        x_t = X[:, :].rearrange("p (t d) -> p t d", t=AT)
        hH, hL = (a[:, :].rearrange("p (k t) -> p k t", k=KD) for a in (HTH, HTL))
        brH, brL = (a[:, :].rearrange("p (c t) -> p c t", c=BC) for a in (BRH, BRL))
        mH, mL = (a[:, :].rearrange("p (k t) -> p k t", k=KD) for a in (MGH, MGL))
        BRA, BRB = BR[:, 0:BC * TOK], BR[:, BC * TOK:2 * BC * TOK]
        merged = MGZ[:, 0:KD * TOK].rearrange("p (k t) -> p k t", k=KD)
        qk = MGZ[:, 0:AT * 2 * H * QK].rearrange("p (t s h e) -> p t s h e", t=AT, s=2, h=H)
        vb = MGZ[:, AT * 2 * H * QK:AT * (2 * H * QK + BW)].rearrange("p (t c) -> p t c", t=AT)
        mod_sb = (HTF[0:2, 0:N_MOD * D], MGZ[0:2, KD * TOK:KD * TOK + N_MOD * D])

        kvqH, kvqL = (WS[:, j * KD * KVQ:(j + 1) * KD * KVQ].rearrange("p (k n) -> p k n", k=KD) for j in range(2))

        def raw_slab(r, n):
            return RAWB[:, r % RAWS * RAW:r % RAWS * RAW + n]

        def parts(s, n):
            return [WS[:, (2 * (s % 2) + j) * RAW:(2 * (s % 2) + j) * RAW + n] for j in range(2)]

        def words(s):
            gate = any(g <= s < g + KD for g in (G_AT, G_SG, G_CV, G_PO))
            return RAW if gate else KD * P

        def slot(s):
            return RING[:, s * SLAB:(s + 1) * SLAB] if s < SLOTS - 1 else HTF[:, 8 * D:8 * D + SLAB]

        def slot3(s, a):
            return slot(s).rearrange("p (a n) -> p a n", a=a)

        def psb(i):
            return ps[:, i, :]

        def bank(i):
            return ps[:, i // 2, (i % 2) * 512:(i % 2 + 1) * 512]

        def shift1(v):
            return MGZ[:, v * 2 * D:v * 2 * D + D]

        def scale1(v):
            return MGZ[:, v * 2 * D + D:(v + 1) * 2 * D]

        gain1 = MGZ[:, 4 * D:5 * D]
        sgub = SG[:, 0:BW]
        sguwT = SG[:, BW:2 * BW].rearrange("p (g q) -> p g q", g=BC)
        g_sgu = SG[:, 2 * BW:3 * BW]
        htok = [BRA[:, j * D:(j + 1) * D] for j in range(2)]
        sguw = BRA[:, 2 * D:2 * D + BW].rearrange("p (g q) -> p g q", g=BC)
        crow = BR[0:16 + 2 * KD, 2 * D + BW:2 * D + BW + P]
        g_kva = BRB[:, 0:128]
        g_qa = BRB[:, 128:384]
        g_qk = BRB[:, 384:384 + 2 * QK].rearrange("p (s e) -> p s e", s=2)
        PARAMS = 576
        cn = [T[:, j * 384:(j + 1) * 384] for j in range(2)]
        cnT = [T[:, 768 + j * 384:768 + (j + 1) * 384] for j in range(2)]
        cosv = T[:, 1536:1536 + LT * ROPE].rearrange("p (t e) -> p t e", t=LT)
        sinv = T[:, 1664:1664 + LT * ROPE].rearrange("p (t e) -> p t e", t=LT)
        ssq = [T[:, 1792 + j * 16:1808 + j * 16] for j in range(2)]
        rsq = [T[:, 1824 + j * 16:1840 + j * 16] for j in range(2)]
        raw = [X[:, j * 1536:(j + 1) * 1536].rearrange("p (s h e) -> p s h e", s=2, h=H) for j in range(2)]
        sqb = [X[:, 3072 + j * 1536:3072 + (j + 1) * 1536] for j in range(2)]
        sqj = [X[:, 3072 + t * 384:3072 + (t + 1) * 384] for t in range(AT)]
        sgv = X[:, 0:AT * BW].rearrange("p (t c) -> p t c", t=AT)
        uT = [X[:, AT * BW + g * TOK:AT * BW + (g + 1) * TOK] for g in range(BC)]
        umix = [T[:, j * TOK:(j + 1) * TOK] for j in range(2)]
        gcs = [X[:, j * TOK:(j + 1) * TOK] for j in range(2)]
        gbs = [X[:, (2 + j) * TOK:(3 + j) * TOK] for j in range(2)]
        cup = [X[:, 4 * TOK + j * CVW:4 * TOK + (j + 1) * CVW] for j in range(2)]
        cvy = [T[:, j * CVW:(j + 1) * CVW] for j in range(2)]
        poolw = X[:, 5400:5400 + BC * P].rearrange("p (g d) -> p g d", g=BC)
        pp = [X[:, j * PLW:(j + 1) * PLW] for j in range(2)]
        pacc = [X[:, (2 + j) * PLW:(3 + j) * PLW] for j in range(2)]
        pooled = [X[:, 4 * PLW + j * TOK:4 * PLW + (j + 1) * TOK] for j in range(2)]
        obuf = X[:, 0:AT * BW].rearrange("p (t c) -> p t c", t=AT)
        qkT = [X[:, 3072 + j * 1536:3072 + (j + 1) * 1536] for j in range(2)]
        probs = [BRB[:, j * TOK:(j + 1) * TOK] for j in range(2)]
        prT = [BRB[:, (2 + j) * TOK:(3 + j) * TOK] for j in range(2)]
        negm = T[:, 0:H * AT]
        rsum = T[:, 64:64 + H * AT]
        rinv = T[:, 128:128 + H * AT]
        sig = [T[:, j * TOK:(j + 1) * TOK] for j in range(2)]
        prod = T[:, 2 * TOK:3 * TOK]
        wsc = sig
        mrow = HTF[:, 0:2 * 3 * D].rearrange("p (v m d) -> p v m d", v=2, m=3)
        gain2 = HTF[:, 6 * D:7 * D]
        h2tok = htok
        late = MGZ[:, 7 * D:12 * D]
        h2T = [late[:, j * D:(j + 1) * D].rearrange("p (k t) -> p k t", k=KD) for j in range(2)]
        junk = BRB[:, 2 * D:3 * D]
        xg = htok
        xgT = h2T
        sil = [late[:, 2 * D + j * FF:2 * D + (j + 1) * FF] for j in range(2)]
        act_a = [late[:, 2 * D + (2 + j) * FF:2 * D + (3 + j) * FF] for j in range(2)]
        act_T = [late[:, 3 * D + j * FF:3 * D + (j + 1) * FF].rearrange("p (k t) -> p k t", k=2) for j in range(2)]
        ysb = [MGZ[:, (5 + j) * D:(6 + j) * D] for j in range(2)]
        yg = [[HTF[:, (3 * j + k) * D:(3 * j + k + 1) * D] for k in range(2)] for j in range(2)]
        ytmp = late[:, 4 * D:5 * D]
        cursor = [PARAMS]

        def rt(*shape):
            n = int(np.prod(shape))
            a = BRB[:, cursor[0]:cursor[0] + n]
            cursor[0] += n
            if len(shape) == 1:
                return a
            names = "abcd"[:len(shape)]
            return a.rearrange(f"p ({' '.join(names)}) -> p {' '.join(names)}",
                               **{n_: s for n_, s in zip(names[:-1], shape[:-1])})

        r_s, r_sb, r_m, r_sc = rt(AT, NE), rt(AT, NE), rt(AT, NE), rt(AT, NE)
        r_oh = [rt(AT, NE), rt(AT, NE)]
        r_pair = rt(AT * NG, 6)
        r_gs, r_gq, r_gm = rt(AT, NG), rt(AT, NG), rt(AT, NG)
        r_mx = rt(AT)
        r_w = [rt(AT), rt(AT)]
        r_den = rt(AT)
        r_cnt = rt(NE, 6)
        r_nb, r_end, r_base = rt(NE), rt(NE), rt(NE)
        r_slot = rt(2, AT)
        r_blk = rt(MAXB, NE)
        r_eid = rt(MAXB)
        assert cursor[0] <= BC * TOK
        slot_i = place("slot_i", 2 * AT, I32)
        eid_i = place("eid_i", MAXB + 1, I32)
        tab_i = place("tab_i", MAXB + 1, I32)
        idx_i = [place(f"idx_i{j}", 1, I32) for j in range(2)]
        tabr = T[0:MAXB + 1, 0:P]
        gw = [r_w[0], r_w[1]]
        rw = place("rw", KD * NE)
        rwv = rw[:, :].rearrange("p (k e) -> p k e", k=KD)
        rbias = place("rbias", NE)
        ones = place("ones", P)
        tri = place("tri", P)
        w4 = place("w4", NG)
        w16 = place("w16", NE)
        steps6 = place("steps6", 6)
        blkno = place("blkno", MAXB)
        tokf = place("tokf", AT)
        zrow = place("zrow", MAXB + 1, over=t0 + 1856)
        iint = place("iint", 64, I32, over=t0 + 1920)

        sems = {}

        def S(name):
            if name not in sems:
                sems[name] = ctx.enter_context(nc.semaphore(name))
            return sems[name]

        def at(name, l, n):
            return n + (signals(name) if l else 0)

        slab_full = [S(f"slab_full{s}") for s in range(SLOTS)]
        slab_used = S("slab_used")
        raw_full = [S(f"raw_full{s}") for s in range(RAWS)]

        def split_no(l, s):
            return at("w_lo", l, len(KVQ_SPLIT) + s + 1)

        def done_no(l, s):
            return at("prod", l, s + 1)

        def cols(w, c0, n):
            return w[:, c0:c0 + n].rearrange("(k p) n -> p k n", p=P)

        def raw_loads(l):
            w_in, k0, r = A["w_in"][l], 0, []
            for n in KVQ_SPLIT:
                r.append([(0, n, KVQ, w_in[k0 * P:(k0 + n) * P, 0:KVQ].rearrange("(k p) n -> p k n", p=P))])
                k0 += n
            r.append([(0, 1, D, A["w_ukv"][l].rearrange("p (a h) e -> p a (h e)", a=1))])
            r.append([(0, 2, H * QK, A["w_uq"][l].rearrange("(k p) h e -> p k (h e)", p=P))])

            def gate(n):
                return [[(0, KD, P, cols(w_in, GATE_OFF + n * D + d * P, P)),
                         (KD * P, BC, P, A["w_branch"][l, n][:, d * P:(d + 1) * P].rearrange("(k p) n -> p k n", p=P))]
                        for d in range(KD)]

            def plain(w, c0):
                return [(0, KD, P, cols(w, c0, P))]

            r += gate(0)
            v0 = SGU_OFF + BW
            r += [[(0, 2, BW, w_in[2 * j * P:2 * (j + 1) * P, v0:v0 + BW].rearrange("(k p) n -> p k n", p=P))] for j in range(4)]
            r += [plain(w_in, SGU_OFF + g * P) for g in range(BC)]
            r += gate(3)
            r += [plain(w_in, CONV_OFF + part * BW + c * P) for c in range(BC) for part in (1, 0, 2)]
            r += gate(1)
            r += [plain(w_in, POOL_OFF + g * P) for g in range(BC)]
            r += gate(2)
            r += [plain(A["w_o"][l], n * P) for n in range(KD)]
            return r

        loads = [raw_loads(l) for l in range(DEPTH)]
        FIRST = len(KVQ_SPLIT) + 2
        assert FIRST + CHUNKS == len(loads[0]) and len(loads[0]) % RAWS == 0
        full_no, sums = {}, [0] * RAWS
        for l_ in range(DEPTH):
            for r_, pieces in enumerate(loads[l_]):
                sums[r_ % RAWS] += 16 * len(pieces)
                full_no[l_, r_] = sums[r_ % RAWS]

        def up_items(l, t):
            return 4 * min(t, tiles(l)) + 2 * max(t - tiles(l), 0)

        block = ctx.enter_context(nc.Block())

        @block.sync
        def _(sp):
            issued = [0]

            def load(shape, src, before=None, at=None):
                n = issued[0] if at is None else at
                if n >= SLOTS or before is not None:
                    need = n - SLOTS + 1
                    sp.wait_ge(slab_used, need if before is None else before + need)
                a, m = shape
                sp.dma_start(slot(n % SLOTS)[:, 0:a * m].rearrange("p (a m) -> p a m", a=a), src)\
                    .then_inc(slab_full[n % SLOTS], 16)
                if at is None:
                    issued[0] += 1

            def mod_cols(l, c0):
                return A["mod_w"][l][:, c0].rearrange("(k p) n -> p k n", p=P)

            for j in range(SLOTS):
                load((KD, 256), mod_cols(0, slice(j * 256, (j + 1) * 256)))
            for l in range(DEPTH):
                start = 1 if l == 0 else 0
                turn0 = l * MC // 2
                with sp.Fori(start, MC // (2 * SLOTS)) as i:
                    for j in range(SLOTS):
                        load((KD, 256), mod_cols(l, bass.ds(i * (256 * SLOTS) + j * 256, 256)), i * SLOTS, turn0 + j)
                issued[0] = (l + 1) * MC // 2

            for l in range(DEPTH):
                if l == 0:
                    sp.wait_ge(S("mod_row"), DEPTH * MC // 2)
                else:
                    sp.wait_ge(S("y_sb"), at("y_sb", l - 1, expert_blocks(W(l - 1))))
                for r, pieces in enumerate(loads[l]):
                    if RAWS <= r < FIRST + 1:
                        sp.wait_ge(S("w_lo"), at("w_lo", l, r - RAWS + 1))
                    elif FIRST + 1 <= r < FIRST + RAWS:
                        sp.wait_ge(S("up_sb"), at("up_sb", l, up_items(l, AT)))
                    elif r >= FIRST + RAWS:
                        sp.wait_ge(S("w_lo"), split_no(l, r - FIRST - RAWS))
                    for o, a, m, src in pieces:
                        sp.dma_start(raw_slab(r, RAW)[:, o:o + a * m].rearrange("p (a m) -> p a m", a=a), src)\
                            .then_inc(raw_full[r % RAWS], 16)
                nb = expert_blocks(W(l))
                w1, w3, w2 = A["moe_w1"][l], A["moe_w3"][l], A["moe_w2"][l]
                sp.wait_ge(S("eid"), at("eid", l, 1))

                def up(b, n, before=None):
                    e = sp.value_load(eid_i[0:1, b] if before is None else eid_i[0:1, bass.ds(b, 1)],
                                      min_val=0, max_val=NE - 1)
                    for w in (w1, w3):
                        load((KD, FF), w[bass.ds(e, 1)].rearrange("e (k p) n -> p (e k) n", p=P), before, n)
                        n = None if n is None else n + 1

                def down(b, n, before=None):
                    e = sp.value_load(eid_i[0:1, b] if before is None else eid_i[0:1, bass.ds(b, 1)],
                                      min_val=0, max_val=NE - 1)
                    load((2, D), w2[bass.ds(e, 1)].rearrange("e (k p) n -> p (e k) n", p=P), before, n)

                up(slice(0, 1), None)
                for b in (1, 2):
                    up(slice(b, b + 1), None)
                    down(slice(b - 1, b), None)
                n0 = issued[0]
                with sp.Fori(0, (nb - 3) // 2) as i:
                    for j in range(2):
                        up(i * 2 + (3 + j), n0 + 3 * j, i * SLOTS)
                        down(i * 2 + (2 + j), n0 + 3 * j + 2, i * SLOTS)
                issued[0] += 3 * (nb - 3)
                down(slice(nb - 1, nb), None)
            sp.wait_ge(S("x_stored"), 16 * LT)

        @block.tensor
        def _(pe):
            used = [0]
            owed = [0]
            mm = pe.matmul

            def pays(ins):
                if owed[0]:
                    ins.then_inc(slab_used, owed[0])
                    owed[0] = 0

            def arrived():
                n = used[0]
                pe.wait_ge(slab_full[n % SLOTS], 16 * (n // SLOTS + 1))
                used[0] += 1
                return n % SLOTS

            def three(out, w, x, n, first, stop):
                (wh, wl), (xh, xl) = w, x
                for i, (a, b) in enumerate(((wh, xh), (wh, xl), (wl, xh))):
                    last = mm(out, a, b, start=(first and i == 0), stop=(stop and i == 2))
                return last

            def chunk(l, s, x, pair, k0=0, kn=KD):
                w = [a.rearrange("p (k n) -> p k n", n=P) for a in parts(s, words(s))]
                last = None
                for k in range(kn):
                    for i, (a, b) in enumerate(((w[0], x[0]), (w[0], x[1]), (w[1], x[0]))):
                        go, end = k == 0 and i == 0, k == kn - 1 and i == 2
                        last = mm(psb(pair)[:, 0:SEQ], a[:, k0 + k, :], b[:, k, 0:SEQ], start=go, stop=end)
                        if W(l) > SEQ:
                            last = mm(psb(pair)[:, SEQ:TOK], a[:, k0 + k, :], b[:, k, SEQ:TOK], start=go, stop=end)
                return last

            pe.wait_ge(S("const"), 2)
            pe.wait_ge(S("c_silu"), 1)
            pe.transpose(psb(3)[:, 0:2 * KD], T[0:2 * KD, 0:P], ident[0:2 * KD, 0:2 * KD]).then_inc(S("c_tr"), 1)
            pe.wait_ge(S("c_col"), 1)
            scv = scT[:, :].rearrange("p (v k) -> p v k", v=2)

            def mod_slab(j, first, read=None):
                if read is not None:
                    pe.wait_ge(S("mod_row"), read)
                for k in range(KD):
                    last = mm(psb(j // 2)[0:2, (j % 2) * 512:(j % 2) * 512 + 256], scv[:, :, k], slot3(j, KD)[:, k, :],
                              start=(k == 0), stop=(k == KD - 1))
                    if k == 0 and not first:
                        last.then_inc(slab_used, 1)
                last.then_inc(S("mod_ps"), 1)

            for j in range(SLOTS):
                pe.wait_ge(slab_full[j], 16)
                mod_slab(j, j == 0)
            for l in range(DEPTH):
                turn0 = l * MC // (2 * SLOTS)
                with pe.Fori(1 if l == 0 else 0, MC // (2 * SLOTS)) as i:
                    for j in range(SLOTS):
                        pe.wait_ge(slab_full[j], i * 16 + 16 * (turn0 + 1))
                        mod_slab(j, False, i * SLOTS + ((turn0 - 1) * SLOTS + j + 1))
            used[0] = DEPTH * MC // 2
            owed[0] = 1
            pe.wait_ge(S("mod_row"), used[0])

            for l in range(DEPTH):
                NT = tiles(l)
                for t in range(AT):
                    pe.wait_ge(S("h_tok"), at("h_tok", l, t + 1))
                    if t >= 2:
                        pe.wait_ge(S("hT_tile"), at("hT_tile", l, t - 1))
                    for k in range(KD):
                        last = pe.transpose(psb(t % 2)[:, k * P:(k + 1) * P], htok[t % 2][:, k * P:(k + 1) * P], ident[:, :])
                        if k == 0:
                            pays(last)
                    last.then_inc(S("h_tr"), 1)

                pe.wait_ge(S("hT_tile"), at("hT_tile", l, AT))
                k0 = 0
                for i, kn in enumerate(KVQ_SPLIT):
                    pe.wait_ge(S("w_lo"), at("w_lo", l, i + 1))
                    for t in range(AT):
                        n = KVQ if t < NT else Q_OFF
                        for k in range(k0, k0 + kn):
                            tok = slice(t * P, (t + 1) * P)
                            last = three(bank(t)[:, 0:n], (hH[:, k, tok], hL[:, k, tok]), (kvqH[:, k, 0:n], kvqL[:, k, 0:n]),
                                         n, k == 0, k == KD - 1)
                    k0 += kn
                last.then_inc(S("tproj"), 1)

                wukv, wuq = raw_slab(3, D), raw_slab(4, 2 * H * QK).rearrange("p (k n) -> p k n", k=2)
                pe.wait_ge(raw_full[0], full_no[l, 3])
                pe.wait_ge(raw_full[1], full_no[l, 4])
                for u in range(AT):
                    pe.wait_ge(S("cn"), at("cn", l, u + 1))
                    for j in range(3 if u < NT else 1):
                        last = pe.transpose(bank(u)[:, j * P:(j + 1) * P], cn[u % 2][:, j * P:(j + 1) * P], ident[:, :])
                    last.then_inc(S("cn_tr"), 1)
                    n0 = up_items(l, u)
                    pe.wait_ge(S("cnT"), at("cnT", l, u + 1))
                    for j in range(2):
                        if u:
                            pe.wait_ge(S("up_sb"), at("up_sb", l, n0 - 2 * j if u <= NT else n0 - 1 + j))
                        mm(bank(6 + j), cnT[u % 2][:, 0:P], wukv[:, j * 512:(j + 1) * 512], start=True, stop=True)\
                            .then_inc(S("up_ps"), 1)
                    if u < NT:
                        for j in range(2):
                            if j:
                                pe.wait_ge(S("up_sb"), at("up_sb", l, n0 + 1))
                            o = bank(6 if j else u)[:, 0:384]
                            for k in range(2):
                                last = mm(o, cnT[u % 2][:, (1 + k) * P:(2 + k) * P], wuq[:, k, j * 384:(j + 1) * 384],
                                          start=(k == 0), stop=(k == 1))
                            last.then_inc(S("up_ps"), 1)
                pe.wait_ge(S("up_sb"), at("up_sb", l, up_items(l, AT)))
                pe.wait_ge(S("par_b"), at("par_b", l, 16 * 8))
                for g in range(BC):
                    pe.transpose(bank(6)[:, g * P:(g + 1) * P], sguw[:, g, :], ident[:, :])
                nc_ = 16 + 2 * KD
                pe.transpose(bank(7)[:, 0:nc_], crow, ident[0:nc_, 0:nc_]).then_inc(S("wT_tr"), 1)
                pe.wait_ge(S("wT"), at("wT", l, 1))

                def gated(q, s0):
                    pe.wait_ge(S("br_lo"), at("br_lo", l, (q + 1) * BC))
                    for d in range(KD):
                        u = q * KD + d
                        pe.wait_ge(S("w_lo"), split_no(l, s0 + d))
                        if d >= 2:
                            pe.wait_ge(S("g_sig"), at("g_sig", l, u - 1))
                        chunk(l, s0 + d, (hH, hL), u % 2).then_inc(S("g_ps"), 1)
                        if d >= 2:
                            pe.wait_ge(S("g_prod"), at("g_prod", l, u - 1))
                        chunk(l, s0 + d, (brH, brL), 2 + u % 2, KD, BC).then_inc(S("prod"), 1)
                    pe.wait_ge(S("g_sig"), at("g_sig", l, (q + 1) * KD))
                    pe.wait_ge(S("g_prod"), at("g_prod", l, (q + 1) * KD))

                pe.wait_ge(S("t_qk"), at("t_qk", l, AT))
                steps = [(h, t) for h in range(H) for t in range(NT)]
                rounds = (AT + NT + 3) // 4

                def transposes(h, r):
                    n = h * rounds + r
                    if n >= 1:
                        pe.wait_ge(S("qkT"), at("qkT", l, n))
                    for i in range(4 * r, min(4 * r + 4, AT + NT)):
                        src = qk[:, i, 0, h, :] if i < AT else qk[:, i - AT, 1, h, :]
                        last = pe.transpose(psb(3)[0:QK, 512 + (i % 4) * P:512 + (i % 4 + 1) * P], src, ident[:, :])
                    last.then_inc(S("qk_tr"), 1)

                def key_tiles(t):
                    return range(0, AT) if t < LT else range(LT, AT)

                for r in range(rounds):
                    transposes(0, r)
                for n in range(len(steps) + 2):
                    if n < len(steps):
                        h, t = steps[n]
                        if t == 0:
                            pe.wait_ge(S("qkT"), at("qkT", l, (h + 1) * rounds))
                        if n >= 2:
                            pe.wait_ge(S("probs"), at("probs", l, n - 1))
                        q = qkT[h % 2][0:QK, (AT + t) * P:(AT + t + 1) * P]
                        if t < LT:
                            mm(psb(n % 2)[:, 0:SEQ], q, qkT[h % 2][0:QK, 0:SEQ], start=True, stop=True)
                        mm(psb(n % 2)[:, SEQ:TOK], q, qkT[h % 2][0:QK, SEQ:TOK], start=True, stop=True)\
                            .then_inc(S("s_ps"), 1)
                        if h + 1 < H and t < rounds:
                            transposes(h + 1, t)
                    if 1 <= n <= len(steps):
                        m = n - 1
                        h, t = steps[m]
                        pe.wait_ge(S("probs"), at("probs", l, m + 1))
                        if m >= 1:
                            pe.wait_ge(S("prT_a"), at("prT_a", l, latent_steps(m, NT)))
                            pe.wait_ge(S("prT_d"), at("prT_d", l, m))
                        for kt in key_tiles(t):
                            last = pe.transpose(psb(2)[:, kt * P:(kt + 1) * P], probs[m % 2][:, kt * P:(kt + 1) * P], ident[:, :])
                        last.then_inc(S("pr_tr"), 1)
                    if n >= 2:
                        m = n - 2
                        h, t = steps[m]
                        pe.wait_ge(S("prT_a"), at("prT_a", l, latent_steps(m + 1, NT)))
                        pe.wait_ge(S("prT_d"), at("prT_d", l, m + 1))
                        if m >= 1:
                            pe.wait_ge(S("o_sb"), at("o_sb", l, m))
                        ks = list(key_tiles(t))
                        for kt in ks:
                            last = mm(psb(3)[:, (m % 2) * VD:(m % 2 + 1) * VD], prT[m % 2][:, kt * P:(kt + 1) * P],
                                      vb[:, kt, h * VD:(h + 1) * VD], start=(kt == ks[0]), stop=(kt == ks[-1]))
                        last.then_inc(S("o_ps"), 1)
                pe.wait_ge(S("o_sb"), at("o_sb", l, len(steps)))
                for c in range(BC):
                    if c >= 2:
                        pe.wait_ge(S("br_lo"), at("br_lo", l, c - 1))
                    for t in range(NT):
                        last = pe.transpose(psb(c % 2)[:, t * P:(t + 1) * P], obuf[:, t, c * P:(c + 1) * P], ident[:, :])
                    last.then_inc(S("o_tr"), 1)
                gated(0, G_AT)

                for j in range(4):
                    pe.wait_ge(S("w_lo"), split_no(l, S_V + j))
                    w = [a.rearrange("p (k n) -> p k n", n=BW) for a in parts(S_V + j, 2 * BW)]
                    for t in range(NT):
                        for i in range(2):
                            k, tok = 2 * j + i, slice(t * P, (t + 1) * P)
                            last = three(bank(t), (hH[:, k, tok], hL[:, k, tok]), (w[0][:, i, :], w[1][:, i, :]),
                                         BW, k == 0, k == KD - 1)
                    last.then_inc(S("prod"), 1)
                home = (3, 0, 1, 2)
                for g in range(BC):
                    pe.wait_ge(S("w_lo"), split_no(l, S_U + g))
                    if g:
                        pe.wait_ge(S("sv_sq"), at("sv_sq", l, min(2 * g, NT)))
                    chunk(l, S_U + g, (hH, hL), home[g]).then_inc(S("prod"), 1)
                pe.wait_ge(S("sgv"), at("sgv", l, NT))
                for g in range(BC):
                    pe.wait_ge(S("sgu_u"), at("sgu_u", l, g + 1))
                    for t in range(NT):
                        last = mm(psb(home[g])[:, t * P:(t + 1) * P], sgv[:, t, g * P:(g + 1) * P], sguwT[:, g, :],
                                  start=True, stop=True)
                    last.then_inc(S("sgu_mix"), 1)
                gated(1, G_SG)

                for c in range(BC):
                    for j in range(3):
                        w = 3 * c + j
                        pe.wait_ge(S("w_lo"), split_no(l, S_CV + w))
                        if w >= 4:
                            pc, pj = divmod(w - 4, 3)
                            if pj < 2:
                                pe.wait_ge(S("cv_evac"), at("cv_evac", l, 2 * pc + pj + 1))
                            else:
                                pe.wait_ge(S("cv_cu"), at("cv_cu", l, pc + 1))
                        chunk(l, S_CV + w, (hH, hL), w % 4).then_inc(S("prod"), 1)
                pe.wait_ge(S("cv_evac"), at("cv_evac", l, 2 * BC))
                gated(2, G_CV)

                pe.wait_ge(S("par_p"), at("par_p", l, 16))
                for g in range(BC + 1):
                    if g < BC:
                        pe.wait_ge(S("w_lo"), split_no(l, S_PO + g))
                        if g >= 2:
                            pe.wait_ge(S("po_pp"), at("po_pp", l, g - 1))
                        chunk(l, S_PO + g, (hH, hL), g % 2).then_inc(S("prod"), 1)
                    if g >= 1:
                        h = g - 1
                        pe.wait_ge(S("po_pl"), at("po_pl", l, h + 1))
                        if h >= 2:
                            pe.wait_ge(S("br_lo"), at("br_lo", l, 3 * BC + h - 1))
                        last = mm(psb(2 + h % 2)[:, 0:SEQ], poolw[:, h, :], pooled[h % 2][:, 0:SEQ], start=True, stop=True)
                        if W(l) > SEQ:
                            last = mm(psb(2 + h % 2)[:, SEQ:TOK], poolw[:, h, :], pooled[h % 2][:, SEQ:TOK], start=True, stop=True)
                        last.then_inc(S("po_mix"), 1)
                gated(3, G_PO)

                pe.wait_ge(S("m_lo"), at("m_lo", l, KD))
                for n in range(KD + 1):
                    if n < KD:
                        pe.wait_ge(S("w_lo"), split_no(l, S_WO + n))
                        if n >= 2:
                            pe.wait_ge(S("w_sc"), at("w_sc", l, n - 1))
                        chunk(l, S_WO + n, (mH, mL), n % 2).then_inc(S("prod"), 1)
                    if n >= 1:
                        m = n - 1
                        pe.wait_ge(S("w_sc"), at("w_sc", l, m + 1))
                        if m >= 2:
                            pe.wait_ge(S("w_x"), at("w_x", l, m - 1))
                        for t in range(NT):
                            last = pe.transpose(psb(2 + m % 2)[:, t * P:(t + 1) * P], wsc[m % 2][:, t * P:(t + 1) * P], ident[:, :])
                        last.then_inc(S("w_tr"), 1)

                pe.wait_ge(S("const_dma"), 48)
                for t in range(NT + 1):
                    if t < NT:
                        pe.wait_ge(S("h2_tok"), at("h2_tok", l, t + 1))
                        if t == 0:
                            pe.wait_ge(S("w_x"), at("w_x", l, KD))
                        if t >= 2:
                            pe.wait_ge(S("h2T"), at("h2T", l, t - 1))
                        for k in range(KD):
                            last = pe.transpose(psb(t % 2)[:, k * P:(k + 1) * P], h2tok[t % 2][:, k * P:(k + 1) * P], ident[:, :])
                            if k == 0:
                                pays(last)
                        last.then_inc(S("h2_tr"), 1)
                    if t >= 1:
                        u = t - 1
                        pe.wait_ge(S("h2T"), at("h2T", l, u + 1))
                        for k in range(KD):
                            last = mm(psb(3)[:, u * NE:(u + 1) * NE], h2T[u % 2][:, k, :], rwv[:, k, :],
                                      start=(k == 0), stop=(k == KD - 1))
                        last.then_inc(S("lg_ps"), 1)

                pe.wait_ge(S("r_oh"), at("r_oh", l, 1))
                for t in range(NT + 1):
                    o = psb(2)[:, t * NE:(t + 1) * NE]
                    prev = list(range(t))
                    for i, u in enumerate(prev):
                        for k in range(2):
                            last = mm(o, ones[:, :], r_oh[k][:, u, :], start=(i == 0 and k == 0),
                                      stop=(t == NT and i == len(prev) - 1 and k == 1))
                    if t < NT:
                        for k in range(2):
                            last = mm(o, tri[:, :], r_oh[k][:, t, :], start=(t == 0 and k == 0), stop=(k == 1))
                last.then_inc(S("rank_ps"), 1)
                nb = expert_blocks(W(l))
                pe.wait_ge(S("tab_ld"), at("tab_ld", l, 16))
                pe.transpose(psb(3)[:, 0:MAXB + 1], tabr, ident[0:MAXB + 1, 0:MAXB + 1]).then_inc(S("tab_ps"), 1)

                def gather_T(b, j, first=False):
                    pe.wait_ge(S(f"xg{j}"), at(f"xg{j}", l, (b // 2 + 1) * 16 if isinstance(b, int) else b))
                    for k in range(KD):
                        last = pe.transpose(psb(0)[:, k * P:(k + 1) * P], xg[j][:, k * P:(k + 1) * P], ident[:, :])
                        if k == 0:
                            pays(last)
                    last.then_inc(S("xT_ps"), 1)

                def hidden(j, s1, s3):
                    for s, o in ((s1, 0), (s3, FF)):
                        for k in range(KD):
                            last = mm(psb(1)[:, o:o + FF], xgT[j][:, k, :], slot3(s, KD)[:, k, :],
                                      start=(k == 0), stop=(k == KD - 1))
                        last.then_inc(slab_used if s == s1 else S("h_ps"), 1)
                    owed[0] += 1

                def down(j, s2):
                    w = slot3(s2, 2)
                    for n in range(2):
                        for k in range(2):
                            last = mm(psb(2 + j)[:, n * 512:(n + 1) * 512], act_T[j][:, k, :], w[:, k, n * 512:(n + 1) * 512],
                                      start=(k == 0), stop=(k == 1))
                    last.then_inc(S("y_ps"), 1)
                    owed[0] += 1

                def act_transpose(j):
                    for k in range(2):
                        last = pe.transpose(psb(1)[:, 512 + k * P:512 + (k + 1) * P], act_a[j][:, k * P:(k + 1) * P], ident[:, :])
                        if k == 0:
                            pays(last)
                    last.then_inc(S("aT_ps"), 1)

                pe.wait_ge(S("tab_i"), at("tab_i", l, 1))
                gather_T(0, 0)
                for b in range(3):
                    pe.wait_ge(S("xgT"), at("xgT", l, b + 1))
                    if b:
                        pe.wait_ge(S("a_sb"), at("a_sb", l, b))
                    hidden(b % 2, arrived(), arrived())
                    gather_T(b + 1, (b + 1) % 2)
                    if b:
                        pe.wait_ge(S("aT_sb"), at("aT_sb", l, b))
                        down((b - 1) % 2, arrived())
                    pe.wait_ge(S("a_sb"), at("a_sb", l, b + 1))
                    act_transpose(b % 2)
                n0 = used[0]
                with pe.Fori(0, (nb - 3) // 2) as i:
                    for j in range(2):
                        par = (3 + j) % 2
                        sl = [(n0 + 3 * j + c) % SLOTS for c in range(3)]
                        turn = [16 * ((n0 + 3 * j + c) // SLOTS + 1) for c in range(3)]
                        b = i * 2 + (3 + j)
                        pe.wait_ge(S("xgT"), at("xgT", l, b + 1))
                        pe.wait_ge(S("a_sb"), at("a_sb", l, b))
                        pe.wait_ge(slab_full[sl[0]], i * 16 + turn[0])
                        pe.wait_ge(slab_full[sl[1]], i * 16 + turn[1])
                        hidden(par, sl[0], sl[1])
                        gather_T(i * 16 + ((4 + j) // 2 + 1) * 16, 1 - par)
                        pe.wait_ge(S("aT_sb"), at("aT_sb", l, b))
                        pe.wait_ge(S("y_sb"), at("y_sb", l, b - 2))
                        pe.wait_ge(slab_full[sl[2]], i * 16 + turn[2])
                        down(1 - par, sl[2])
                        pe.wait_ge(S("a_sb"), at("a_sb", l, b + 1))
                        act_transpose(par)
                used[0] += 3 * (nb - 3)
                pe.wait_ge(S("aT_sb"), at("aT_sb", l, nb))
                pe.wait_ge(S("y_sb"), at("y_sb", l, nb - 2))
                down((nb - 1) % 2, arrived())

        @block.scalar
        def _(act):
            act_f = act.activation
            chain = [0]

            def link(ins):
                chain[0] += 1
                ins.then_inc(S("act_chain"), 1)
                act.wait_ge(S("act_chain"), chain[0])

            for t in range(AT):
                src = A["x"][0, t * P:(t + 1) * P, :] if t < LT else A["ctx"][0, (t - LT) * P:(t - LT + 1) * P, :]
                act.dma_start(x_t[:, t, :], src).then_inc(S("x_in"), 16)
            act.wait_ge(S("c_rows"), 32)
            act_f(T[0:2 * KD, 0:P], T[0:2 * KD, P:2 * P], ACT.Silu).then_inc(S("c_silu"), 1)
            act.wait_ge(S("c_tr"), 1)
            act_f(scT[:, :], psb(3)[:, 0:2 * KD], ACT.Copy).then_inc(S("c_col"), 1)
            act.wait_ge(S("c_col"), 1)

            for l in range(DEPTH):
                NT = tiles(l)
                if l == 0:
                    act.wait_ge(S("x_in"), 16 * AT)
                for t in range(AT):
                    if l > 0:
                        act.wait_ge(S("x_new"), at("x_new", l - 1, t + 1))
                    if t:
                        act.wait_ge(S("n1_sq"), at("n1_sq", l, t))
                    act_f(psb(3), x_t[:, t, :], ACT.Square, scale=D ** -0.5, accum_out=st[:, t:t + 1]).then_inc(S("n1_sq"), 1)
                act.wait_ge(S("n1_eps"), at("n1_eps", l, 1))
                act_f(srt[:, 0:AT], rst[:, 0:AT], ACT.Sqrt).then_inc(S("n1_rt"), 1)
                k0 = 0
                for i, kn in enumerate(KVQ_SPLIT):
                    act.wait_ge(raw_full[i], full_no[l, i])
                    act_f(kvqH[:, k0:k0 + kn, :], raw_slab(i, kn * KVQ).rearrange("p (k n) -> p k n", k=kn), ACT.Copy)\
                        .then_inc(S("w_hi"), 1)
                    k0 += kn
                for t in range(AT):
                    act.wait_ge(S("h_tr"), at("h_tr", l, t + 1))
                    act_f(hH[:, :, t * P:(t + 1) * P], psb(t % 2).rearrange("p (k t) -> p k t", k=KD), ACT.Copy)\
                        .then_inc(S("hT_hi"), 1)

                def evacuate(t):
                    full = t < NT
                    act.wait_ge(S("cn_tr"), at("cn_tr", l, t + 1))
                    n = 384 if full else P
                    act_f(cnT[t % 2][:, 0:n], bank(t)[:, 0:n], ACT.Copy).then_inc(S("cnT"), 1)
                    if t >= 2:
                        act.wait_ge(S("t_qk"), at("t_qk", l, t - 1))
                    for j in range(2):
                        act.wait_ge(S("up_ps"), at("up_ps", l, up_items(l, t) + j + 1))
                        kv = bank(6 + j).rearrange("p (h e) -> p h e", h=4)
                        act_f(raw[t % 2][:, 0, 4 * j:4 * j + 4, 0:NOPE], kv[:, :, 0:NOPE], ACT.Copy)
                        act_f(vb[:, t, j * 256:(j + 1) * 256].rearrange("p (h e) -> p h e", h=4), kv[:, :, NOPE:P], ACT.Copy)\
                            .then_inc(S("up_sb"), 1)
                    if full:
                        for j in range(2):
                            act.wait_ge(S("up_ps"), at("up_ps", l, up_items(l, t) + j + 3))
                            act_f(raw[t % 2][:, 1, 4 * j:4 * j + 4, :],
                                  bank(6 if j else t)[:, 0:384].rearrange("p (h e) -> p h e", h=4), ACT.Copy).then_inc(S("up_sb"), 1)
                    n = (2 if full else 1) * H * QK
                    act.wait_ge(S("up_sb"), at("up_sb", l, up_items(l, t + 1)))
                    act.wait_ge(S("cn"), at("cn", l, t + 1))
                    if t >= 2:
                        act.wait_ge(S("t_ss"), at("t_ss", l, t - 1))
                    act_f(sqb[t % 2][:, 0:n], raw[t % 2].rearrange("p s h e -> p (s h e)")[:, 0:n], ACT.Square)\
                        .then_inc(S("t_sqd"), 1)

                def head_roots(t):
                    n = 2 * H if t < NT else H
                    act.wait_ge(S("t_ss"), at("t_ss", l, t + 1))
                    act_f(rsq[t % 2][:, 0:n], ssq[t % 2][:, 0:n], ACT.Sqrt).then_inc(S("t_hrt"), 1)

                if l > 0:
                    act.wait_ge(S("x_spilled"), 16 * AT)
                act.wait_ge(S("h_tr"), at("h_tr", l, AT))
                act.wait_ge(S("tproj"), at("tproj", l, 1))
                for t in range(AT):
                    if t < NT:
                        act_f(sqj[t][:, P:384], bank(t)[:, Q_OFF:CONV_OFF], ACT.Square, scale=Q_LORA ** -0.5,
                              accum_out=st[:, AT + t:AT + t + 1])
                    last = act_f(sqj[t][:, 0:P], bank(t)[:, 0:KV_LORA], ACT.Square, scale=KV_LORA ** -0.5,
                                 accum_out=st[:, t:t + 1])
                last.then_inc(S("t_sq"), 1)
                act.wait_ge(S("t_eps"), at("t_eps", l, 1))
                act_f(srt[:, 0:AT + NT], rst[:, 0:AT + NT], ACT.Sqrt).then_inc(S("t_rt"), 1)
                for t in range(AT + 1):
                    if t < AT:
                        evacuate(t)
                    if t >= 1:
                        head_roots(t - 1)
                act.wait_ge(S("wT_tr"), at("wT_tr", l, 1))
                act_f(sguwT, bank(6).rearrange("p (g q) -> p g q", g=BC), ACT.Copy)
                act_f(cw[:, :], bank(7)[:, 0:16 + 2 * KD], ACT.Copy).then_inc(S("wT"), 1)

                def split(s):
                    if s >= CHUNKS:
                        return
                    r = FIRST + s
                    act.wait_ge(raw_full[r % RAWS], full_no[l, r])
                    if s >= 2:
                        act.wait_ge(S("prod"), done_no(l, s - 2))
                    act_f(parts(s, words(s))[0], raw_slab(r, words(s)), ACT.Copy).then_inc(S("w_hi"), 1)

                def branch_hi(q, c, src):
                    act_f(brH[:, c, 0:W(l)], src[:, 0:W(l)], ACT.Copy).then_inc(S("br_hi"), 1)

                def conv_hi(c):
                    for a, b, o in [(0, SEQ, CVL)] + ([(SEQ, TOK, CVC)] if W(l) > SEQ else []):
                        last = act_f(brH[:, c, a:b], cvy[c % 2][:, o:o + b - a], ACT.Copy)
                    last.then_inc(S("br_hi"), 1)

                def gated(q, s0):
                    for d in range(KD):
                        u = q * KD + d
                        act.wait_ge(S("g_ps"), at("g_ps", l, u + 1))
                        if u >= 2:
                            act.wait_ge(S("g_prod"), at("g_prod", l, u - 1))
                        act_f(sig[u % 2][:, 0:W(l)], psb(u % 2)[:, 0:W(l)], ACT.Sigmoid).then_inc(S("g_sig"), 1)
                        split(s0 + d + 2)
                        if q == 3 and d:
                            merged_hi(d - 1)

                def merged_hi(d):
                    act.wait_ge(S("g_prod"), at("g_prod", l, 3 * KD + d + 1))
                    act_f(mH[:, d, 0:W(l)], merged[:, d, 0:W(l)], ACT.Copy).then_inc(S("m_hi"), 1)

                split(0)
                split(1)
                steps = [(h, t) for h in range(H) for t in range(NT)]
                rounds = (AT + NT + 3) // 4

                def head_T(h, r):
                    act.wait_ge(S("qk_tr"), at("qk_tr", l, h * rounds + r + 1))
                    if h >= 2 and r == 0:
                        act.wait_ge(S("s_ps"), at("s_ps", l, (h - 1) * NT))
                    n = min(4, AT + NT - 4 * r) * P
                    act_f(qkT[h % 2][0:QK, r * 512:r * 512 + n], psb(3)[0:QK, 512:512 + n], ACT.Copy).then_inc(S("qkT"), 1)

                for r in range(rounds):
                    head_T(0, r)
                for n in range(len(steps) + 1):
                    if n < len(steps):
                        h, t = steps[n]
                        lo = 0 if t < LT else SEQ
                        act.wait_ge(S("negmax"), at("negmax", l, n + 1))
                        if n >= 2:
                            act.wait_ge(S("pr_tr"), at("pr_tr", l, n - 1))
                        act_f(probs[n % 2][:, lo:TOK], psb(n % 2)[:, lo:TOK], ACT.Exp, bias=negm[:, n:n + 1],
                              accum_out=rsum[:, n:n + 1]).then_inc(S("probs"), 1)
                        if h + 1 < H and t < rounds:
                            head_T(h + 1, t)
                    if n >= 1 and steps[n - 1][1] < LT:
                        m = n - 1
                        act.wait_ge(S("pr_tr"), at("pr_tr", l, m + 1))
                        if m >= 2:
                            act.wait_ge(S("o_ps"), at("o_ps", l, m - 1))
                        act_f(prT[m % 2][:, 0:SEQ], psb(2)[:, 0:SEQ], ACT.Copy).then_inc(S("prT_a"), 1)
                for c in range(BC):
                    act.wait_ge(S("o_tr"), at("o_tr", l, c + 1))
                    branch_hi(0, c, psb(c % 2))
                gated(0, G_AT)
                for j in range(4):
                    split(S_V + j + 2)
                act.wait_ge(S("prod"), done_no(l, S_V + 3))
                for t in range(NT):
                    link(act_f(sgv[:, t, :], bank(t), ACT.Gelu_apprx_tanh))
                    act_f(bank(t), sgv[:, t, :], ACT.Square, scale=BW ** -0.5, accum_out=st[:, t:t + 1]).then_inc(S("sv_sq"), 1)
                act.wait_ge(S("sv_eps"), at("sv_eps", l, 1))
                act_f(srt[:, 0:NT], rst[:, 0:NT], ACT.Sqrt).then_inc(S("sv_rt"), 1)
                for g in range(BC):
                    act.wait_ge(S("prod"), done_no(l, S_U + g))
                    act_f(uT[g][:, 0:W(l)], psb((3, 0, 1, 2)[g])[:, 0:W(l)], ACT.Gelu_apprx_tanh).then_inc(S("sgu_u"), 1)
                    split(S_U + g + 2)
                for g in range(BC):
                    act.wait_ge(S("sgu_sum"), at("sgu_sum", l, g + 1))
                    branch_hi(1, g, umix[g % 2])
                gated(1, G_SG)
                for c in range(BC):
                    for j in range(2):
                        w = 3 * c + j
                        act.wait_ge(S("prod"), done_no(l, S_CV + w))
                        if c >= 2:
                            act.wait_ge(S("cv_y"), at("cv_y", l, c - 1))
                        act_f((gcs, gbs)[j][c % 2][:, 0:W(l)], psb(w % 4)[:, 0:W(l)], ACT.Copy).then_inc(S("cv_evac"), 1)
                        split(S_CV + w + 2)
                    if c:
                        act.wait_ge(S("cv_y"), at("cv_y", l, c))
                        conv_hi(c - 1)
                    split(S_CV + 3 * c + 4)
                act.wait_ge(S("cv_y"), at("cv_y", l, BC))
                conv_hi(BC - 1)
                gated(2, G_CV)
                act.wait_ge(S("po_pad"), at("po_pad", l, 1))
                for g in range(BC + 1):
                    if g < BC:
                        act.wait_ge(S("prod"), done_no(l, S_PO + g))
                        if g >= 2:
                            act.wait_ge(S("po_pl"), at("po_pl", l, g - 1))
                        last = act_f(pp[g % 2][:, PLL:PLL + SEQ], psb(g % 2)[:, 0:SEQ], ACT.Copy)
                        if W(l) > SEQ:
                            last = act_f(pp[g % 2][:, PLC:PLC + CTX], psb(g % 2)[:, SEQ:TOK], ACT.Copy)
                        last.then_inc(S("po_pp"), 1)
                        split(S_PO + g + 2)
                    if g >= 1:
                        h = g - 1
                        act.wait_ge(S("po_mix"), at("po_mix", l, h + 1))
                        act_f(brH[:, h, 0:W(l)], psb(2 + h % 2)[:, 0:W(l)], ACT.Copy, scale=cw[:, 12 + h:13 + h])\
                            .then_inc(S("br_hi"), 1)
                act.wait_ge(S("po_mix"), at("po_mix", l, BC))
                for t in range(NT):
                    if l == 0:
                        src = A["x"][0, t * P:(t + 1) * P, :] if t < LT else A["ctx"][0, (t - LT) * P:(t - LT + 1) * P, :]
                    else:
                        src = x_spill[t * P:(t + 1) * P, :]
                    act.dma_start(x_t[:, t, :], src).then_inc(S("x_back"), 16)
                gated(3, G_PO)
                merged_hi(KD - 1)
                for n in range(KD):
                    act.wait_ge(S("prod"), done_no(l, S_WO + n))
                    if n >= 2:
                        act.wait_ge(S("w_tr"), at("w_tr", l, n - 1))
                    g = 16 + n
                    last = act_f(wsc[n % 2][:, 0:SEQ], psb(n % 2)[:, 0:SEQ], ACT.Copy, scale=cw[:, g:g + 1])
                    if W(l) > SEQ:
                        last = act_f(wsc[n % 2][:, SEQ:TOK], psb(n % 2)[:, SEQ:TOK], ACT.Copy, scale=cw[:, g + KD:g + KD + 1])
                    last.then_inc(S("w_sc"), 1)
                    split(S_WO + n + 2)
                act.wait_ge(S("w_x"), at("w_x", l, KD))
                for t in range(NT):
                    if t:
                        act.wait_ge(S("n2_sq"), at("n2_sq", l, t))
                    act_f(junk, x_t[:, t, :], ACT.Square, scale=D ** -0.5, accum_out=st[:, t:t + 1]).then_inc(S("n2_sq"), 1)
                act.wait_ge(S("n2_eps"), at("n2_eps", l, 1))
                act_f(srt[:, 0:NT], rst[:, 0:NT], ACT.Sqrt).then_inc(S("n2_rt"), 1)
                for t in range(NT):
                    act.wait_ge(S("h2_tok"), at("h2_tok", l, t + 1))
                    act.dma_start(h2_rows[t * P:(t + 1) * P, :], h2tok[t % 2]).then_inc(S(f"h2_st{t % 2}"), 16)
                    act.wait_ge(S("h2_tr"), at("h2_tr", l, t + 1))
                    if t >= 2:
                        act.wait_ge(S("lg_ps"), at("lg_ps", l, t - 1))
                    act_f(h2T[t % 2], psb(t % 2).rearrange("p (k t) -> p k t", k=KD), ACT.Copy).then_inc(S("h2T"), 1)
                act.wait_ge(S("lg_ps"), at("lg_ps", l, NT))
                act_f(r_s[:, 0:NT, :], psb(3)[:, 0:NT * NE].rearrange("p (t e) -> p t e", t=NT), ACT.Sigmoid)\
                    .then_inc(S("r_s"), 1)

                nb = expert_blocks(W(l))

                def silu(b, j, first=False):
                    act.wait_ge(S("h_ps"), at("h_ps", l, b + 1))
                    if not first:
                        act.wait_ge(S("a_sb"), at("a_sb", l, b - 1))
                    act_f(sil[j], psb(1)[:, 0:FF], ACT.Silu).then_inc(S("sil"), 1)

                def rows_T(b, j):
                    act.wait_ge(S("xT_ps"), at("xT_ps", l, b + 1))
                    act_f(xgT[j], psb(0).rearrange("p (k t) -> p k t", k=KD), ACT.Copy).then_inc(S("xgT"), 1)

                def hidden_T(b, j):
                    act.wait_ge(S("aT_ps"), at("aT_ps", l, b + 1))
                    act_f(act_T[j], psb(1)[:, 512:768].rearrange("p (k t) -> p k t", k=2), ACT.Copy).then_inc(S("aT_sb"), 1)

                def store(b, j, dyn=False):
                    act.wait_ge(S("y_sb"), at("y_sb", l, b + 1))
                    dst = y_rows[l][bass.ds(b * P, P), :] if dyn else y_rows[l][b * P:(b + 1) * P, :]
                    act.dma_start(dst, ysb[j]).then_inc(S(f"y_st{j}"), 16)

                rows_T(0, 0)
                for b in range(3):
                    silu(b, b % 2, b < 2)
                    rows_T(b + 1, (b + 1) % 2)
                    hidden_T(b, b % 2)
                    if b >= 2:
                        store(b - 2, b % 2)
                with act.Fori(0, (nb - 3) // 2) as i:
                    for j in range(2):
                        par = (3 + j) % 2
                        b = i * 2 + (3 + j)
                        silu(b, par)
                        rows_T(b + 1, 1 - par)
                        hidden_T(b, par)
                        store(b - 2, par, True)
                for b in (nb - 2, nb - 1):
                    store(b, b % 2)
                if l == DEPTH - 1:
                    for t in range(LT):
                        act.wait_ge(S("x_new"), at("x_new", l, t + 1))
                        act.dma_start(out[0, t * P:(t + 1) * P, :], x_t[:, t, :]).then_inc(S("x_stored"), 16)
                else:
                    for t in range(AT):
                        act.wait_ge(S("x_new"), at("x_new", l, t + 1))
                        act.dma_start(x_spill[t * P:(t + 1) * P, :], x_t[:, t, :]).then_inc(S("x_spilled"), 16)

        @block.vector
        def _(dve):
            chain = [0]

            def link(ins):
                chain[0] += 1
                ins.then_inc(S("dve_chain"), 1)
                dve.wait_ge(S("dve_chain"), chain[0])

            tt, ts, stt, cp = dve.tensor_tensor, dve.tensor_scalar, dve.scalar_tensor_tensor, dve.tensor_copy

            dve.wait_ge(S("mod_b"), 16 * 2 * DEPTH)
            for l in range(DEPTH):
                rows = mod_sb[l]
                with dve.Fori(0, MC // (2 * SLOTS)) as i:
                    for j in range(SLOTS):
                        dve.wait_ge(S("mod_ps"), i * SLOTS + (l * MC // 2 + j + 1))
                        o = rows[:, bass.ds(i * (256 * SLOTS) + j * 256, 256)]
                        tt(o, o, psb(j // 2)[0:2, (j % 2) * 512:(j % 2) * 512 + 256], ALU.add).then_inc(S("mod_row"), 1)

            for l in range(DEPTH):
                NT = tiles(l)
                dve.wait_ge(S("par_n1"), at("par_n1", l, 16 * 3))
                for v in range(2):
                    last = stt(scale1(v), scale1(v), 1.0, gain1, ALU.add, ALU.mult)
                dve.wait_ge(S("n1_sq"), at("n1_sq", l, AT))
                ts(rst[:, 0:AT], st[:, 0:AT], EPS, None, ALU.add).then_inc(S("n1_eps"), 1)
                dve.wait_ge(S("n1_rt"), at("n1_rt", l, 1))
                link(dve.reciprocal(rst[:, 0:AT], srt[:, 0:AT]))

                def h_lo(t):
                    tok = slice(t * P, (t + 1) * P)
                    dve.wait_ge(S("hT_hi"), at("hT_hi", l, t + 1))
                    tt(hL[:, :, tok], psb(t % 2).rearrange("p (k t) -> p k t", k=KD), hH[:, :, tok].bitcast(F32), ALU.subtract)\
                        .then_inc(S("hT_tile"), 1)

                for t in range(AT):
                    v = 0 if t < LT else 1
                    if t >= 2:
                        dve.wait_ge(S("h_tr"), at("h_tr", l, t - 1))
                    link(stt(htok[t % 2], x_t[:, t, :], rst[:, t:t + 1], scale1(v), ALU.mult, ALU.mult))
                    tt(htok[t % 2], htok[t % 2], shift1(v), ALU.add).then_inc(S("h_tok"), 1)
                    if t < len(KVQ_SPLIT):
                        kn, k0 = KVQ_SPLIT[t], sum(KVQ_SPLIT[:t])
                        dve.wait_ge(S("w_hi"), at("w_hi", l, t + 1))
                        tt(kvqL[:, k0:k0 + kn, :], raw_slab(t, kn * KVQ).rearrange("p (k n) -> p k n", k=kn),
                           kvqH[:, k0:k0 + kn, :].bitcast(F32), ALU.subtract).then_inc(S("w_lo"), 1)
                    if t:
                        h_lo(t - 1)
                h_lo(AT - 1)

                def small_norms(t):
                    full = t < NT
                    b = bank(t)
                    if t >= 2:
                        dve.wait_ge(S("t_qk"), at("t_qk", l, t - 1))
                        dve.wait_ge(S("cn_tr"), at("cn_tr", l, t - 1))
                    cp(raw[t % 2][:, 0, :, NOPE:QK], b[:, None, KR_OFF:Q_OFF].to_broadcast([P, H, ROPE]))
                    last = stt(cn[t % 2][:, 0:P], b[:, 0:KV_LORA], rst[:, t:t + 1], g_kva, ALU.mult, ALU.mult)
                    if full:
                        last = stt(cn[t % 2][:, P:384], b[:, Q_OFF:CONV_OFF], rst[:, AT + t:AT + t + 1], g_qa, ALU.mult, ALU.mult)
                    last.then_inc(S("cn"), 1)

                def head_squares(t):
                    n = 2 * H if t < NT else H
                    dve.wait_ge(S("t_sqd"), at("t_sqd", l, t + 1))
                    link(dve.tensor_reduce(ssq[t % 2][:, 0:n], sqb[t % 2][:, 0:n * QK].rearrange("p (h e) -> p h e", e=QK),
                                           AX.X, ALU.add))
                    ts(ssq[t % 2][:, 0:n], ssq[t % 2][:, 0:n], 1.0 / QK, EPS, ALU.mult, ALU.add).then_inc(S("t_ss"), 1)

                def head_norms(t):
                    n = 2 * H if t < NT else H
                    dve.wait_ge(S("t_hrt"), at("t_hrt", l, t + 1))
                    link(dve.reciprocal(rsq[t % 2][:, 0:n], rsq[t % 2][:, 0:n]))
                    r = raw[t % 2].rearrange("p s h e -> p (s h) e")[:, 0:n, :]
                    link(tt(r, r, rsq[t % 2][:, 0:n, None].to_broadcast([P, n, QK]), ALU.mult))
                    for s in range(n // H):
                        last = tt(qk[:, t, s], raw[t % 2][:, s], g_qk[:, s:s + 1, :].to_broadcast([P, H, QK]), ALU.mult)
                    last.then_inc(S("t_gain"), 1)

                if l > 0:
                    dve.wait_ge(S("x_spilled"), 16 * AT)
                dve.wait_ge(S("par_b"), at("par_b", l, 16 * 8))
                dve.wait_ge(S("g_scaled"), at("g_scaled", l, 1))
                dve.wait_ge(S("h_tr"), at("h_tr", l, AT))
                dve.wait_ge(S("t_sq"), at("t_sq", l, 1))
                ts(rst[:, 0:AT + NT], st[:, 0:AT + NT], EPS, None, ALU.add).then_inc(S("t_eps"), 1)
                dve.wait_ge(S("t_rt"), at("t_rt", l, 1))
                link(dve.reciprocal(rst[:, 0:AT + NT], srt[:, 0:AT + NT]))
                for t in range(AT + 2):
                    if t >= 2:
                        head_norms(t - 2)
                    if t < AT:
                        small_norms(t)
                    if 1 <= t <= AT:
                        head_squares(t - 1)

                def split(s):
                    if s >= CHUNKS:
                        return
                    hi, lo = parts(s, words(s))
                    dve.wait_ge(S("w_hi"), split_no(l, s))
                    tt(lo, raw_slab(FIRST + s, words(s)), hi.bitcast(F32), ALU.subtract).then_inc(S("w_lo"), 1)

                def branch_lo(q, c, src):
                    dve.wait_ge(S("br_hi"), at("br_hi", l, q * BC + c + 1))
                    tt(brL[:, c, 0:W(l)], src[:, 0:W(l)], brH[:, c, 0:W(l)].bitcast(F32), ALU.subtract).then_inc(S("br_lo"), 1)

                def gated(q, s0):
                    for d in range(KD):
                        u = q * KD + d
                        dve.wait_ge(S("prod"), done_no(l, s0 + d))
                        dve.wait_ge(S("g_sig"), at("g_sig", l, u + 1))
                        o = merged[:, d, 0:W(l)]
                        if q == 0:
                            tt(o, sig[u % 2][:, 0:W(l)], psb(2 + u % 2)[:, 0:W(l)], ALU.mult).then_inc(S("g_prod"), 1)
                        else:
                            dve.wait_ge(S("g_prod"), at("g_prod", l, u))
                            link(tt(prod[:, 0:W(l)], sig[u % 2][:, 0:W(l)], psb(2 + u % 2)[:, 0:W(l)], ALU.mult))
                            tt(o, o, prod[:, 0:W(l)], ALU.add).then_inc(S("g_prod"), 1)
                        split(s0 + d + 2)
                        if q == 3 and d:
                            merged_lo(d - 1)

                def merged_lo(d):
                    dve.wait_ge(S("m_hi"), at("m_hi", l, d + 1))
                    tt(mL[:, d, 0:W(l)], merged[:, d, 0:W(l)], mH[:, d, 0:W(l)].bitcast(F32), ALU.subtract).then_inc(S("m_lo"), 1)

                split(0)
                split(1)
                steps = [(h, t) for h in range(H) for t in range(NT)]
                for n in range(len(steps) + 2):
                    if n < len(steps):
                        h, t = steps[n]
                        lo = 0 if t < LT else SEQ
                        dve.wait_ge(S("s_ps"), at("s_ps", l, n + 1))
                        dve.tensor_reduce(negm[:, n:n + 1], psb(n % 2)[:, lo:TOK], AX.X, ALU.max, negate=True)\
                            .then_inc(S("negmax"), 1)
                    if 1 <= n <= len(steps):
                        m = n - 1
                        h, t = steps[m]
                        dve.wait_ge(S("pr_tr"), at("pr_tr", l, m + 1))
                        if m >= 2:
                            dve.wait_ge(S("o_ps"), at("o_ps", l, m - 1))
                        cp(prT[m % 2][:, SEQ:TOK], psb(2)[:, SEQ:TOK]).then_inc(S("prT_d"), 1)
                    if n >= 2:
                        m = n - 2
                        h, t = steps[m]
                        dve.wait_ge(S("o_ps"), at("o_ps", l, m + 1))
                        link(dve.reciprocal(rinv[:, m:m + 1], rsum[:, m:m + 1]))
                        ts(obuf[:, t, h * VD:(h + 1) * VD], psb(3)[:, (m % 2) * VD:(m % 2 + 1) * VD], rinv[:, m:m + 1], None,
                           ALU.mult).then_inc(S("o_sb"), 1)
                for c in range(BC):
                    branch_lo(0, c, psb(c % 2))
                gated(0, G_AT)

                for j in range(4):
                    split(S_V + j + 2)
                dve.wait_ge(S("sv_sq"), at("sv_sq", l, NT))
                ts(rst[:, 0:NT], st[:, 0:NT], EPS, None, ALU.add).then_inc(S("sv_eps"), 1)
                dve.wait_ge(S("sv_rt"), at("sv_rt", l, 1))
                link(dve.reciprocal(rst[:, 0:NT], srt[:, 0:NT]))
                for t in range(NT):
                    stt(sgv[:, t, :], sgv[:, t, :], rst[:, t:t + 1], g_sgu, ALU.mult, ALU.mult).then_inc(S("sgv"), 1)
                for g in range(BC):
                    split(S_U + g + 2)
                dve.wait_ge(S("par_sb"), at("par_sb", l, 16))
                for g in range(BC + 1):
                    if g < BC:
                        dve.wait_ge(S("sgu_mix"), at("sgu_mix", l, g + 1))
                        m3 = psb((3, 0, 1, 2)[g])[:, 0:W(l)].rearrange("p (t q) -> p t q", q=P)
                        um = umix[g % 2][:, 0:W(l)]
                        if g >= 2:
                            dve.wait_ge(S("br_lo"), at("br_lo", l, BC + g - 1))
                        link(tt(um.rearrange("p (t q) -> p t q", q=P), m3,
                                sgub[:, None, g * P:(g + 1) * P].to_broadcast([P, NT, P]), ALU.add))
                        tt(um, um, uT[g][:, 0:W(l)], ALU.mult).then_inc(S("sgu_sum"), 1)
                    if g >= 1:
                        branch_lo(1, g - 1, umix[(g - 1) % 2])
                gated(1, G_SG)

                dve.memset(cup[0], 0.0)
                link(dve.memset(cup[1], 0.0))
                cstreams = [(0, SEQ, CVL)] + ([(SEQ, TOK, CVC)] if W(l) > SEQ else [])
                hi_ = CVC + CTX if W(l) > SEQ else CVL + SEQ

                def conv_lo(c):
                    dve.wait_ge(S("br_hi"), at("br_hi", l, 2 * BC + c + 1))
                    for a, b, o in cstreams:
                        last = tt(brL[:, c, a:b], cvy[c % 2][:, o:o + b - a], brH[:, c, a:b].bitcast(F32), ALU.subtract)
                    last.then_inc(S("br_lo"), 1)

                for c in range(BC):
                    w = 3 * c + 2
                    split(S_CV + 3 * c + 2)
                    split(S_CV + 3 * c + 3)
                    if c:
                        conv_lo(c - 1)
                    dve.wait_ge(S("prod"), done_no(l, S_CV + w))
                    dve.wait_ge(S("cv_evac"), at("cv_evac", l, 2 * c + 2))
                    cu = cup[c % 2]
                    for a, b, o in cstreams:
                        last = tt(cu[:, o:o + b - a], gcs[c % 2][:, a:b], psb(w % 4)[:, a:b], ALU.mult)
                    last.then_inc(S("cv_cu"), 1)
                    split(S_CV + 3 * c + 4)
                    dve.wait_ge(S("cv_cu"), at("cv_cu", l, c + 1))
                    if c >= 2:
                        dve.wait_ge(S("br_lo"), at("br_lo", l, 2 * BC + c - 1))
                    y = cvy[c % 2][:, 1:hi_]
                    link(ts(y, cu[:, 1:hi_], cw[:, 4 + c:5 + c], None, ALU.mult))
                    link(stt(y, cu[:, 0:hi_ - 1], cw[:, c:c + 1], y, ALU.mult, ALU.add))
                    link(stt(y, cu[:, 2:hi_ + 1], cw[:, 8 + c:9 + c], y, ALU.mult, ALU.add))
                    for a, b, o in cstreams:
                        z = cvy[c % 2][:, o:o + b - a]
                        last = tt(z, z, gbs[c % 2][:, a:b], ALU.mult)
                    last.then_inc(S("cv_y"), 1)
                conv_lo(BC - 1)
                gated(2, G_CV)

                dve.wait_ge(S("const_dma"), 48)
                for j in range(2):
                    last = dve.memset(pp[j], 0.0)
                last.then_inc(S("po_pad"), 1)
                pstreams = [(0, SEQ, PLL)] + ([(SEQ, TOK, PLC)] if W(l) > SEQ else [])

                def pool_lo(h):
                    dve.wait_ge(S("br_hi"), at("br_hi", l, 3 * BC + h + 1))
                    stt(brL[:, h, 0:W(l)], psb(2 + h % 2)[:, 0:W(l)], cw[:, 12 + h:13 + h], brH[:, h, 0:W(l)].bitcast(F32),
                        ALU.mult, ALU.subtract).then_inc(S("br_lo"), 1)

                for g, win_ in enumerate(WINDOWS):
                    split(S_PO + g + 2)
                    dve.wait_ge(S("po_pp"), at("po_pp", l, g + 1))
                    if g:
                        dve.wait_ge(S("po_pl"), at("po_pl", l, g))
                    src, lo, k = pp[g % 2], 1, 1
                    link(tt(pacc[0][:, 1:PLW], src[:, 0:PLW - 1], src[:, 1:PLW], ALU.add))
                    cur, lo, hi = 0, 1, PLW
                    while 2 * k < win_:
                        link(tt(pacc[1 - cur][:, lo + k:hi - k], pacc[cur][:, lo:hi - 2 * k], pacc[cur][:, lo + 2 * k:hi], ALU.add))
                        cur, lo, hi, k = 1 - cur, lo + k, hi - k, 2 * k
                    s_ = pacc[cur]
                    e = edge[:, g * 2 * PP:(g + 1) * 2 * PP]
                    for a, b, o in pstreams:
                        n = b - a
                        tt(s_[:, o:o + PP], s_[:, o:o + PP], e[:, 0:PP], ALU.mult)
                        last = tt(s_[:, o + n - PP:o + n], s_[:, o + n - PP:o + n], e[:, PP:2 * PP], ALU.mult)
                    link(last)
                    if g >= 2:
                        dve.wait_ge(S("po_mix"), at("po_mix", l, g - 1))
                    for a, b, o in pstreams:
                        last = stt(pooled[g % 2][:, a:b], s_[:, o:o + b - a], 1.0 / win_, src[:, o:o + b - a], ALU.mult, ALU.subtract)
                    last.then_inc(S("po_pl"), 1)
                    if g:
                        pool_lo(g - 1)
                pool_lo(BC - 1)
                gated(3, G_PO)
                merged_lo(KD - 1)

                dve.wait_ge(S("x_back"), at("x_back", l, 16 * NT))
                for n in range(KD):
                    split(S_WO + n + 2)
                    dve.wait_ge(S("w_tr"), at("w_tr", l, n + 1))
                    xs = x_t[:, 0:NT, n * P:(n + 1) * P]
                    tt(xs, xs, psb(2 + n % 2)[:, 0:W(l)].rearrange("p (t c) -> p t c", c=P), ALU.add).then_inc(S("w_x"), 1)
                dve.wait_ge(S("par_n2"), at("par_n2", l, 16 * 3))
                for v in range(2):
                    last = stt(mrow[:, v, 1, :], mrow[:, v, 1, :], 1.0, gain2, ALU.add, ALU.mult)
                dve.wait_ge(S("n2_sq"), at("n2_sq", l, NT))
                ts(rst[:, 0:NT], st[:, 0:NT], EPS, None, ALU.add).then_inc(S("n2_eps"), 1)
                dve.wait_ge(S("n2_rt"), at("n2_rt", l, 1))
                link(dve.reciprocal(rst[:, 0:NT], srt[:, 0:NT]))
                for t in range(NT):
                    v = 0 if t < LT else 1
                    if t >= 2:
                        dve.wait_ge(S("h2_tr"), at("h2_tr", l, t - 1))
                        dve.wait_ge(S(f"h2_st{t % 2}"), at(f"h2_st{t % 2}", l, 16 * (t // 2)))
                    link(stt(h2tok[t % 2], x_t[:, t, :], rst[:, t:t + 1], mrow[:, v, 1, :], ALU.mult, ALU.mult))
                    tt(h2tok[t % 2], h2tok[t % 2], mrow[:, v, 0, :], ALU.add).then_inc(S("h2_tok"), 1)

                s, sbv, m_, sc = (a[:, 0:NT, :] for a in (r_s, r_sb, r_m, r_sc))
                oh = [a[:, 0:NT, :] for a in r_oh]

                def bc(a, n):
                    return a[:, :, None].to_broadcast([P, a.shape[1], n])

                dve.wait_ge(S("r_s"), at("r_s", l, 1))
                dve.wait_ge(S("const"), 8)
                link(tt(sbv, s, rbias[:, None, :].to_broadcast([P, NT, NE]), ALU.add))
                g3 = sbv.rearrange("p t (g e) -> p (t g) e", g=NG)
                pr = r_pair[:, 0:NT * NG, :]
                tt(pr[:, :, 0:3], g3[:, :, 0:3], g3[:, :, 1:4], ALU.add)
                tt(pr[:, :, 3:5], g3[:, :, 0:2], g3[:, :, 2:4], ALU.add)
                link(tt(pr[:, :, 5:6], g3[:, :, 0:1], g3[:, :, 3:4], ALU.add))
                gs, gq, gm = (a[:, 0:NT, :] for a in (r_gs, r_gq, r_gm))
                mx = r_mx[:, 0:NT]
                link(dve.tensor_reduce(gs.rearrange("p t g -> p (t g)"), pr, AX.X, ALU.max))

                def first_max(dst, src, weights, tmp, n):
                    link(dve.tensor_reduce(mx, src, AX.X, ALU.max))
                    link(tt(tmp, src, bc(mx, n), ALU.is_ge))
                    link(tt(tmp, tmp, weights[:, None, :].to_broadcast([P, NT, n]), ALU.mult))
                    link(dve.tensor_reduce(mx, tmp, AX.X, ALU.max))
                    link(tt(dst, tmp, bc(mx, n), ALU.is_equal))

                first_max(gm, gs, w4, gq, NG)
                link(ts(gq, gm, BIG, -BIG, ALU.mult, ALU.add))
                m3 = m_.rearrange("p t (g e) -> p (t g) e", g=NG)
                link(tt(m3, g3, bc(gm.rearrange("p t g -> p (t g)"), EG), ALU.mult))
                link(tt(m3, m3, bc(gq.rearrange("p t g -> p (t g)"), EG), ALU.add))
                first_max(oh[0], m_, w16, sc, NE)
                link(stt(m_, oh[0], -3.0e38, m_, ALU.mult, ALU.add))
                first_max(oh[1], m_, w16, sc, NE)
                cp(r_den[:, 0:1], oh[1][:, 0, 0:1]).then_inc(S("r_oh"), 1)
                for k in range(2):
                    link(tt(sc, oh[k], s, ALU.mult))
                    link(dve.tensor_reduce(gw[k][:, 0:NT], sc, AX.X, ALU.add))
                link(tt(r_den[:, 0:NT], gw[0][:, 0:NT], gw[1][:, 0:NT], ALU.add))
                link(dve.reciprocal(r_den[:, 0:NT], r_den[:, 0:NT]))
                for k in range(2):
                    tt(gw[k][:, 0:NT], gw[k][:, 0:NT], r_den[:, 0:NT], ALU.mult)
                nb = expert_blocks(W(l))
                dve.wait_ge(S("rank_ps"), at("rank_ps", l, 1))
                cnt = psb(2)[:, NT * NE:(NT + 1) * NE]
                link(tt(r_cnt, cnt[:, :, None].to_broadcast([P, NE, 6]), steps6[:, None, :].to_broadcast([P, NE, 6]), ALU.is_gt))
                link(dve.tensor_reduce(r_nb, r_cnt, AX.X, ALU.add))
                link(dve.tensor_tensor_scan(r_end, ones[:, 0:NE], r_nb, 0.0, ALU.mult, ALU.add))
                link(tt(r_base, r_end, r_nb, ALU.subtract))
                link(ts(r_base, r_base, float(P), None, ALU.mult))
                link(tt(m_, psb(2)[:, 0:NT * NE].rearrange("p (t e) -> p t e", t=NT), r_base[:, None, :].to_broadcast([P, NT, NE]), ALU.add))
                for k in range(2):
                    link(tt(sc, m_, oh[k], ALU.mult))
                    link(dve.tensor_reduce(r_slot[:, k, 0:NT], sc, AX.X, ALU.add))
                cp(slot_i[:, :], r_slot.rearrange("p k t -> p (k t)")).then_inc(S("slots"), 1) if NT == AT else \
                    cp(slot_i[:, :].rearrange("p (k t) -> p k t", k=2)[:, :, 0:NT], r_slot[:, :, 0:NT]).then_inc(S("slots"), 1)
                blk = r_blk[:, 0:nb, :]
                link(tt(blk, r_end[:, None, :].to_broadcast([P, nb, NE]), blkno[:, 0:nb, None].to_broadcast([P, nb, NE]), ALU.is_le))
                link(dve.tensor_reduce(r_eid[:, 0:nb], blk, AX.X, ALU.add))
                link(ts(r_eid[:, 0:nb], r_eid[:, 0:nb], float(NE - 1), None, ALU.min))
                cp(eid_i[:, 0:nb], r_eid[:, 0:nb]).then_inc(S("eid"), 1)
                dve.wait_ge(S("tab_ps"), at("tab_ps", l, 1))
                cp(tab_i[:, :], psb(3)[:, 0:MAXB + 1]).then_inc(S("tab_i"), 1)

                def hidden(b, j, first=False):
                    dve.wait_ge(S("sil"), at("sil", l, b + 1))
                    if not first:
                        dve.wait_ge(S("aT_ps"), at("aT_ps", l, b - 1))
                    tt(act_a[j], sil[j], psb(1)[:, FF:2 * FF], ALU.mult).then_inc(S("a_sb"), 1)

                def rows_out(b, j, stored=None):
                    dve.wait_ge(S("y_ps"), at("y_ps", l, b + 1))
                    if stored is not None:
                        dve.wait_ge(S(f"y_st{j}"), at(f"y_st{j}", l, stored))
                    cp(ysb[j], psb(2 + j)).then_inc(S("y_sb"), 1)

                for b in range(3):
                    hidden(b, b % 2, b < 2)
                    if b:
                        rows_out(b - 1, (b - 1) % 2)
                with dve.Fori(0, (nb - 3) // 2) as i:
                    for j in range(2):
                        par = (3 + j) % 2
                        b = i * 2 + (3 + j)
                        hidden(b, par)
                        rows_out(b - 1, 1 - par, i * 16 + 16)
                rows_out(nb - 1, (nb - 1) % 2, 16 * ((nb - 1) // 2))

                for t in range(NT):
                    v = 0 if t < LT else 1
                    j = t % 2
                    dve.wait_ge(S(f"yg{j}"), at(f"yg{j}", l, 32 * (t // 2 + 1)))
                    if t:
                        dve.wait_ge(S("x_new"), at("x_new", l, t))
                    link(ts(ytmp, yg[j][0], gw[0][:, t:t + 1], None, ALU.mult))
                    link(stt(ytmp, yg[j][1], gw[1][:, t:t + 1], ytmp, ALU.mult, ALU.add))
                    ins = tt(ytmp, ytmp, mrow[:, v, 2, :], ALU.mult)
                    ins.then_inc(S("yg_free"), 1)
                    dve.wait_ge(S("yg_free"), at("yg_free", l, t + 1))
                    tt(x_t[:, t, :], x_t[:, t, :], ytmp, ALU.add).then_inc(S("x_new"), 1)

        @block.gpsimd
        def _(pool):
            chain = [0]

            def link(ins):
                chain[0] += 1
                ins.then_inc(S("pool_chain"), 1)
                pool.wait_ge(S("pool_chain"), chain[0])

            pool.dma_start(T[0:KD, P:2 * P], A["c"][0].rearrange("(k p) -> k p", p=P)).then_inc(S("c_rows"), 16)
            pool.dma_start(T[KD:2 * KD, P:2 * P], A["c_ctx"].rearrange("(k p) -> k p", p=P)).then_inc(S("c_rows"), 16)
            link(pool.memset(ident[:, :], 0.0))
            pool.affine_select(out=ident[:, :], in_=ident[:, :], compare_op=ALU.not_equal, fill=1.0, base=0,
                               pattern=[[-1, P]], channel_multiplier=1).then_inc(S("const"), 1)
            link(pool.memset(ones[:, :], 1.0))
            pool.affine_select(out=tri[:, :], in_=ones[:, :], compare_op=ALU.is_gt, fill=0.0, base=0,
                               pattern=[[1, P]], channel_multiplier=-1).then_inc(S("const"), 1)
            for l in range(DEPTH):
                for v in range(2):
                    pool.dma_start(mod_sb[l][v:v + 1, :], A["mod_b"][l].rearrange("(a n) -> a n", a=1)).then_inc(S("mod_b"), 16)
            pool.dma_start(rwv, A["router_w"].rearrange("(k p) e -> p k e", p=P)).then_inc(S("const_dma"), 16)
            pool.dma_start(rbias[:, :], A["router_b"].rearrange("(a e) -> a e", a=1).partition_broadcast(P)).then_inc(S("const_dma"), 16)
            pool.dma_start(edge[:, :], A["edges"].rearrange("g e -> (g e)").rearrange("(a n) -> a n", a=1).partition_broadcast(P))\
                .then_inc(S("const_dma"), 16)

            def counter(dst, at_, n, base, step, channel):
                link(pool.iota(iint[:, at_:at_ + n], [[step, n]], base=base, channel_multiplier=channel))
                pool.tensor_copy(dst, iint[:, at_:at_ + n]).then_inc(S("const"), 1)

            counter(w4[:, :], 0, NG, NG, -1, 0)
            counter(w16[:, :], 4, NE, NE, -1, 0)
            counter(steps6[:, :], 20, 6, 0, P, 0)
            counter(blkno[:, :], 26, MAXB, 0, 1, 0)
            counter(tokf[:, :], 56, AT, 0, P, 1)
            pool.memset(zrow[:, :], 0.0).then_inc(S("const"), 1)
            pool.wait_ge(S("const"), 8)
            for l in range(DEPTH):
                pool.dma_start(token_of[l].rearrange("(p b) o -> p (b o)", p=P), zrow[:, :]).then_inc(S("tab_zero"), 16)
            for l in range(DEPTH):
                pool.wait_ge(S("mod_row"), (l + 1) * MC // 2)
                pool.dma_start(mod_rows[l], mod_sb[l]).then_inc(S("mod_st"), 16)
            pool.wait_ge(S("mod_st"), 16 * DEPTH)

            def row(a):
                return a.rearrange("(a n) -> a n", a=1).partition_broadcast(P)

            def parameters(l):
                for v in range(2):
                    pool.dma_start(MGZ[:, v * 2 * D:(v + 1) * 2 * D], row(mod_rows[l, v, 0:2 * D])).then_inc(S("par_n1"), 16)
                pool.dma_start(gain1, row(A["norm1_g"][l])).then_inc(S("par_n1"), 16)
                pool.dma_start(g_qk[:, 0, :], row(A["k_norm_g"][l])).then_inc(S("par_g"), 16)
                pool.dma_start(g_qk[:, 1, :], row(A["q_norm_g"][l])).then_inc(S("par_g"), 16)
                for dst, src in ((g_kva, row(A["kv_a_norm_g"][l])), (g_qa, row(A["q_a_norm_g"][l])),
                                 (g_sgu, row(A["sgu_norm_g"][l])),
                                 (sguw, A["sgu_w"][l].rearrange("g p q -> p g q")),
                                 (crow[0:12, :], A["conv_w"][l].rearrange("k (c p) -> (k c) p", p=P)),
                                 (crow[12:16, :], A["pool_scale"][l].rearrange("(c p) -> c p", p=P)),
                                 (crow[16:24, :], mod_rows[l, 0, 2 * D:3 * D].rearrange("(c p) -> c p", p=P)),
                                 (crow[24:32, :], mod_rows[l, 1, 2 * D:3 * D].rearrange("(c p) -> c p", p=P))):
                    pool.dma_start(dst, src).then_inc(S("par_b"), 16)
                pool.dma_start(sgub, row(A["sgu_b"][l].rearrange("g q -> (g q)"))).then_inc(S("par_sb"), 16)
                pool.wait_ge(S("par_g"), at("par_g", l, 32))
                pool.tensor_scalar(g_qk[:, 1, :], g_qk[:, 1, :], SCALE, None, ALU.mult).then_inc(S("g_scaled"), 1)

            parameters(0)
            for l in range(DEPTH):
                NT = tiles(l)
                if l > 0:
                    pool.wait_ge(S("x_new"), at("x_new", l - 1, tiles(l - 1)))
                pool.dma_start(T[:, 1536:1792], A["rope"].rearrange("p s t e -> p (s t e)")).then_inc(S("par_r"), 16)
                pool.wait_ge(S("par_r"), 16 * (l + 1))

                def rotate(t):
                    pool.wait_ge(S("t_gain"), at("t_gain", l, t + 1))
                    if t >= LT:
                        pool.sem_inc(S("t_qk"), 1)
                        return
                    n = 2 * H
                    r = qk[:, t].rearrange("p s h e -> p (s h) e")[:, :, NOPE:QK]
                    t1 = sqb[t % 2][:, 0:n * ROPE].rearrange("p (h e) -> p h e", h=n)
                    t2 = sqb[t % 2][:, n * ROPE:2 * n * ROPE].rearrange("p (h e) -> p h e", h=n)
                    pool.tensor_tensor(t1, r, cosv[:, t:t + 1, :].to_broadcast([P, n, ROPE]), ALU.mult)
                    link(pool.tensor_tensor(t2, r, sinv[:, t:t + 1, :].to_broadcast([P, n, ROPE]), ALU.mult))
                    pool.tensor_tensor(r[:, :, 0:HALF], t1[:, :, 0:HALF], t2[:, :, HALF:ROPE], ALU.subtract)
                    pool.tensor_tensor(r[:, :, HALF:ROPE], t2[:, :, 0:HALF], t1[:, :, HALF:ROPE], ALU.add).then_inc(S("t_qk"), 1)

                for t in range(AT):
                    rotate(t)

                pool.wait_ge(S("o_tr"), at("o_tr", l, BC))
                pool.wait_ge(S("g_prod"), at("g_prod", l, 2 * KD))
                pool.dma_start(poolw, A["pool_w"][l].rearrange("g c d -> c g d")).then_inc(S("par_p"), 16)
                pool.wait_ge(S("prod"), done_no(l, S_WO - 1))
                for v in range(2):
                    pool.dma_start(HTF[:, v * 3 * D:(v + 1) * 3 * D], row(mod_rows[l, v, 3 * D:6 * D])).then_inc(S("par_n2"), 16)
                pool.dma_start(gain2, row(A["norm2_g"][l])).then_inc(S("par_n2"), 16)

                pool.wait_ge(S("tab_zero"), 16 * DEPTH)
                pool.wait_ge(S("slots"), at("slots", l, 1))
                for k in range(2):
                    for t in range(NT):
                        c = k * AT + t
                        pool.indirect_dma_start(out=token_of[l], out_offset=bass.IndirectOffsetOnAxis(slot_i[:, c:c + 1], 0),
                                                in_=tokf[:, t:t + 1], in_offset=None).then_inc(S("tab_st"), 16)
                pool.wait_ge(S("tab_st"), at("tab_st", l, 16 * 2 * NT))
                pool.dma_start(tabr, token_of[l].rearrange("(b p) o -> b (p o)", p=P)).then_inc(S("tab_ld"), 16)
                pool.wait_ge(S("tab_i"), at("tab_i", l, 1))
                for t in range(2):
                    pool.wait_ge(S(f"h2_st{t}"), at(f"h2_st{t}", l, 16 * ((NT + 1 - t) // 2)))
                pool.wait_ge(S("h2_tr"), at("h2_tr", l, NT))
                nb = expert_blocks(W(l))

                def gather(b, j, n, dyn=False):
                    src = tab_i[:, bass.ds(b, 1)] if dyn else tab_i[:, b:b + 1]
                    pool.tensor_copy(idx_i[j][:, :], src).then_inc(S("idx"), 1)
                    pool.wait_ge(S("idx"), at("idx", l, n + 1))
                    pool.sem_inc(S("idx_seen"), 1)
                    pool.indirect_dma_start(out=xg[j], out_offset=None, in_=h2_rows,
                                            in_offset=bass.IndirectOffsetOnAxis(idx_i[j][:, :], 0)).then_inc(S(f"xg{j}"), 16)

                gather(0, 0, 0)
                gather(1, 1, 1)
                with pool.Fori(0, (nb - 1) // 2) as i:
                    for j in range(2):
                        pool.wait_ge(S("xT_ps"), at("xT_ps", l, i * 2 + (1 + j)))
                        gather(i * 2 + (2 + j), j, i * 2 + (2 + j), True)
                if l + 1 < DEPTH:
                    parameters(l + 1)
                for j in range(2):
                    pool.wait_ge(S(f"y_st{j}"), at(f"y_st{j}", l, 16 * ((nb + 1 - j) // 2)))
                for t in range(NT):
                    j = t % 2
                    if t >= 2:
                        pool.wait_ge(S("yg_free"), at("yg_free", l, t - 1))
                    for k in range(2):
                        c = k * AT + t
                        pool.indirect_dma_start(out=yg[j][k], out_offset=None, in_=y_rows[l],
                                                in_offset=bass.IndirectOffsetOnAxis(slot_i[:, c:c + 1], 0)).then_inc(S(f"yg{j}"), 16)
        return len(sems)


_INS = ["x", "c", "ctx", "c_ctx", "mod_w", "mod_b", "norm1_g", "norm2_g", "w_in", "kv_a_norm_g", "w_ukv", "k_norm_g",
        "q_a_norm_g", "w_uq", "q_norm_g", "conv_w", "pool_w", "pool_scale", "sgu_norm_g", "sgu_w", "sgu_b",
        "w_branch", "w_o", "router_w", "router_b", "moe_w1", "moe_w3", "moe_w2"]


def kernel(**inputs):
    import concourse.bacc as bacc
    from concourse.bass_utils import run_bass_kernel_spmd

    nc = bacc.Bacc("TRN2", target_bir_lowering=False, num_devices=1)
    arrays, aps = {}, {}
    tables = {"rope": rope_tables(), "edges": pool_edges()}
    for name in _INS + list(tables):
        a = np.ascontiguousarray(tables[name] if name in tables else inputs[name])
        arrays[f"in_{name}"] = a
        aps[name] = nc.dram_tensor(f"in_{name}", a.shape, mybir.dt.from_np(a.dtype), kind="ExternalInput").ap()
    out = nc.dram_tensor("out", [1, SEQ, D], F32, kind="ExternalOutput").ap()
    trunk(nc, aps, out)
    r = run_bass_kernel_spmd(nc, [arrays], core_ids=[0])
    return r.results[0]["out"]
```

```python
from contextlib import ExitStack

import numpy as np
import concourse.bass as bass
from concourse import mybir

F32 = mybir.dt.float32
F32R = mybir.dt.float32r
I32 = mybir.dt.int32
ALU = mybir.AluOpType
ACT = mybir.ActivationFunctionType
AX = mybir.AxisListType

P = 128
D = 1024
KD = D // P
DEPTH = 2
SEQ = 512
CTX = 256
TOK = SEQ + CTX
LT = SEQ // P
AT = TOK // P
N_MOD = 6
MC = N_MOD * KD
EPS = 1e-6
GRID_W = 64

BW = 512
BC = BW // P
H = 8
NOPE, ROPE, VD = 64, 32, 64
QK = NOPE + ROPE
HALF = ROPE // 2
AXIS_PAIRS = ROPE // 4
KV_LORA, Q_LORA = 128, 256
SCALE = QK ** -0.5

KR_OFF = KV_LORA
Q_OFF = KR_OFF + ROPE
CONV_OFF = Q_OFF + Q_LORA
POOL_OFF = CONV_OFF + 3 * BW
SGU_OFF = POOL_OFF + BW
GATE_OFF = SGU_OFF + 2 * BW
WINDOWS = (2, 4, 8, 16)

NE, NG = 16, 4
EG = NE // NG
FF = 256
BIG = 1.0e30

SLOTS = 6
SLAB = 2048
RAWS, RAW = 3, (KD + BC) * P
KVQ = CONV_OFF
KVQ_SPLIT = (3, 3, 2)

G_AT, S_V, S_U = 0, KD, KD + 4
G_SG = S_U + BC
S_CV = G_SG + KD
G_CV = S_CV + 3 * BC
S_PO = G_CV + KD
G_PO = S_PO + BC
S_WO = G_PO + KD
CHUNKS = S_WO + KD
SPLITS = len(KVQ_SPLIT) + CHUNKS
MAXB = (2 * TOK + NE * (P - 1)) // P

CVL, CVC, CVW = 1, 1 + SEQ + 2, SEQ + CTX + 4
PP = 8
PLL, PLC, PLW = PP, PP + SEQ + 2 * PP, SEQ + CTX + 4 * PP


def expert_blocks(tokens):
    return (2 * tokens + NE * (P - 1)) // P


def signals(name):
    steps, blocks = H * AT, expert_blocks(TOK)
    rounds = H * ((2 * AT + 3) // 4)
    once = "eid g_scaled n2_eps n2_rt r_oh r_s rank_ps slots sv_eps sv_rt lg_sb lg_tr t_sq t_eps t_rt tab_i tab_oh tab_ps wT wT_tr"
    by_tile = ("cn cnT cn_tr h2T h2_tok h2_tr hT_hi hT_tile h_tok h_tr lg_ps n1_sq n2_sq sgv sv_sq t_gain t_hrt t_qk "
               "t_sqd t_ss x_new y_w0 yg_free n1_eps n1_rt")
    by_chunk = "cv_cu po_mix po_pl po_pp sgu_mix sgu_sum sgu_u"
    by_step = "negmax o_ps o_sb p_norm prT_d pr_tr probs s_ps"
    by_block = "aT_ps aT_sb a_sb h_ps sil y_ps y_sb"
    counts = {
        **dict.fromkeys(once.split(), 1), **dict.fromkeys(by_tile.split(), AT), **dict.fromkeys(by_chunk.split(), BC),
        **dict.fromkeys(by_step.split(), steps), "prT_a": H * LT, **dict.fromkeys(by_block.split(), blocks),
        **dict.fromkeys(("g_prod", "g_ps", "g_sig"), 4 * KD), **dict.fromkeys(("qkT", "qk_hi", "qk_tr"), rounds),
        **dict.fromkeys(("idx", "xT_ps", "xgT"), blocks + 1), **dict.fromkeys(("m_hi", "m_lo", "w_sc", "w_tr", "w_x"), KD),
        **dict.fromkeys(("up_ps", "up_sb"), 4 * AT), **dict.fromkeys(("br_hi", "br_lo"), 4 * BC),
        **dict.fromkeys(("w_hi", "w_lo"), SPLITS), "prod": CHUNKS, "tproj": 1, "cv_evac": 2 * BC, "cv_y": BC, "po_pad": 1,
        "h2_st0": 16 * (AT // 3), "h2_st1": 16 * (AT // 3), "h2_st2": 16 * (AT // 3), "par_b": 16 * 8, "par_g": 32, "par_n1": 48, "par_n2": 48,
        "par_g2": 16, "par_p": 16, "par_sb": 16, "x_back": 16 * AT,
        "xg0": 16 * (blocks // 2 + 1), "xg1": 16 * ((blocks + 1) // 2),
        "y_st0": 16 * ((blocks + 1) // 2), "y_st1": 16 * (blocks // 2), **{f"yg{j}": 32 * (AT // 3) for j in range(3)},
    }
    return counts[name]


def latent_steps(n, nt):
    return n // nt * LT + min(n % nt, LT)


def rope_tables():
    t = np.arange(SEQ)
    grid = np.stack([t // GRID_W, t % GRID_W], -1).astype(np.float32)
    inv = (np.float32(10000.0) ** (-np.arange(AXIS_PAIRS, dtype=np.float32) / np.float32(AXIS_PAIRS))).astype(np.float32)
    ang = np.concatenate([grid[:, :1] * inv, grid[:, 1:] * inv], -1).astype(np.float32).astype(np.float64)
    tabs = [np.concatenate([f(ang), f(ang)], -1).astype(np.float32) for f in (np.cos, np.sin)]
    return np.ascontiguousarray(np.stack([x.reshape(LT, P, ROPE).transpose(1, 0, 2) for x in tabs], 1))


def pool_edges():
    rows = []
    for w in WINDOWS:
        first = [w / (min(j + w - w // 2, w)) for j in range(PP)]
        last = [w / (min(PP - j, w - w // 2) + w // 2) for j in range(PP)]
        rows.append(first + last)
    return np.asarray(rows, np.float32)


def trunk(nc, A, out):
    mod_rows = nc.dram_tensor("mod_rows", [DEPTH, 2, N_MOD * D], F32, kind="Internal").ap()
    x_spill = nc.dram_tensor("x_spill", [TOK, D], F32, kind="Internal").ap()
    h2_rows = nc.dram_tensor("h2_rows", [TOK, D], F32, kind="Internal").ap()
    y_rows = [nc.dram_tensor(f"y_rows_{l}", [expert_blocks(SEQ if l else TOK) * P, D], F32, kind="Internal").ap()
              for l in range(DEPTH)]

    with ExitStack() as ctx:
        free = [0]
        base = (nc.sbuf_base + 31) // 32 * 32

        def place(name, width, dt=F32, parts=P, over=None):
            at_ = free[0] if over is None else over
            if over is None:
                free[0] += (width + 7) // 8 * 8
            return nc.alloc_sbuf_tensor_at(name, [parts, width], dt, offset=base + 4 * at_)

        X = place("X", AT * D)
        HTF = place("HTF", 2 * KD * TOK)
        HTH = place("HTH", KD * TOK, F32R, over=AT * D)
        HTL = place("HTL", KD * TOK, F32R, over=2 * AT * D)
        br0 = free[0]
        BR = place("BR", 2 * BC * TOK)
        BRH = place("BRH", BC * TOK, F32R, over=br0)
        BRL = place("BRL", BC * TOK, F32R, over=br0 + BC * TOK)
        mg0 = free[0]
        MGZ = place("MGZ", 2 * KD * TOK)
        MGL = place("MGL", KD * TOK, F32R, over=mg0)
        MGH = place("MGH", KD * TOK, F32R, over=mg0 + KD * TOK)
        ring0 = free[0]
        RAWB = place("RAWB", RAWS * RAW)
        WS = place("WS", 2 * KD * KVQ, F32R)
        RING = place("RING", (SLOTS - 1) * SLAB, over=ring0)
        assert (SLOTS - 1) * SLAB <= free[0] - ring0 and 4 * RAW <= 2 * KD * KVQ
        t0 = free[0]
        T = place("T", 2304)
        SG = place("SG", 3 * BW)
        ident = place("ident", P)
        cw = place("cw", 16 + 2 * KD)
        edge = place("edge", 4 * 2 * PP)
        st = place("st", 2 * AT)
        rst = place("rst", 2 * AT)
        srt = place("srt", 2 * AT)
        scT = place("scT", 2 * KD)
        scH, scL = place("scH", 2 * KD, F32R), place("scL", 2 * KD, F32R)
        QKH = place("QKH", 3072, F32R, over=3072)
        QKL0 = place("QKL0", 1536, F32R, over=br0 + 5 * TOK)
        QKL1 = place("QKL1", 1536, F32R, over=t0 + 512)
        MODH = place("MODH", 3 * SLAB, F32R, over=br0)
        MODL0 = place("MODL0", SLAB, F32R, over=AT * D + 6 * D)
        MODL2 = place("MODL2", SLAB, F32R, over=t0)
        MODL1 = place("MODL1", SLAB, F32R, over=AT * D + 10 * D)
        ps = ctx.enter_context(nc.psum_tensor("ps", [P, 4, 1024], F32))

        def W(l):
            return TOK if l < DEPTH - 1 else SEQ

        def tiles(l):
            return W(l) // P

        x_t = X[:, :].rearrange("p (t d) -> p t d", t=AT)
        hH, hL = (a[:, :].rearrange("p (k t) -> p k t", k=KD) for a in (HTH, HTL))
        brH, brL = (a[:, :].rearrange("p (c t) -> p c t", c=BC) for a in (BRH, BRL))
        mH, mL = (a[:, :].rearrange("p (k t) -> p k t", k=KD) for a in (MGH, MGL))
        BRA, BRB = BR[:, 0:BC * TOK], BR[:, BC * TOK:2 * BC * TOK]
        merged = MGZ[:, 0:KD * TOK].rearrange("p (k t) -> p k t", k=KD)
        qk = MGZ[:, 0:AT * 2 * H * QK].rearrange("p (t s h e) -> p t s h e", t=AT, s=2, h=H)
        vb = MGZ[:, AT * 2 * H * QK:AT * (2 * H * QK + BW)].rearrange("p (t c) -> p t c", t=AT)
        mod_hi = [MODH[:, j * SLAB:(j + 1) * SLAB].rearrange("p (k n) -> p k n", k=KD) for j in range(3)]
        mod_lo = [a[:, :].rearrange("p (k n) -> p k n", k=KD) for a in (MODL0, MODL1, MODL2)]
        mod_sb = (HTF[0:2, 0:N_MOD * D], MGZ[0:2, KD * TOK:KD * TOK + N_MOD * D])

        kvqH, kvqL = (WS[:, j * KD * KVQ:(j + 1) * KD * KVQ].rearrange("p (k n) -> p k n", k=KD) for j in range(2))

        def raw_slab(r, n):
            return RAWB[:, r % RAWS * RAW:r % RAWS * RAW + n]

        def parts(s, n):
            return [WS[:, (2 * (s % 2) + j) * RAW:(2 * (s % 2) + j) * RAW + n] for j in range(2)]

        def words(s):
            gate = any(g <= s < g + KD for g in (G_AT, G_SG, G_CV, G_PO))
            return RAW if gate else KD * P

        def slot(s):
            return RING[:, s * SLAB:(s + 1) * SLAB] if s < SLOTS - 1 else HTF[:, 8 * D:8 * D + SLAB]

        def slot3(s, a):
            return slot(s).rearrange("p (a n) -> p a n", a=a)

        def psb(i):
            return ps[:, i, :]

        def bank(i):
            return ps[:, i // 2, (i % 2) * 512:(i % 2 + 1) * 512]

        def shift1(v):
            return MGZ[:, v * 2 * D:v * 2 * D + D]

        def scale1(v):
            return MGZ[:, v * 2 * D + D:(v + 1) * 2 * D]

        gain1 = MGZ[:, 4 * D:5 * D]
        sgub = SG[:, 0:BW]
        sguwT = SG[:, BW:2 * BW].rearrange("p (g q) -> p g q", g=BC)
        g_sgu = SG[:, 2 * BW:3 * BW]
        htok = [BRA[:, j * D:(j + 1) * D] for j in range(2)]
        sguw = BRA[:, 2 * D:2 * D + BW].rearrange("p (g q) -> p g q", g=BC)
        crow = BR[0:16 + 2 * KD, 2 * D + BW:2 * D + BW + P]
        g_kva = BRB[:, 0:128]
        g_qa = BRB[:, 128:384]
        g_qk = BRB[:, 384:384 + 2 * QK].rearrange("p (s e) -> p s e", s=2)
        PARAMS = 576
        cn = [T[:, j * 384:(j + 1) * 384] for j in range(2)]
        cnT = [T[:, 768 + j * 384:768 + (j + 1) * 384] for j in range(2)]
        cosv = T[:, 1536:1536 + LT * ROPE].rearrange("p (t e) -> p t e", t=LT)
        sinv = T[:, 1664:1664 + LT * ROPE].rearrange("p (t e) -> p t e", t=LT)
        ssq = [T[:, 1792 + j * 16:1808 + j * 16] for j in range(2)]
        rsq = [T[:, 1824 + j * 16:1840 + j * 16] for j in range(2)]
        RB = 4
        raw = [X[:, j * 1536:(j + 1) * 1536].rearrange("p (s h e) -> p s h e", s=2, h=H) for j in range(RB)]
        sqj = [X[:, 3072 + t * 384:3072 + (t + 1) * 384] for t in range(AT)]
        sgv = X[:, 0:AT * BW].rearrange("p (t c) -> p t c", t=AT)
        uT = [X[:, AT * BW + g * TOK:AT * BW + (g + 1) * TOK] for g in range(BC)]
        umix = [T[:, j * TOK:(j + 1) * TOK] for j in range(2)]
        gcs = [X[:, j * TOK:(j + 1) * TOK] for j in range(2)]
        gbs = [X[:, (2 + j) * TOK:(3 + j) * TOK] for j in range(2)]
        cup = [X[:, 4 * TOK + j * CVW:4 * TOK + (j + 1) * CVW] for j in range(2)]
        cvy = [T[:, j * CVW:(j + 1) * CVW] for j in range(2)]
        poolw = X[:, 5400:5400 + BC * P].rearrange("p (g d) -> p g d", g=BC)
        pp = [X[:, j * PLW:(j + 1) * PLW] for j in range(2)]
        pacc = [X[:, (2 + j) * PLW:(3 + j) * PLW] for j in range(2)]
        pooled = [X[:, 4 * PLW + j * TOK:4 * PLW + (j + 1) * TOK] for j in range(2)]
        oT = X[:, 0:BC * TOK].rearrange("p (c t) -> p c t", c=BC)
        qkH = [QKH[:, j * 1536:(j + 1) * 1536] for j in range(2)]
        qkL = [QKL0, QKL1]
        probs = [BR[:, j * TOK:(j + 1) * TOK] for j in range(3)]
        prT = [BR[:, (3 + j) * TOK:(4 + j) * TOK] for j in range(2)]
        negm = T[:, 0:H * AT]
        rsum = T[:, 64:64 + H * AT]
        rinv = T[:, 128:128 + H * AT]
        sig = [T[:, j * TOK:(j + 1) * TOK] for j in range(2)]
        prod = T[:, 2 * TOK:3 * TOK]
        wsc = sig
        mrow = HTF[:, 0:4 * D].rearrange("p (v m d) -> p v m d", v=2, m=2)
        gain2 = HTF[:, 4 * D:5 * D]
        grow = T[:, 0:2 * D].rearrange("p (v d) -> p v d", v=2)
        h2tok = [BRA[:, j * D:(j + 1) * D] for j in range(3)]
        late = MGZ[:, 7 * D:12 * D]
        h2T = [late[:, j * D:(j + 1) * D].rearrange("p (k t) -> p k t", k=KD) for j in range(2)]
        junk = BRB[:, 2 * D:3 * D]
        xg = htok
        xgT = h2T
        sil = [late[:, 2 * D + j * FF:2 * D + (j + 1) * FF] for j in range(2)]
        act_a = [late[:, 2 * D + (2 + j) * FF:2 * D + (3 + j) * FF] for j in range(2)]
        act_T = [late[:, 3 * D + j * FF:3 * D + (j + 1) * FF].rearrange("p (k t) -> p k t", k=2) for j in range(2)]
        ysb = [MGZ[:, (5 + j) * D:(6 + j) * D] for j in range(2)]
        yg = [[MGZ[:, (5 + 2 * j + k) * D:(6 + 2 * j + k) * D] for k in range(2)] for j in range(3)]
        ytmp = [late[:, 4 * D:5 * D], junk]
        cursor = [PARAMS]

        def rt(*shape):
            n = int(np.prod(shape))
            a = BRB[:, cursor[0]:cursor[0] + n]
            cursor[0] += n
            if len(shape) == 1:
                return a
            names = "abcd"[:len(shape)]
            return a.rearrange(f"p ({' '.join(names)}) -> p {' '.join(names)}",
                               **{n_: s for n_, s in zip(names[:-1], shape[:-1])})

        r_s, r_sb, r_m, r_sc = rt(AT, NE), rt(AT, NE), rt(AT, NE), rt(AT, NE)
        r_oh = [rt(AT, NE), rt(AT, NE)]
        r_any = rt(AT + 1, NE)
        r_pair = rt(AT * NG, 6)
        r_gs, r_gq, r_gm = rt(AT, NG), rt(AT, NG), rt(AT, NG)
        r_mx = rt(AT)
        r_w = [rt(AT), rt(AT)]
        r_den = rt(AT)
        r_cnt = rt(NE, 6)
        r_nb, r_end, r_base = rt(NE), rt(NE), rt(NE)
        r_slot, r_place = rt(2, AT), rt(2, AT)
        r_blk = rt(MAXB, NE)
        r_eid = rt(MAXB)
        assert cursor[0] <= BC * TOK
        slot_i = place("slot_i", 2 * AT, I32)
        eid_i = place("eid_i", MAXB + 1, I32)
        tab_i = place("tab_i", MAXB + 1, I32)
        idx_i = [place(f"idx_i{j}", 1, I32) for j in range(2)]
        lgT = MGZ[0:NE, 0:TOK]
        NB = MAXB + 1
        ge_blk = MGZ[:, 0:2 * AT * (NB + 1)].rearrange("p (k t b) -> p k t b", k=2, t=AT)
        tok_blk = MGZ[:, 512:512 + 2 * AT * NB].rearrange("p (k t b) -> p k t b", k=2, t=AT)
        at_place = MGZ[:, D:D + 2 * AT * P].rearrange("p (k t j) -> p k t j", k=2, t=AT)
        assert 2 * AT * (NB + 1) <= 512
        gw = [r_w[0], r_w[1]]
        rw = place("rw", KD * NE)
        rwv = rw[:, :].rearrange("p (k e) -> p k e", k=KD)
        rbias = place("rbias", NE)
        ones = place("ones", P)
        tri = place("tri", P)
        w4 = place("w4", NG)
        w16 = place("w16", NE)
        steps6 = place("steps6", 6)
        blkno = place("blkno", MAXB)
        blk0 = place("blk0", MAXB + 2)
        placeno = place("placeno", P)
        tokf = place("tokf", AT)
        iint = place("iint", 256, I32, over=t0 + 1024)

        sems = {}

        def S(name):
            if name not in sems:
                sems[name] = ctx.enter_context(nc.semaphore(name))
            return sems[name]

        def at(name, l, n):
            return n + (signals(name) if l else 0)

        slab_full = [S(f"slab_full{s}") for s in range(SLOTS)]
        slab_used = S("slab_used")
        raw_full = [S(f"raw_full{s}") for s in range(RAWS)]

        def split_no(l, s):
            return at("w_lo", l, len(KVQ_SPLIT) + s + 1)

        def done_no(l, s):
            return at("prod", l, s + 1)

        def cols(w, c0, n):
            return w[:, c0:c0 + n].rearrange("(k p) n -> p k n", p=P)

        def raw_loads(l):
            w_in, k0, r = A["w_in"][l], 0, []
            for n in KVQ_SPLIT:
                r.append([(0, n, KVQ, w_in[k0 * P:(k0 + n) * P, 0:KVQ].rearrange("(k p) n -> p k n", p=P))])
                k0 += n
            r.append([(0, 1, D, A["w_ukv"][l].rearrange("p (a h) e -> p a (h e)", a=1))])
            r.append([(0, 2, H * QK, A["w_uq"][l].rearrange("(k p) h e -> p k (h e)", p=P))])

            def gate(n):
                return [[(0, KD, P, cols(w_in, GATE_OFF + n * D + d * P, P)),
                         (KD * P, BC, P, A["w_branch"][l, n][:, d * P:(d + 1) * P].rearrange("(k p) n -> p k n", p=P))]
                        for d in range(KD)]

            def plain(w, c0):
                return [(0, KD, P, cols(w, c0, P))]

            r += gate(0)
            v0 = SGU_OFF + BW
            r += [[(0, 2, BW, w_in[2 * j * P:2 * (j + 1) * P, v0:v0 + BW].rearrange("(k p) n -> p k n", p=P))] for j in range(4)]
            r += [plain(w_in, SGU_OFF + g * P) for g in range(BC)]
            r += gate(3)
            r += [plain(w_in, CONV_OFF + part * BW + c * P) for c in range(BC) for part in (1, 0, 2)]
            r += gate(1)
            r += [plain(w_in, POOL_OFF + g * P) for g in reversed(range(BC))]
            r += gate(2)
            r += [plain(A["w_o"][l], n * P) for n in range(KD)]
            return r

        loads = [raw_loads(l) for l in range(DEPTH)]
        FIRST = len(KVQ_SPLIT) + 2
        assert FIRST + CHUNKS == len(loads[0]) and len(loads[0]) % RAWS == 0
        full_no, sums = {}, [0] * RAWS
        for l_ in range(DEPTH):
            for r_, pieces in enumerate(loads[l_]):
                sums[r_ % RAWS] += 16 * len(pieces)
                full_no[l_, r_] = sums[r_ % RAWS]

        def up_items(l, t):
            return 4 * min(t, tiles(l)) + 2 * max(t - tiles(l), 0)

        block = ctx.enter_context(nc.Block())

        @block.sync
        def _(sp):
            issued = [0]

            def load(shape, src, before=None, at=None):
                n = issued[0] if at is None else at
                if n >= SLOTS or before is not None:
                    need = n - SLOTS + 1
                    sp.wait_ge(slab_used, need if before is None else before + need)
                a, m = shape
                sp.dma_start(slot(n % SLOTS)[:, 0:a * m].rearrange("p (a m) -> p a m", a=a), src)\
                    .then_inc(slab_full[n % SLOTS], 16)
                if at is None:
                    issued[0] += 1

            def mod_cols(l, c0):
                return A["mod_w"][l][:, c0].rearrange("(k p) n -> p k n", p=P)

            for j in range(SLOTS):
                load((KD, 256), mod_cols(0, slice(j * 256, (j + 1) * 256)))
            for l in range(DEPTH):
                start = 1 if l == 0 else 0
                turn0 = l * MC // 2
                with sp.Fori(start, MC // (2 * SLOTS)) as i:
                    for j in range(SLOTS):
                        load((KD, 256), mod_cols(l, bass.ds(i * (256 * SLOTS) + j * 256, 256)), i * SLOTS, turn0 + j)
                issued[0] = (l + 1) * MC // 2

            for l in range(DEPTH):
                if l == 0:
                    sp.wait_ge(S("mod_row"), DEPTH * MC // 2)
                else:
                    sp.wait_ge(S("y_sb"), at("y_sb", l - 1, expert_blocks(W(l - 1))))
                for r, pieces in enumerate(loads[l]):
                    if RAWS <= r < FIRST + 1:
                        sp.wait_ge(S("w_lo"), at("w_lo", l, r - RAWS + 1))
                    elif FIRST + 1 <= r < FIRST + RAWS:
                        sp.wait_ge(S("up_sb"), at("up_sb", l, up_items(l, AT)))
                    elif r >= FIRST + RAWS:
                        sp.wait_ge(S("w_lo"), split_no(l, r - FIRST - RAWS))
                    for o, a, m, src in pieces:
                        sp.dma_start(raw_slab(r, RAW)[:, o:o + a * m].rearrange("p (a m) -> p a m", a=a), src)\
                            .then_inc(raw_full[r % RAWS], 16)
                nb = expert_blocks(W(l))
                w1, w3, w2 = A["moe_w1"][l], A["moe_w3"][l], A["moe_w2"][l]
                sp.wait_ge(S("eid"), at("eid", l, 1))

                def up(b, n, before=None):
                    e = sp.value_load(eid_i[0:1, b] if before is None else eid_i[0:1, bass.ds(b, 1)],
                                      min_val=0, max_val=NE - 1)
                    for w in (w1, w3):
                        load((KD, FF), w[bass.ds(e, 1)].rearrange("e (k p) n -> p (e k) n", p=P), before, n)
                        n = None if n is None else n + 1

                def down(b, n, before=None):
                    e = sp.value_load(eid_i[0:1, b] if before is None else eid_i[0:1, bass.ds(b, 1)],
                                      min_val=0, max_val=NE - 1)
                    load((2, D), w2[bass.ds(e, 1)].rearrange("e (k p) n -> p (e k) n", p=P), before, n)

                up(slice(0, 1), None)
                sp.wait_ge(S("idx"), at("idx", l, 2))
                for b in (1, 2):
                    up(slice(b, b + 1), None)
                    down(slice(b - 1, b), None)
                n0 = issued[0]
                with sp.Fori(0, (nb - 3) // 2) as i:
                    for j in range(2):
                        up(i * 2 + (3 + j), n0 + 3 * j, i * SLOTS)
                        down(i * 2 + (2 + j), n0 + 3 * j + 2, i * SLOTS)
                issued[0] += 3 * (nb - 3)
                down(slice(nb - 1, nb), None)
            sp.wait_ge(S("x_stored"), 16 * LT)

        @block.tensor
        def _(pe):
            used = [0]
            owed = [0]
            mm = pe.matmul

            def pays(ins):
                if owed[0]:
                    ins.then_inc(slab_used, owed[0])
                    owed[0] = 0

            def arrived():
                n = used[0]
                pe.wait_ge(slab_full[n % SLOTS], 16 * (n // SLOTS + 1))
                used[0] += 1
                return n % SLOTS

            def three(out, w, x, n, first, stop):
                (wh, wl), (xh, xl) = w, x
                for i, (a, b) in enumerate(((wh, xh), (wh, xl), (wl, xh))):
                    last = mm(out, a, b, start=(first and i == 0), stop=(stop and i == 2))
                return last

            def chunk(l, s, x, pair, k0=0, kn=KD):
                w = [a.rearrange("p (k n) -> p k n", n=P) for a in parts(s, words(s))]
                last = None
                for k in range(kn):
                    for i, (a, b) in enumerate(((w[0], x[0]), (w[0], x[1]), (w[1], x[0]))):
                        go, end = k == 0 and i == 0, k == kn - 1 and i == 2
                        last = mm(psb(pair)[:, 0:SEQ], a[:, k0 + k, :], b[:, k, 0:SEQ], start=go, stop=end)
                        if W(l) > SEQ:
                            last = mm(psb(pair)[:, SEQ:TOK], a[:, k0 + k, :], b[:, k, SEQ:TOK], start=go, stop=end)
                return last

            pe.wait_ge(S("const"), 2)
            pe.wait_ge(S("c_silu"), 1)
            pe.transpose(psb(3)[:, 0:2 * KD], T[0:2 * KD, 0:P], ident[0:2 * KD, 0:2 * KD]).then_inc(S("c_tr"), 1)
            pe.wait_ge(S("c_col"), 1)
            scv = [a[:, :].rearrange("p (v k) -> p v k", v=2) for a in (scH, scL)]

            def mod_slab(j, split, read=None):
                pe.wait_ge(slab_used, split)
                if read is not None:
                    pe.wait_ge(S("mod_row"), read)
                w = (mod_hi[j % 3], mod_lo[j % 3])
                for k in range(KD):
                    last = three(bank(j)[0:2, 0:256], (scv[0][:, :, k], scv[1][:, :, k]), (w[0][:, k, :], w[1][:, k, :]),
                                 256, k == 0, k == KD - 1)
                last.then_inc(S("mod_ps"), 1)

            for j in range(SLOTS):
                mod_slab(j, j + 1)
            with pe.Fori(1, DEPTH * MC // (2 * SLOTS)) as i:
                for j in range(SLOTS):
                    mod_slab(j, i * SLOTS + (j + 1), i * SLOTS + (j + 1 - SLOTS))
            used[0] = DEPTH * MC // 2
            pe.wait_ge(S("mod_row"), used[0])

            for l in range(DEPTH):
                NT = tiles(l)
                for t in range(AT):
                    pe.wait_ge(S("h_tok"), at("h_tok", l, t + 1))
                    if t >= 2:
                        pe.wait_ge(S("hT_tile"), at("hT_tile", l, t - 1))
                    for k in range(KD):
                        last = pe.transpose(psb(t % 2)[:, k * P:(k + 1) * P], htok[t % 2][:, k * P:(k + 1) * P], ident[:, :])
                        if k == 0:
                            pays(last)
                    last.then_inc(S("h_tr"), 1)

                pe.wait_ge(S("hT_tile"), at("hT_tile", l, AT))
                k0 = 0
                for i, kn in enumerate(KVQ_SPLIT):
                    pe.wait_ge(S("w_lo"), at("w_lo", l, i + 1))
                    for t in range(AT):
                        n = KVQ if t < NT else Q_OFF
                        for k in range(k0, k0 + kn):
                            tok = slice(t * P, (t + 1) * P)
                            last = three(bank(t)[:, 0:n], (hH[:, k, tok], hL[:, k, tok]), (kvqH[:, k, 0:n], kvqL[:, k, 0:n]),
                                         n, k == 0, k == KD - 1)
                    k0 += kn
                last.then_inc(S("tproj"), 1)

                wukv, wuq = raw_slab(3, D), raw_slab(4, 2 * H * QK).rearrange("p (k n) -> p k n", k=2)
                pe.wait_ge(raw_full[0], full_no[l, 3])
                pe.wait_ge(raw_full[1], full_no[l, 4])
                for u in range(AT):
                    pe.wait_ge(S("cn"), at("cn", l, u + 1))
                    for j in range(3 if u < NT else 1):
                        last = pe.transpose(bank(u)[:, j * P:(j + 1) * P], cn[u % 2][:, j * P:(j + 1) * P], ident[:, :])
                    last.then_inc(S("cn_tr"), 1)
                    n0 = up_items(l, u)
                    pe.wait_ge(S("cnT"), at("cnT", l, u + 1))
                    for j in range(2):
                        if u:
                            pe.wait_ge(S("up_sb"), at("up_sb", l, n0 - 2 * j if u <= NT else n0 - 1 + j))
                        mm(bank(6 + j), cnT[u % 2][:, 0:P], wukv[:, j * 512:(j + 1) * 512], start=True, stop=True)\
                            .then_inc(S("up_ps"), 1)
                    if u < NT:
                        for j in range(2):
                            if j:
                                pe.wait_ge(S("up_sb"), at("up_sb", l, n0 + 1))
                            o = bank(6 if j else u)[:, 0:384]
                            for k in range(2):
                                last = mm(o, cnT[u % 2][:, (1 + k) * P:(2 + k) * P], wuq[:, k, j * 384:(j + 1) * 384],
                                          start=(k == 0), stop=(k == 1))
                            last.then_inc(S("up_ps"), 1)
                pe.wait_ge(S("up_sb"), at("up_sb", l, up_items(l, AT)))
                pe.wait_ge(S("par_b"), at("par_b", l, 16 * 8))
                for g in range(BC):
                    pe.transpose(bank(6)[:, g * P:(g + 1) * P], sguw[:, g, :], ident[:, :])
                nc_ = 16 + 2 * KD
                pe.transpose(bank(7)[:, 0:nc_], crow, ident[0:nc_, 0:nc_]).then_inc(S("wT_tr"), 1)
                pe.wait_ge(S("wT"), at("wT", l, 1))

                def gate(q, s0, d):
                    u = q * KD + d
                    pe.wait_ge(S("w_lo"), split_no(l, s0 + d))
                    if d >= 2:
                        pe.wait_ge(S("g_sig"), at("g_sig", l, u - 1))
                    chunk(l, s0 + d, (hH, hL), u % 2).then_inc(S("g_ps"), 1)

                def gated(q, s0, begun=0):
                    for d in range(KD):
                        u = q * KD + d
                        if d >= begun:
                            gate(q, s0, d)
                        if d == 0:
                            pe.wait_ge(S("br_lo"), at("br_lo", l, (q + 1) * BC))
                        if d >= 2:
                            pe.wait_ge(S("g_prod"), at("g_prod", l, u - 1))
                        chunk(l, s0 + d, (brH, brL), 2 + u % 2, KD, BC).then_inc(S("prod"), 1)
                    pe.wait_ge(S("g_sig"), at("g_sig", l, (q + 1) * KD))
                    pe.wait_ge(S("g_prod"), at("g_prod", l, (q + 1) * KD))

                pe.wait_ge(S("t_qk"), at("t_qk", l, AT))
                steps = [(h, t) for h in range(H) for t in range(NT)]
                rounds = (AT + NT + 3) // 4

                def transposes(h, r):
                    n = h * rounds + r
                    if n >= 1:
                        pe.wait_ge(S("qkT"), at("qkT", l, n))
                    for i in range(4 * r, min(4 * r + 4, AT + NT)):
                        src = qk[:, i, 0, h, :] if i < AT else qk[:, i - AT, 1, h, :]
                        last = pe.transpose(psb(3)[0:QK, 512 + (i % 4) * P:512 + (i % 4 + 1) * P], src, ident[:, :])
                    last.then_inc(S("qk_tr"), 1)

                def key_tiles(t):
                    return range(0, AT) if t < LT else range(LT, AT)

                for r in range(rounds):
                    transposes(0, r)
                for n in range(len(steps) + 3):
                    if n < len(steps):
                        h, t = steps[n]
                        if t == 0:
                            pe.wait_ge(S("qkT"), at("qkT", l, (h + 1) * rounds))
                        if n >= 2:
                            pe.wait_ge(S("probs"), at("probs", l, n - 1))
                        qt = slice((AT + t) * P, (AT + t + 1) * P)
                        q = [a[h % 2][0:QK, qt] for a in (qkH, qkL)]
                        for a, b in ([(0, SEQ)] if t < LT else []) + [(SEQ, TOK)]:
                            last = three(psb(n % 2)[:, a:b], q, [x[h % 2][0:QK, a:b] for x in (qkH, qkL)], b - a, True, True)
                        last.then_inc(S("s_ps"), 1)
                        if h + 1 < H and t < rounds:
                            transposes(h + 1, t)
                    if 2 <= n <= len(steps) + 1:
                        m = n - 2
                        h, t = steps[m]
                        pe.wait_ge(S("p_norm"), at("p_norm", l, m + 1))
                        if m >= 1:
                            pe.wait_ge(S("prT_a"), at("prT_a", l, latent_steps(m, NT)))
                            pe.wait_ge(S("prT_d"), at("prT_d", l, m))
                        for kt in key_tiles(t):
                            last = pe.transpose(psb(2)[:, kt * P:(kt + 1) * P], probs[m % 3][:, kt * P:(kt + 1) * P], ident[:, :])
                        last.then_inc(S("pr_tr"), 1)
                    if n >= 3:
                        m = n - 3
                        h, t = steps[m]
                        pe.wait_ge(S("prT_a"), at("prT_a", l, latent_steps(m + 1, NT)))
                        pe.wait_ge(S("prT_d"), at("prT_d", l, m + 1))
                        if m >= 1:
                            pe.wait_ge(S("o_sb"), at("o_sb", l, m))
                        ks = list(key_tiles(t))
                        for kt in ks:
                            last = mm(psb(3)[0:VD, (m % 2) * P:(m % 2 + 1) * P], vb[:, kt, h * VD:(h + 1) * VD],
                                      prT[m % 2][:, kt * P:(kt + 1) * P], start=(kt == ks[0]), stop=(kt == ks[-1]))
                        last.then_inc(S("o_ps"), 1)
                pe.wait_ge(S("probs"), at("probs", l, len(steps)))
                gated(0, G_AT)

                for j in range(4):
                    pe.wait_ge(S("w_lo"), split_no(l, S_V + j))
                    w = [a.rearrange("p (k n) -> p k n", n=BW) for a in parts(S_V + j, 2 * BW)]
                    for t in range(NT):
                        for i in range(2):
                            k, tok = 2 * j + i, slice(t * P, (t + 1) * P)
                            last = three(bank(t), (hH[:, k, tok], hL[:, k, tok]), (w[0][:, i, :], w[1][:, i, :]),
                                         BW, k == 0, k == KD - 1)
                    last.then_inc(S("prod"), 1)
                home = (3, 0, 1, 2)
                for g in range(BC):
                    pe.wait_ge(S("w_lo"), split_no(l, S_U + g))
                    if g:
                        pe.wait_ge(S("sv_sq"), at("sv_sq", l, min(2 * g, NT)))
                    chunk(l, S_U + g, (hH, hL), home[g]).then_inc(S("prod"), 1)
                pe.wait_ge(S("sgv"), at("sgv", l, NT))
                for g in range(BC):
                    pe.wait_ge(S("sgu_u"), at("sgu_u", l, g + 1))
                    for t in range(NT):
                        last = mm(psb(home[g])[:, t * P:(t + 1) * P], sgv[:, t, g * P:(g + 1) * P], sguwT[:, g, :],
                                  start=True, stop=True)
                    last.then_inc(S("sgu_mix"), 1)
                pe.wait_ge(S("sgu_sum"), at("sgu_sum", l, 2))
                gated(1, G_SG)

                for c in range(BC):
                    for j in range(3):
                        w = 3 * c + j
                        pe.wait_ge(S("w_lo"), split_no(l, S_CV + w))
                        if w >= 4:
                            pc, pj = divmod(w - 4, 3)
                            if pj < 2:
                                pe.wait_ge(S("cv_evac"), at("cv_evac", l, 2 * pc + pj + 1))
                            else:
                                pe.wait_ge(S("cv_cu"), at("cv_cu", l, pc + 1))
                        chunk(l, S_CV + w, (hH, hL), w % 4).then_inc(S("prod"), 1)
                pe.wait_ge(S("cv_cu"), at("cv_cu", l, 3))
                gated(2, G_CV)

                pe.wait_ge(S("par_p"), at("par_p", l, 16))
                for g in range(BC + 1):
                    if g < BC:
                        pe.wait_ge(S("w_lo"), split_no(l, S_PO + g))
                        if g >= 2:
                            pe.wait_ge(S("po_pp"), at("po_pp", l, g - 1))
                        chunk(l, S_PO + g, (hH, hL), g % 2).then_inc(S("prod"), 1)
                    else:
                        pe.wait_ge(S("po_pp"), at("po_pp", l, 3))
                        gate(3, G_PO, 0)
                    if g >= 1:
                        h = g - 1
                        pe.wait_ge(S("po_pl"), at("po_pl", l, h + 1))
                        if h >= 2:
                            pe.wait_ge(S("br_lo"), at("br_lo", l, 3 * BC + h - 1))
                        last = mm(psb(2 + h % 2)[:, 0:SEQ], poolw[:, BC - 1 - h, :], pooled[h % 2][:, 0:SEQ], start=True, stop=True)
                        if W(l) > SEQ:
                            last = mm(psb(2 + h % 2)[:, SEQ:TOK], poolw[:, BC - 1 - h, :], pooled[h % 2][:, SEQ:TOK], start=True, stop=True)
                        last.then_inc(S("po_mix"), 1)
                gated(3, G_PO, 1)

                pe.wait_ge(S("m_lo"), at("m_lo", l, KD))
                for n in range(KD + 1):
                    if n < KD:
                        pe.wait_ge(S("w_lo"), split_no(l, S_WO + n))
                        if n >= 2:
                            pe.wait_ge(S("w_sc"), at("w_sc", l, n - 1))
                        chunk(l, S_WO + n, (mH, mL), n % 2).then_inc(S("prod"), 1)
                    if n >= 1:
                        m = n - 1
                        pe.wait_ge(S("w_sc"), at("w_sc", l, m + 1))
                        if m >= 2:
                            pe.wait_ge(S("w_x"), at("w_x", l, m - 1))
                        for t in range(NT):
                            last = pe.transpose(psb(2 + m % 2)[:, t * P:(t + 1) * P], wsc[m % 2][:, t * P:(t + 1) * P], ident[:, :])
                        last.then_inc(S("w_tr"), 1)

                pe.wait_ge(S("const_dma"), 48)
                for t in range(NT + 1):
                    if t < NT:
                        pe.wait_ge(S("h2_tok"), at("h2_tok", l, t + 1))
                        if t == 0:
                            pe.wait_ge(S("w_x"), at("w_x", l, KD))
                        if t >= 2:
                            pe.wait_ge(S("h2T"), at("h2T", l, t - 1))
                        for k in range(KD):
                            last = pe.transpose(psb(t % 2)[:, k * P:(k + 1) * P], h2tok[t % 3][:, k * P:(k + 1) * P], ident[:, :])
                            if k == 0:
                                pays(last)
                        last.then_inc(S("h2_tr"), 1)
                    if t >= 1:
                        u = t - 1
                        pe.wait_ge(S("h2T"), at("h2T", l, u + 1))
                        for k in range(KD):
                            last = mm(psb(3)[0:NE, u * P:(u + 1) * P], rwv[:, k, :], h2T[u % 2][:, k, :],
                                      start=(k == 0), stop=(k == KD - 1))
                        last.then_inc(S("lg_ps"), 1)
                pe.wait_ge(S("lg_sb"), at("lg_sb", l, 1))
                for t in range(NT):
                    last = pe.transpose(psb(2)[:, t * NE:(t + 1) * NE], lgT[:, t * P:(t + 1) * P], ident[0:NE, 0:NE])
                last.then_inc(S("lg_tr"), 1)

                pe.wait_ge(S("r_oh"), at("r_oh", l, 1))
                rank = psb(2)[:, 0:(NT + 1) * NE].rearrange("p (t e) -> p t e", e=NE)
                mm(rank, tri[:, :], r_any[:, 0:NT + 1, :], start=True, stop=False)
                for t in range(NT):
                    last = mm(rank[:, t + 1:NT + 1, :], ones[:, :], r_any[:, t:t + 1, :].to_broadcast([P, NT - t, NE]),
                              start=False, stop=(t == NT - 1))
                last.then_inc(S("rank_ps"), 1)
                nb = expert_blocks(W(l))
                pe.wait_ge(S("tab_oh"), at("tab_oh", l, 1))
                for i in range(2 * NT):
                    k, t = i // NT, i % NT
                    last = mm(psb(3)[:, 0:nb + 1], at_place[:, k, t, :], tok_blk[:, k, t, 0:nb + 1],
                              start=(i == 0), stop=(i == 2 * NT - 1))
                last.then_inc(S("tab_ps"), 1)

                def gather_T(b, j, first=False):
                    pe.wait_ge(S(f"xg{j}"), at(f"xg{j}", l, (b // 2 + 1) * 16 if isinstance(b, int) else b))
                    for k in range(KD):
                        last = pe.transpose(psb(0)[:, k * P:(k + 1) * P], xg[j][:, k * P:(k + 1) * P], ident[:, :])
                        if k == 0:
                            pays(last)
                    last.then_inc(S("xT_ps"), 1)

                def hidden(j, s1, s3):
                    for s, o in ((s1, 0), (s3, FF)):
                        for k in range(KD):
                            last = mm(psb(1)[:, o:o + FF], xgT[j][:, k, :], slot3(s, KD)[:, k, :],
                                      start=(k == 0), stop=(k == KD - 1))
                        last.then_inc(slab_used if s == s1 else S("h_ps"), 1)
                    owed[0] += 1

                def down(j, s2):
                    w = slot3(s2, 2)
                    for n in range(2):
                        for k in range(2):
                            last = mm(psb(2 + j)[:, n * 512:(n + 1) * 512], act_T[j][:, k, :], w[:, k, n * 512:(n + 1) * 512],
                                      start=(k == 0), stop=(k == 1))
                    last.then_inc(S("y_ps"), 1)
                    owed[0] += 1

                def act_transpose(j):
                    for k in range(2):
                        last = pe.transpose(psb(1)[:, 512 + k * P:512 + (k + 1) * P], act_a[j][:, k * P:(k + 1) * P], ident[:, :])
                        if k == 0:
                            pays(last)
                    last.then_inc(S("aT_ps"), 1)

                pe.wait_ge(S("tab_i"), at("tab_i", l, 1))
                gather_T(0, 0)
                for b in range(3):
                    pe.wait_ge(S("xgT"), at("xgT", l, b + 1))
                    if b:
                        pe.wait_ge(S("a_sb"), at("a_sb", l, b))
                    hidden(b % 2, arrived(), arrived())
                    gather_T(b + 1, (b + 1) % 2)
                    if b:
                        pe.wait_ge(S("aT_sb"), at("aT_sb", l, b))
                        down((b - 1) % 2, arrived())
                    pe.wait_ge(S("a_sb"), at("a_sb", l, b + 1))
                    act_transpose(b % 2)
                n0 = used[0]
                with pe.Fori(0, (nb - 3) // 2) as i:
                    for j in range(2):
                        par = (3 + j) % 2
                        sl = [(n0 + 3 * j + c) % SLOTS for c in range(3)]
                        turn = [16 * ((n0 + 3 * j + c) // SLOTS + 1) for c in range(3)]
                        b = i * 2 + (3 + j)
                        pe.wait_ge(S("xgT"), at("xgT", l, b + 1))
                        pe.wait_ge(S("a_sb"), at("a_sb", l, b))
                        pe.wait_ge(slab_full[sl[0]], i * 16 + turn[0])
                        pe.wait_ge(slab_full[sl[1]], i * 16 + turn[1])
                        hidden(par, sl[0], sl[1])
                        gather_T(i * 16 + ((4 + j) // 2 + 1) * 16, 1 - par)
                        pe.wait_ge(S("aT_sb"), at("aT_sb", l, b))
                        pe.wait_ge(S("y_sb"), at("y_sb", l, b - 2))
                        pe.wait_ge(slab_full[sl[2]], i * 16 + turn[2])
                        down(1 - par, sl[2])
                        pe.wait_ge(S("a_sb"), at("a_sb", l, b + 1))
                        act_transpose(par)
                used[0] += 3 * (nb - 3)
                pe.wait_ge(S("aT_sb"), at("aT_sb", l, nb))
                pe.wait_ge(S("y_sb"), at("y_sb", l, nb - 2))
                down((nb - 1) % 2, arrived())

        @block.scalar
        def _(act):
            act_f = act.activation
            chain = [0]

            def link(ins):
                chain[0] += 1
                ins.then_inc(S("act_chain"), 1)
                act.wait_ge(S("act_chain"), chain[0])

            act.wait_ge(S("c_rows"), 32)
            act_f(T[0:2 * KD, 0:P], T[0:2 * KD, P:2 * P], ACT.Silu).then_inc(S("c_silu"), 1)
            act.wait_ge(S("c_tr"), 1)
            act_f(scT[:, :], psb(3)[:, 0:2 * KD], ACT.Copy).then_inc(S("c_col"), 1)
            act.wait_ge(S("c_col"), 1)
            act_f(scH[:, :], scT[:, :], ACT.Copy).then_inc(S("c_hi"), 1)

            def mod_hi_part(j, full, used_=None):
                act.wait_ge(slab_full[j], full)
                if used_ is not None:
                    act.wait_ge(S("mod_ps"), used_)
                act_f(mod_hi[j % 3], slot3(j, KD), ACT.Copy).then_inc(S("mod_hi"), 1)

            for j in range(SLOTS):
                mod_hi_part(j, 16, j - 2 if j >= 3 else None)
            for t in range(AT):
                src = A["x"][0, t * P:(t + 1) * P, :] if t < LT else A["ctx"][0, (t - LT) * P:(t - LT + 1) * P, :]
                act.dma_start(x_t[:, t, :], src).then_inc(S("x_in"), 16)
            with act.Fori(1, DEPTH * MC // (2 * SLOTS)) as i:
                for j in range(SLOTS):
                    mod_hi_part(j, i * 16 + 16, i * SLOTS + (j - 2))

            def to_h(l, t):
                if 1 <= t <= AT:
                    if l > 0:
                        act.wait_ge(S("x_new"), at("x_new", l - 1, t))
                        act.dma_start(x_spill[(t - 1) * P:t * P, :], x_t[:, t - 1, :]).then_inc(S("x_spilled"), 16)
                    if t > 1:
                        act.wait_ge(S("n1_sq"), at("n1_sq", l, t - 1))
                    act_f(psb(3), x_t[:, t - 1, :], ACT.Square, scale=D ** -0.5, accum_out=st[:, t - 1:t]).then_inc(S("n1_sq"), 1)
                if 2 <= t <= AT + 1:
                    act.wait_ge(S("n1_eps"), at("n1_eps", l, t - 1))
                    act_f(srt[:, t - 2:t - 1], rst[:, t - 2:t - 1], ACT.Sqrt).then_inc(S("n1_rt"), 1)
                if 3 <= t < 3 + len(KVQ_SPLIT):
                    i, k0, kn = t - 3, sum(KVQ_SPLIT[:t - 3]), KVQ_SPLIT[t - 3]
                    act.wait_ge(raw_full[i], full_no[l, i])
                    act_f(kvqH[:, k0:k0 + kn, :], raw_slab(i, kn * KVQ).rearrange("p (k n) -> p k n", k=kn), ACT.Copy)\
                        .then_inc(S("w_hi"), 1)
                if t >= 3:
                    u = t - 3
                    act.wait_ge(S("h_tr"), at("h_tr", l, u + 1))
                    act_f(hH[:, :, u * P:(u + 1) * P], psb(u % 2).rearrange("p (k t) -> p k t", k=KD), ACT.Copy)\
                        .then_inc(S("hT_hi"), 1)

            for l in range(DEPTH):
                NT = tiles(l)
                if l == 0:
                    act.wait_ge(S("x_in"), 16 * AT)
                    for t in range(AT + 3):
                        to_h(l, t)

                def evacuate(t):
                    full = t < NT
                    act.wait_ge(S("cn_tr"), at("cn_tr", l, t + 1))
                    n = 384 if full else P
                    act_f(cnT[t % 2][:, 0:n], bank(t)[:, 0:n], ACT.Copy).then_inc(S("cnT"), 1)
                    if t >= RB:
                        act.wait_ge(S("t_qk"), at("t_qk", l, t - RB + 1))
                    for j in range(2):
                        act.wait_ge(S("up_ps"), at("up_ps", l, up_items(l, t) + j + 1))
                        kv = bank(6 + j).rearrange("p (h e) -> p h e", h=4)
                        act_f(raw[t % RB][:, 0, 4 * j:4 * j + 4, 0:NOPE], kv[:, :, 0:NOPE], ACT.Copy)
                        act_f(vb[:, t, j * 256:(j + 1) * 256].rearrange("p (h e) -> p h e", h=4), kv[:, :, NOPE:P], ACT.Copy)\
                            .then_inc(S("up_sb"), 1)
                    if full:
                        for j in range(2):
                            act.wait_ge(S("up_ps"), at("up_ps", l, up_items(l, t) + j + 3))
                            act_f(raw[t % RB][:, 1, 4 * j:4 * j + 4, :],
                                  bank(6 if j else t)[:, 0:384].rearrange("p (h e) -> p h e", h=4), ACT.Copy).then_inc(S("up_sb"), 1)
                    n = (2 if full else 1) * H * QK
                    act.wait_ge(S("up_sb"), at("up_sb", l, up_items(l, t + 1)))
                    act.wait_ge(S("cn"), at("cn", l, t + 1))
                    act_f(qk[:, t].rearrange("p s h e -> p (s h e)")[:, 0:n], raw[t % RB].rearrange("p s h e -> p (s h e)")[:, 0:n], ACT.Square)\
                        .then_inc(S("t_sqd"), 1)

                def head_roots(t):
                    n = 2 * H if t < NT else H
                    act.wait_ge(S("t_ss"), at("t_ss", l, t + 1))
                    act_f(rsq[t % 2][:, 0:n], ssq[t % 2][:, 0:n], ACT.Sqrt).then_inc(S("t_hrt"), 1)

                if l > 0:
                    act.wait_ge(S("x_spilled"), 16 * AT)
                act.wait_ge(S("h_tr"), at("h_tr", l, AT))
                act.wait_ge(S("tproj"), at("tproj", l, 1))
                for t in range(AT):
                    if t < NT:
                        act_f(sqj[t][:, P:384], bank(t)[:, Q_OFF:CONV_OFF], ACT.Square, scale=Q_LORA ** -0.5,
                              accum_out=st[:, AT + t:AT + t + 1])
                    last = act_f(sqj[t][:, 0:P], bank(t)[:, 0:KV_LORA], ACT.Square, scale=KV_LORA ** -0.5,
                                 accum_out=st[:, t:t + 1])
                last.then_inc(S("t_sq"), 1)
                act.wait_ge(S("t_eps"), at("t_eps", l, 1))
                act_f(srt[:, 0:AT + NT], rst[:, 0:AT + NT], ACT.Sqrt).then_inc(S("t_rt"), 1)
                for t in range(AT + 1):
                    if t < AT:
                        evacuate(t)
                    if t >= 1:
                        head_roots(t - 1)
                act.wait_ge(S("wT_tr"), at("wT_tr", l, 1))
                act_f(sguwT, bank(6).rearrange("p (g q) -> p g q", g=BC), ACT.Copy)
                act_f(cw[:, :], bank(7)[:, 0:16 + 2 * KD], ACT.Copy).then_inc(S("wT"), 1)

                def split(s):
                    if s >= CHUNKS:
                        return
                    r = FIRST + s
                    act.wait_ge(raw_full[r % RAWS], full_no[l, r])
                    if s >= 2:
                        act.wait_ge(S("prod"), done_no(l, s - 2))
                    act_f(parts(s, words(s))[0], raw_slab(r, words(s)), ACT.Copy).then_inc(S("w_hi"), 1)

                def branch_hi(q, c, src):
                    act_f(brH[:, c, 0:W(l)], src[:, 0:W(l)], ACT.Copy).then_inc(S("br_hi"), 1)

                def conv_hi(c):
                    for a, b, o in [(0, SEQ, CVL)] + ([(SEQ, TOK, CVC)] if W(l) > SEQ else []):
                        last = act_f(brH[:, c, a:b], cvy[c % 2][:, o:o + b - a], ACT.Copy)
                    last.then_inc(S("br_hi"), 1)

                def gated(q, s0):
                    for d in range(KD):
                        u = q * KD + d
                        if d == 0:
                            act.wait_ge(S("br_lo"), at("br_lo", l, (q + 1) * BC))
                        act.wait_ge(S("g_ps"), at("g_ps", l, u + 1))
                        if u >= 2:
                            act.wait_ge(S("g_prod"), at("g_prod", l, u - 1))
                        act_f(sig[u % 2][:, 0:W(l)], psb(u % 2)[:, 0:W(l)], ACT.Sigmoid).then_inc(S("g_sig"), 1)
                        split(s0 + d + 2)
                        if q == 3 and d:
                            merged_hi(d - 1)

                def merged_hi(d):
                    act.wait_ge(S("g_prod"), at("g_prod", l, 3 * KD + d + 1))
                    act_f(mH[:, d, 0:W(l)], merged[:, d, 0:W(l)], ACT.Copy).then_inc(S("m_hi"), 1)

                split(0)
                split(1)
                steps = [(h, t) for h in range(H) for t in range(NT)]
                rounds = (AT + NT + 3) // 4

                def head_T(h, r):
                    act.wait_ge(S("qk_tr"), at("qk_tr", l, h * rounds + r + 1))
                    if h >= 2 and r == 0:
                        act.wait_ge(S("s_ps"), at("s_ps", l, (h - 1) * NT))
                    n = min(4, AT + NT - 4 * r) * P
                    act_f(qkH[h % 2][0:QK, r * 512:r * 512 + n], psb(3)[0:QK, 512:512 + n], ACT.Copy).then_inc(S("qk_hi"), 1)

                for r in range(rounds):
                    head_T(0, r)
                for n in range(len(steps) + 2):
                    if n < len(steps):
                        h, t = steps[n]
                        lo = 0 if t < LT else SEQ
                        act.wait_ge(S("negmax"), at("negmax", l, n + 1))
                        if n >= 3:
                            act.wait_ge(S("pr_tr"), at("pr_tr", l, n - 2))
                        act_f(probs[n % 3][:, lo:TOK], psb(n % 2)[:, lo:TOK], ACT.Exp, bias=negm[:, n:n + 1],
                              accum_out=rsum[:, n:n + 1]).then_inc(S("probs"), 1)
                        if h + 1 < H and t < rounds:
                            head_T(h + 1, t)
                    if n >= 2 and steps[n - 2][1] < LT:
                        m = n - 2
                        act.wait_ge(S("pr_tr"), at("pr_tr", l, m + 1))
                        if m >= 2:
                            act.wait_ge(S("o_ps"), at("o_ps", l, m - 1))
                        act_f(prT[m % 2][:, 0:SEQ], psb(2)[:, 0:SEQ], ACT.Copy).then_inc(S("prT_a"), 1)
                act.wait_ge(S("o_sb"), at("o_sb", l, len(steps)))
                for c in range(BC):
                    branch_hi(0, c, oT[:, c, :])
                gated(0, G_AT)
                for j in range(4):
                    split(S_V + j + 2)
                act.wait_ge(S("prod"), done_no(l, S_V + 3))
                for t in range(NT):
                    link(act_f(sgv[:, t, :], bank(t), ACT.Gelu_apprx_tanh))
                    act_f(bank(t), sgv[:, t, :], ACT.Square, scale=BW ** -0.5, accum_out=st[:, t:t + 1]).then_inc(S("sv_sq"), 1)
                act.wait_ge(S("sv_eps"), at("sv_eps", l, 1))
                act_f(srt[:, 0:NT], rst[:, 0:NT], ACT.Sqrt).then_inc(S("sv_rt"), 1)
                for g in range(BC):
                    act.wait_ge(S("prod"), done_no(l, S_U + g))
                    act_f(uT[g][:, 0:W(l)], psb((3, 0, 1, 2)[g])[:, 0:W(l)], ACT.Gelu_apprx_tanh).then_inc(S("sgu_u"), 1)
                    split(S_U + g + 2)
                for g in range(BC):
                    act.wait_ge(S("sgu_sum"), at("sgu_sum", l, g + 1))
                    branch_hi(1, g, umix[g % 2])
                gated(1, G_SG)
                for c in range(BC):
                    for j in range(2):
                        w = 3 * c + j
                        act.wait_ge(S("prod"), done_no(l, S_CV + w))
                        if c >= 2:
                            act.wait_ge(S("cv_y"), at("cv_y", l, c - 1))
                        act_f((gcs, gbs)[j][c % 2][:, 0:W(l)], psb(w % 4)[:, 0:W(l)], ACT.Copy).then_inc(S("cv_evac"), 1)
                        split(S_CV + w + 2)
                    if c:
                        act.wait_ge(S("cv_y"), at("cv_y", l, c))
                        conv_hi(c - 1)
                    split(S_CV + 3 * c + 4)
                act.wait_ge(S("cv_y"), at("cv_y", l, BC))
                conv_hi(BC - 1)
                gated(2, G_CV)
                act.wait_ge(S("po_pad"), at("po_pad", l, 1))
                for g in range(BC + 1):
                    if g < BC:
                        act.wait_ge(S("prod"), done_no(l, S_PO + g))
                        if g >= 2:
                            act.wait_ge(S("po_pl"), at("po_pl", l, g - 1))
                        last = act_f(pp[g % 2][:, PLL:PLL + SEQ], psb(g % 2)[:, 0:SEQ], ACT.Copy)
                        if W(l) > SEQ:
                            last = act_f(pp[g % 2][:, PLC:PLC + CTX], psb(g % 2)[:, SEQ:TOK], ACT.Copy)
                        last.then_inc(S("po_pp"), 1)
                        split(S_PO + g + 2)
                    if g >= 1:
                        h = g - 1
                        act.wait_ge(S("po_mix"), at("po_mix", l, h + 1))
                        c = BC - 1 - h
                        act_f(brH[:, c, 0:W(l)], psb(2 + h % 2)[:, 0:W(l)], ACT.Copy, scale=cw[:, 12 + c:13 + c])\
                            .then_inc(S("br_hi"), 1)
                act.wait_ge(S("po_mix"), at("po_mix", l, BC))
                for t in range(NT):
                    if l == 0:
                        src = A["x"][0, t * P:(t + 1) * P, :] if t < LT else A["ctx"][0, (t - LT) * P:(t - LT + 1) * P, :]
                    else:
                        src = x_spill[t * P:(t + 1) * P, :]
                    act.dma_start(x_t[:, t, :], src).then_inc(S("x_back"), 16)
                gated(3, G_PO)
                merged_hi(KD - 1)
                for n in range(KD):
                    act.wait_ge(S("prod"), done_no(l, S_WO + n))
                    if n >= 2:
                        act.wait_ge(S("w_tr"), at("w_tr", l, n - 1))
                    g = 16 + n
                    last = act_f(wsc[n % 2][:, 0:SEQ], psb(n % 2)[:, 0:SEQ], ACT.Copy, scale=cw[:, g:g + 1])
                    if W(l) > SEQ:
                        last = act_f(wsc[n % 2][:, SEQ:TOK], psb(n % 2)[:, SEQ:TOK], ACT.Copy, scale=cw[:, g + KD:g + KD + 1])
                    last.then_inc(S("w_sc"), 1)
                    split(S_WO + n + 2)
                act.wait_ge(S("w_x"), at("w_x", l, KD))
                for t in range(NT):
                    if t:
                        act.wait_ge(S("n2_sq"), at("n2_sq", l, t))
                    act_f(junk, x_t[:, t, :], ACT.Square, scale=D ** -0.5, accum_out=st[:, t:t + 1]).then_inc(S("n2_sq"), 1)
                act.wait_ge(S("n2_eps"), at("n2_eps", l, 1))
                act_f(srt[:, 0:NT], rst[:, 0:NT], ACT.Sqrt).then_inc(S("n2_rt"), 1)
                for t in range(NT):
                    act.wait_ge(S("h2_tok"), at("h2_tok", l, t + 1))
                    act.dma_start(h2_rows[t * P:(t + 1) * P, :], h2tok[t % 3]).then_inc(S(f"h2_st{t % 3}"), 16)
                    act.wait_ge(S("h2_tr"), at("h2_tr", l, t + 1))
                    if t >= 2:
                        act.wait_ge(S("lg_ps"), at("lg_ps", l, t - 1))
                    act_f(h2T[t % 2], psb(t % 2).rearrange("p (k t) -> p k t", k=KD), ACT.Copy).then_inc(S("h2T"), 1)
                act.wait_ge(S("lg_ps"), at("lg_ps", l, NT))
                act_f(lgT[:, 0:W(l)], psb(3)[0:NE, 0:W(l)], ACT.Copy).then_inc(S("lg_sb"), 1)
                act.wait_ge(S("lg_tr"), at("lg_tr", l, 1))
                act_f(r_s[:, 0:NT, :], psb(2)[:, 0:NT * NE].rearrange("p (t e) -> p t e", t=NT), ACT.Sigmoid)\
                    .then_inc(S("r_s"), 1)

                nb = expert_blocks(W(l))

                def silu(b, j, first=False):
                    act.wait_ge(S("h_ps"), at("h_ps", l, b + 1))
                    if not first:
                        act.wait_ge(S("a_sb"), at("a_sb", l, b - 1))
                    act_f(sil[j], psb(1)[:, 0:FF], ACT.Silu).then_inc(S("sil"), 1)

                def rows_T(b, j):
                    act.wait_ge(S("xT_ps"), at("xT_ps", l, b + 1))
                    act_f(xgT[j], psb(0).rearrange("p (k t) -> p k t", k=KD), ACT.Copy).then_inc(S("xgT"), 1)

                def hidden_T(b, j):
                    act.wait_ge(S("aT_ps"), at("aT_ps", l, b + 1))
                    act_f(act_T[j], psb(1)[:, 512:768].rearrange("p (k t) -> p k t", k=2), ACT.Copy).then_inc(S("aT_sb"), 1)

                def store(b, j, dyn=False):
                    act.wait_ge(S("y_sb"), at("y_sb", l, b + 1))
                    dst = y_rows[l][bass.ds(b * P, P), :] if dyn else y_rows[l][b * P:(b + 1) * P, :]
                    act.dma_start(dst, ysb[j]).then_inc(S(f"y_st{j}"), 16)

                rows_T(0, 0)
                for b in range(3):
                    silu(b, b % 2, b < 2)
                    rows_T(b + 1, (b + 1) % 2)
                    hidden_T(b, b % 2)
                    if b >= 2:
                        store(b - 2, b % 2)
                with act.Fori(0, (nb - 3) // 2) as i:
                    for j in range(2):
                        par = (3 + j) % 2
                        b = i * 2 + (3 + j)
                        silu(b, par)
                        rows_T(b + 1, 1 - par)
                        hidden_T(b, par)
                        store(b - 2, par, True)
                for b in (nb - 2, nb - 1):
                    store(b, b % 2)
                for t in range(NT + 3):
                    if t < NT:
                        act.wait_ge(S(f"yg{t % 3}"), at(f"yg{t % 3}", l, 32 * (t // 3 + 1)))
                        if t >= 2:
                            act.wait_ge(S("x_new"), at("x_new", l, t - 1))
                        act_f(ytmp[t % 2], yg[t % 3][0], ACT.Copy, scale=gw[0][:, t:t + 1]).then_inc(S("y_w0"), 1)
                    if l < DEPTH - 1:
                        to_h(l + 1, t)
                    elif 1 <= t <= NT:
                        act.wait_ge(S("x_new"), at("x_new", l, t))
                        act.dma_start(out[0, (t - 1) * P:t * P, :], x_t[:, t - 1, :]).then_inc(S("x_stored"), 16)

        @block.vector
        def _(dve):
            chain = [0]

            def link(ins):
                chain[0] += 1
                ins.then_inc(S("dve_chain"), 1)
                dve.wait_ge(S("dve_chain"), chain[0])

            tt, ts, stt, cp = dve.tensor_tensor, dve.tensor_scalar, dve.scalar_tensor_tensor, dve.tensor_copy

            dve.wait_ge(S("c_hi"), 1)
            tt(scL[:, :], scT[:, :], scH[:, :].bitcast(F32), ALU.subtract).then_inc(S("c_lo"), 1)
            dve.wait_ge(S("const"), 9)

            def mod_part(j, n):
                dve.wait_ge(S("mod_hi"), n)
                tt(mod_lo[j % 3], slot3(j, KD), mod_hi[j % 3].bitcast(F32), ALU.subtract).then_inc(slab_used, 1)

            def mod_out(l, j, n, col):
                dve.wait_ge(S("mod_ps"), n)
                o = mod_sb[l][:, bass.ds(col, 256)]
                tt(o, o, bank(j)[0:2, 0:256], ALU.add).then_inc(S("mod_row"), 1)

            for l in range(DEPTH):
                n = l * MC // 2
                for j in range(SLOTS):
                    mod_part(j, n + j + 1)
                    if l == 0 and j == 1:
                        dve.wait_ge(S("mod_b"), 16 * 2 * DEPTH)
                    if j:
                        mod_out(l, j - 1, n + j, (j - 1) * 256)
                    elif l:
                        mod_out(l - 1, SLOTS - 1, n, N_MOD * D - 256)
                with dve.Fori(1, MC // (2 * SLOTS)) as i:
                    for j in range(SLOTS):
                        mod_part(j, i * SLOTS + (n + j + 1))
                        mod_out(l, (j - 1) % SLOTS, i * SLOTS + (n + j), i * (256 * SLOTS) + (j - 1) * 256)
            mod_out(DEPTH - 1, SLOTS - 1, DEPTH * MC // 2, N_MOD * D - 256)

            def scale_rows(l):
                dve.wait_ge(S("par_n1"), at("par_n1", l, 16 * 3))
                for v in range(2):
                    last = stt(scale1(v), scale1(v), 1.0, gain1, ALU.add, ALU.mult)
                link(last)

            def to_h(l, t):
                if 1 <= t <= AT:
                    dve.wait_ge(S("n1_sq"), at("n1_sq", l, t))
                    ts(rst[:, t - 1:t], st[:, t - 1:t], EPS, None, ALU.add).then_inc(S("n1_eps"), 1)
                if 2 <= t <= AT + 1:
                    u = t - 2
                    v = 0 if u < LT else 1
                    dve.wait_ge(S("n1_rt"), at("n1_rt", l, u + 1))
                    link(dve.reciprocal(rst[:, u:u + 1], srt[:, u:u + 1]))
                    if u >= 2:
                        dve.wait_ge(S("h_tr"), at("h_tr", l, u - 1))
                    link(stt(htok[u % 2], x_t[:, u, :], rst[:, u:u + 1], scale1(v), ALU.mult, ALU.mult))
                    tt(htok[u % 2], htok[u % 2], shift1(v), ALU.add).then_inc(S("h_tok"), 1)
                if 3 <= t < 3 + len(KVQ_SPLIT):
                    i, k0, kn = t - 3, sum(KVQ_SPLIT[:t - 3]), KVQ_SPLIT[t - 3]
                    dve.wait_ge(S("w_hi"), at("w_hi", l, i + 1))
                    tt(kvqL[:, k0:k0 + kn, :], raw_slab(i, kn * KVQ).rearrange("p (k n) -> p k n", k=kn),
                       kvqH[:, k0:k0 + kn, :].bitcast(F32), ALU.subtract).then_inc(S("w_lo"), 1)
                if t >= 3:
                    u = t - 3
                    tok = slice(u * P, (u + 1) * P)
                    dve.wait_ge(S("hT_hi"), at("hT_hi", l, u + 1))
                    tt(hL[:, :, tok], psb(u % 2).rearrange("p (k t) -> p k t", k=KD), hH[:, :, tok].bitcast(F32), ALU.subtract)\
                        .then_inc(S("hT_tile"), 1)

            for l in range(DEPTH):
                NT = tiles(l)
                if l == 0:
                    scale_rows(l)
                    for t in range(AT + 3):
                        to_h(l, t)

                def small_norms(t):
                    full = t < NT
                    b = bank(t)
                    if t >= RB:
                        dve.wait_ge(S("t_qk"), at("t_qk", l, t - RB + 1))
                    if t >= 2:
                        dve.wait_ge(S("cn_tr"), at("cn_tr", l, t - 1))
                    cp(raw[t % RB][:, 0, :, NOPE:QK], b[:, None, KR_OFF:Q_OFF].to_broadcast([P, H, ROPE]))
                    last = stt(cn[t % 2][:, 0:P], b[:, 0:KV_LORA], rst[:, t:t + 1], g_kva, ALU.mult, ALU.mult)
                    if full:
                        last = stt(cn[t % 2][:, P:384], b[:, Q_OFF:CONV_OFF], rst[:, AT + t:AT + t + 1], g_qa, ALU.mult, ALU.mult)
                    last.then_inc(S("cn"), 1)

                def head_squares(t):
                    n = 2 * H if t < NT else H
                    dve.wait_ge(S("t_sqd"), at("t_sqd", l, t + 1))
                    link(dve.tensor_reduce(ssq[t % 2][:, 0:n], qk[:, t].rearrange("p s h e -> p (s h) e")[:, 0:n, :],
                                           AX.X, ALU.add))
                    ts(ssq[t % 2][:, 0:n], ssq[t % 2][:, 0:n], 1.0 / QK, EPS, ALU.mult, ALU.add).then_inc(S("t_ss"), 1)

                def head_norms(t):
                    n = 2 * H if t < NT else H
                    dve.wait_ge(S("t_hrt"), at("t_hrt", l, t + 1))
                    link(dve.reciprocal(rsq[t % 2][:, 0:n], rsq[t % 2][:, 0:n]))
                    r = raw[t % RB].rearrange("p s h e -> p (s h) e")[:, 0:n, :]
                    link(tt(r, r, rsq[t % 2][:, 0:n, None].to_broadcast([P, n, QK]), ALU.mult))
                    for s in range(n // H):
                        last = tt(qk[:, t, s], raw[t % RB][:, s], g_qk[:, s:s + 1, :].to_broadcast([P, H, QK]), ALU.mult)
                    last.then_inc(S("t_gain"), 1)

                if l > 0:
                    dve.wait_ge(S("x_spilled"), 16 * AT)
                dve.wait_ge(S("par_b"), at("par_b", l, 16 * 8))
                dve.wait_ge(S("g_scaled"), at("g_scaled", l, 1))
                dve.wait_ge(S("h_tr"), at("h_tr", l, AT))
                dve.wait_ge(S("t_sq"), at("t_sq", l, 1))
                ts(rst[:, 0:AT + NT], st[:, 0:AT + NT], EPS, None, ALU.add).then_inc(S("t_eps"), 1)
                dve.wait_ge(S("t_rt"), at("t_rt", l, 1))
                link(dve.reciprocal(rst[:, 0:AT + NT], srt[:, 0:AT + NT]))
                for t in range(AT + 3):
                    if t < AT:
                        small_norms(t)
                    if 2 <= t <= AT + 1:
                        head_squares(t - 2)
                    if t >= 3:
                        head_norms(t - 3)

                def split(s):
                    if s >= CHUNKS:
                        return
                    hi, lo = parts(s, words(s))
                    dve.wait_ge(S("w_hi"), split_no(l, s))
                    tt(lo, raw_slab(FIRST + s, words(s)), hi.bitcast(F32), ALU.subtract).then_inc(S("w_lo"), 1)

                def branch_lo(q, c, src):
                    dve.wait_ge(S("br_hi"), at("br_hi", l, q * BC + c + 1))
                    tt(brL[:, c, 0:W(l)], src[:, 0:W(l)], brH[:, c, 0:W(l)].bitcast(F32), ALU.subtract).then_inc(S("br_lo"), 1)

                def gated(q, s0):
                    for d in range(KD):
                        u = q * KD + d
                        dve.wait_ge(S("prod"), done_no(l, s0 + d))
                        dve.wait_ge(S("g_sig"), at("g_sig", l, u + 1))
                        o = merged[:, d, 0:W(l)]
                        if q == 0:
                            tt(o, sig[u % 2][:, 0:W(l)], psb(2 + u % 2)[:, 0:W(l)], ALU.mult).then_inc(S("g_prod"), 1)
                        else:
                            dve.wait_ge(S("g_prod"), at("g_prod", l, u))
                            link(tt(prod[:, 0:W(l)], sig[u % 2][:, 0:W(l)], psb(2 + u % 2)[:, 0:W(l)], ALU.mult))
                            tt(o, o, prod[:, 0:W(l)], ALU.add).then_inc(S("g_prod"), 1)
                        split(s0 + d + 2)
                        if q == 3 and d:
                            merged_lo(d - 1)

                def merged_lo(d):
                    dve.wait_ge(S("m_hi"), at("m_hi", l, d + 1))
                    tt(mL[:, d, 0:W(l)], merged[:, d, 0:W(l)], mH[:, d, 0:W(l)].bitcast(F32), ALU.subtract).then_inc(S("m_lo"), 1)

                split(0)
                split(1)
                steps = [(h, t) for h in range(H) for t in range(NT)]
                rounds = (AT + NT + 3) // 4

                def head_lo(h, r):
                    dve.wait_ge(S("qk_hi"), at("qk_hi", l, h * rounds + r + 1))
                    n = min(4, AT + NT - 4 * r) * P
                    tt(qkL[h % 2][0:QK, r * 512:r * 512 + n], psb(3)[0:QK, 512:512 + n],
                       qkH[h % 2][0:QK, r * 512:r * 512 + n].bitcast(F32), ALU.subtract).then_inc(S("qkT"), 1)

                for r in range(rounds):
                    head_lo(0, r)
                for n in range(len(steps) + 3):
                    if n < len(steps):
                        h, t = steps[n]
                        if t and t <= rounds and h + 1 < H:
                            head_lo(h + 1, t - 1)
                        lo = 0 if t < LT else SEQ
                        dve.wait_ge(S("s_ps"), at("s_ps", l, n + 1))
                        dve.tensor_reduce(negm[:, n:n + 1], psb(n % 2)[:, lo:TOK], AX.X, ALU.max, negate=True)\
                            .then_inc(S("negmax"), 1)
                    if 1 <= n <= len(steps):
                        m = n - 1
                        lo = 0 if steps[m][1] < LT else SEQ
                        dve.wait_ge(S("probs"), at("probs", l, m + 1))
                        link(dve.reciprocal(rinv[:, m:m + 1], rsum[:, m:m + 1]))
                        ts(probs[m % 3][:, lo:TOK], probs[m % 3][:, lo:TOK], rinv[:, m:m + 1], None, ALU.mult).then_inc(S("p_norm"), 1)
                    if 2 <= n <= len(steps) + 1:
                        m = n - 2
                        h, t = steps[m]
                        dve.wait_ge(S("pr_tr"), at("pr_tr", l, m + 1))
                        if m >= 2:
                            dve.wait_ge(S("o_ps"), at("o_ps", l, m - 1))
                        cp(prT[m % 2][:, SEQ:TOK], psb(2)[:, SEQ:TOK]).then_inc(S("prT_d"), 1)
                    if n >= 3:
                        m = n - 3
                        h, t = steps[m]
                        dve.wait_ge(S("o_ps"), at("o_ps", l, m + 1))
                        c0 = h % 2 * VD
                        cp(oT[c0:c0 + VD, h // 2, t * P:(t + 1) * P], psb(3)[0:VD, (m % 2) * P:(m % 2 + 1) * P])\
                            .then_inc(S("o_sb"), 1)
                for c in range(BC):
                    branch_lo(0, c, oT[:, c, :])
                gated(0, G_AT)

                for j in range(4):
                    split(S_V + j + 2)
                dve.wait_ge(S("sv_sq"), at("sv_sq", l, NT))
                ts(rst[:, 0:NT], st[:, 0:NT], EPS, None, ALU.add).then_inc(S("sv_eps"), 1)
                dve.wait_ge(S("sv_rt"), at("sv_rt", l, 1))
                link(dve.reciprocal(rst[:, 0:NT], srt[:, 0:NT]))
                for t in range(NT):
                    stt(sgv[:, t, :], sgv[:, t, :], rst[:, t:t + 1], g_sgu, ALU.mult, ALU.mult).then_inc(S("sgv"), 1)
                for g in range(BC):
                    split(S_U + g + 2)
                dve.wait_ge(S("par_sb"), at("par_sb", l, 16))
                for g in range(BC + 1):
                    if g < BC:
                        dve.wait_ge(S("sgu_mix"), at("sgu_mix", l, g + 1))
                        m3 = psb((3, 0, 1, 2)[g])[:, 0:W(l)].rearrange("p (t q) -> p t q", q=P)
                        um = umix[g % 2][:, 0:W(l)]
                        if g >= 2:
                            dve.wait_ge(S("br_lo"), at("br_lo", l, BC + g - 1))
                        link(tt(um.rearrange("p (t q) -> p t q", q=P), m3,
                                sgub[:, None, g * P:(g + 1) * P].to_broadcast([P, NT, P]), ALU.add))
                        tt(um, um, uT[g][:, 0:W(l)], ALU.mult).then_inc(S("sgu_sum"), 1)
                    if g >= 1:
                        branch_lo(1, g - 1, umix[(g - 1) % 2])
                gated(1, G_SG)

                dve.memset(cup[0], 0.0)
                link(dve.memset(cup[1], 0.0))
                cstreams = [(0, SEQ, CVL)] + ([(SEQ, TOK, CVC)] if W(l) > SEQ else [])
                hi_ = CVC + CTX if W(l) > SEQ else CVL + SEQ

                def conv_lo(c):
                    dve.wait_ge(S("br_hi"), at("br_hi", l, 2 * BC + c + 1))
                    for a, b, o in cstreams:
                        last = tt(brL[:, c, a:b], cvy[c % 2][:, o:o + b - a], brH[:, c, a:b].bitcast(F32), ALU.subtract)
                    last.then_inc(S("br_lo"), 1)

                for c in range(BC):
                    w = 3 * c + 2
                    split(S_CV + 3 * c + 2)
                    split(S_CV + 3 * c + 3)
                    if c:
                        conv_lo(c - 1)
                    dve.wait_ge(S("prod"), done_no(l, S_CV + w))
                    dve.wait_ge(S("cv_evac"), at("cv_evac", l, 2 * c + 2))
                    cu = cup[c % 2]
                    for a, b, o in cstreams:
                        last = tt(cu[:, o:o + b - a], gcs[c % 2][:, a:b], psb(w % 4)[:, a:b], ALU.mult)
                    last.then_inc(S("cv_cu"), 1)
                    split(S_CV + 3 * c + 4)
                    dve.wait_ge(S("cv_cu"), at("cv_cu", l, c + 1))
                    if c >= 2:
                        dve.wait_ge(S("br_lo"), at("br_lo", l, 2 * BC + c - 1))
                    y = cvy[c % 2][:, 1:hi_]
                    link(ts(y, cu[:, 1:hi_], cw[:, 4 + c:5 + c], None, ALU.mult))
                    link(stt(y, cu[:, 0:hi_ - 1], cw[:, c:c + 1], y, ALU.mult, ALU.add))
                    link(stt(y, cu[:, 2:hi_ + 1], cw[:, 8 + c:9 + c], y, ALU.mult, ALU.add))
                    for a, b, o in cstreams:
                        z = cvy[c % 2][:, o:o + b - a]
                        last = tt(z, z, gbs[c % 2][:, a:b], ALU.mult)
                    last.then_inc(S("cv_y"), 1)
                conv_lo(BC - 1)
                gated(2, G_CV)

                dve.wait_ge(S("const_dma"), 48)
                for j in range(2):
                    last = dve.memset(pp[j], 0.0)
                last.then_inc(S("po_pad"), 1)
                pstreams = [(0, SEQ, PLL)] + ([(SEQ, TOK, PLC)] if W(l) > SEQ else [])

                def pool_lo(h):
                    dve.wait_ge(S("br_hi"), at("br_hi", l, 3 * BC + h + 1))
                    c = BC - 1 - h
                    stt(brL[:, c, 0:W(l)], psb(2 + h % 2)[:, 0:W(l)], cw[:, 12 + c:13 + c], brH[:, c, 0:W(l)].bitcast(F32),
                        ALU.mult, ALU.subtract).then_inc(S("br_lo"), 1)

                for g in range(BC):
                    win_ = WINDOWS[BC - 1 - g]
                    split(S_PO + g + 2)
                    dve.wait_ge(S("po_pp"), at("po_pp", l, g + 1))
                    if g:
                        dve.wait_ge(S("po_pl"), at("po_pl", l, g))
                    src, lo, k = pp[g % 2], 1, 1
                    link(tt(pacc[0][:, 1:PLW], src[:, 0:PLW - 1], src[:, 1:PLW], ALU.add))
                    cur, lo, hi = 0, 1, PLW
                    while 2 * k < win_:
                        link(tt(pacc[1 - cur][:, lo + k:hi - k], pacc[cur][:, lo:hi - 2 * k], pacc[cur][:, lo + 2 * k:hi], ALU.add))
                        cur, lo, hi, k = 1 - cur, lo + k, hi - k, 2 * k
                    s_ = pacc[cur]
                    e = edge[:, (BC - 1 - g) * 2 * PP:(BC - g) * 2 * PP]
                    for a, b, o in pstreams:
                        n = b - a
                        tt(s_[:, o:o + PP], s_[:, o:o + PP], e[:, 0:PP], ALU.mult)
                        last = tt(s_[:, o + n - PP:o + n], s_[:, o + n - PP:o + n], e[:, PP:2 * PP], ALU.mult)
                    link(last)
                    if g >= 2:
                        dve.wait_ge(S("po_mix"), at("po_mix", l, g - 1))
                    for a, b, o in pstreams:
                        last = stt(pooled[g % 2][:, a:b], s_[:, o:o + b - a], 1.0 / win_, src[:, o:o + b - a], ALU.mult, ALU.subtract)
                    last.then_inc(S("po_pl"), 1)
                    if g:
                        pool_lo(g - 1)
                pool_lo(BC - 1)
                gated(3, G_PO)
                merged_lo(KD - 1)

                dve.wait_ge(S("x_back"), at("x_back", l, 16 * NT))
                for n in range(KD):
                    split(S_WO + n + 2)
                    dve.wait_ge(S("w_tr"), at("w_tr", l, n + 1))
                    xs = x_t[:, 0:NT, n * P:(n + 1) * P]
                    tt(xs, xs, psb(2 + n % 2)[:, 0:W(l)].rearrange("p (t c) -> p t c", c=P), ALU.add).then_inc(S("w_x"), 1)
                dve.wait_ge(S("par_n2"), at("par_n2", l, 16 * 3))
                for v in range(2):
                    last = stt(mrow[:, v, 1, :], mrow[:, v, 1, :], 1.0, gain2, ALU.add, ALU.mult)
                dve.wait_ge(S("n2_sq"), at("n2_sq", l, NT))
                ts(rst[:, 0:NT], st[:, 0:NT], EPS, None, ALU.add).then_inc(S("n2_eps"), 1)
                dve.wait_ge(S("n2_rt"), at("n2_rt", l, 1))
                link(dve.reciprocal(rst[:, 0:NT], srt[:, 0:NT]))
                for t in range(NT):
                    v = 0 if t < LT else 1
                    if t >= 3:
                        dve.wait_ge(S("h2_tr"), at("h2_tr", l, t - 2))
                        dve.wait_ge(S(f"h2_st{t % 3}"), at(f"h2_st{t % 3}", l, 16 * (t // 3)))
                    link(stt(h2tok[t % 3], x_t[:, t, :], rst[:, t:t + 1], mrow[:, v, 1, :], ALU.mult, ALU.mult))
                    tt(h2tok[t % 3], h2tok[t % 3], mrow[:, v, 0, :], ALU.add).then_inc(S("h2_tok"), 1)

                s, sbv, m_, sc = (a[:, 0:NT, :] for a in (r_s, r_sb, r_m, r_sc))
                oh = [a[:, 0:NT, :] for a in r_oh]

                def bc(a, n):
                    return a[:, :, None].to_broadcast([P, a.shape[1], n])

                dve.wait_ge(S("r_s"), at("r_s", l, 1))
                dve.wait_ge(S("const"), 9)
                link(tt(sbv, s, rbias[:, None, :].to_broadcast([P, NT, NE]), ALU.add))
                g3 = sbv.rearrange("p t (g e) -> p (t g) e", g=NG)
                pr = r_pair[:, 0:NT * NG, :]
                tt(pr[:, :, 0:3], g3[:, :, 0:3], g3[:, :, 1:4], ALU.add)
                tt(pr[:, :, 3:5], g3[:, :, 0:2], g3[:, :, 2:4], ALU.add)
                link(tt(pr[:, :, 5:6], g3[:, :, 0:1], g3[:, :, 3:4], ALU.add))
                gs, gq, gm = (a[:, 0:NT, :] for a in (r_gs, r_gq, r_gm))
                mx = r_mx[:, 0:NT]
                link(dve.tensor_reduce(gs.rearrange("p t g -> p (t g)"), pr, AX.X, ALU.max))

                def first_max(dst, src, weights, tmp, n):
                    link(dve.tensor_reduce(mx, src, AX.X, ALU.max))
                    link(tt(tmp, src, bc(mx, n), ALU.is_ge))
                    link(tt(tmp, tmp, weights[:, None, :].to_broadcast([P, NT, n]), ALU.mult))
                    link(dve.tensor_reduce(mx, tmp, AX.X, ALU.max))
                    link(tt(dst, tmp, bc(mx, n), ALU.is_equal))

                first_max(gm, gs, w4, gq, NG)
                link(ts(gq, gm, BIG, -BIG, ALU.mult, ALU.add))
                m3 = m_.rearrange("p t (g e) -> p (t g) e", g=NG)
                link(tt(m3, g3, bc(gm.rearrange("p t g -> p (t g)"), EG), ALU.mult))
                link(tt(m3, m3, bc(gq.rearrange("p t g -> p (t g)"), EG), ALU.add))
                first_max(oh[0], m_, w16, sc, NE)
                link(stt(m_, oh[0], -3.0e38, m_, ALU.mult, ALU.add))
                first_max(oh[1], m_, w16, sc, NE)
                dve.memset(r_any[:, NT, :], 0.0)
                tt(r_any[:, 0:NT, :], oh[0], oh[1], ALU.add).then_inc(S("r_oh"), 1)
                for k in range(2):
                    link(tt(sc, oh[k], s, ALU.mult))
                    link(dve.tensor_reduce(gw[k][:, 0:NT], sc, AX.X, ALU.add))
                link(tt(r_den[:, 0:NT], gw[0][:, 0:NT], gw[1][:, 0:NT], ALU.add))
                link(dve.reciprocal(r_den[:, 0:NT], r_den[:, 0:NT]))
                for k in range(2):
                    tt(gw[k][:, 0:NT], gw[k][:, 0:NT], r_den[:, 0:NT], ALU.mult)
                nb = expert_blocks(W(l))
                dve.wait_ge(S("rank_ps"), at("rank_ps", l, 1))
                cnt = psb(2)[:, NT * NE:(NT + 1) * NE]
                link(tt(r_cnt, cnt[:, :, None].to_broadcast([P, NE, 6]), steps6[:, None, :].to_broadcast([P, NE, 6]), ALU.is_gt))
                link(dve.tensor_reduce(r_nb, r_cnt, AX.X, ALU.add))
                link(dve.tensor_tensor_scan(r_end, ones[:, 0:NE], r_nb, 0.0, ALU.mult, ALU.add))
                link(tt(r_base, r_end, r_nb, ALU.subtract))
                link(ts(r_base, r_base, float(P), None, ALU.mult))
                link(tt(m_, psb(2)[:, 0:NT * NE].rearrange("p (t e) -> p t e", t=NT), r_base[:, None, :].to_broadcast([P, NT, NE]), ALU.add))
                for k in range(2):
                    link(tt(sc, m_, oh[k], ALU.mult))
                    link(dve.tensor_reduce(r_slot[:, k, 0:NT], sc, AX.X, ALU.add))
                cp(slot_i[:, :], r_slot.rearrange("p k t -> p (k t)")).then_inc(S("slots"), 1) if NT == AT else \
                    cp(slot_i[:, :].rearrange("p (k t) -> p k t", k=2)[:, :, 0:NT], r_slot[:, :, 0:NT]).then_inc(S("slots"), 1)
                blk = r_blk[:, 0:nb, :]
                link(tt(blk, r_end[:, None, :].to_broadcast([P, nb, NE]), blkno[:, 0:nb, None].to_broadcast([P, nb, NE]), ALU.is_le))
                link(dve.tensor_reduce(r_eid[:, 0:nb], blk, AX.X, ALU.add))
                link(ts(r_eid[:, 0:nb], r_eid[:, 0:nb], float(NE - 1), None, ALU.min))
                cp(eid_i[:, 0:nb], r_eid[:, 0:nb]).then_inc(S("eid"), 1)
                for k in range(2):
                    tt(ge_blk[:, k, 0:NT, 0:nb + 2], blk0[:, None, 0:nb + 2].to_broadcast([P, NT, nb + 2]),
                       r_slot[:, k, 0:NT, None].to_broadcast([P, NT, nb + 2]), ALU.is_le).then_inc(S("dve_chain"), 1)
                chain[0] += 2
                dve.wait_ge(S("dve_chain"), chain[0])
                for k in range(2):
                    tt(tok_blk[:, k, 0:NT, 0:nb + 1], ge_blk[:, k, 0:NT, 0:nb + 1], ge_blk[:, k, 0:NT, 1:nb + 2], ALU.subtract)
                    link(dve.tensor_reduce(r_place[:, k, 0:NT], ge_blk[:, k, 0:NT, 1:nb + 2], AX.X, ALU.add))
                for k in range(2):
                    tt(tok_blk[:, k, 0:NT, 0:nb + 1], tok_blk[:, k, 0:NT, 0:nb + 1],
                       tokf[:, 0:NT, None].to_broadcast([P, NT, nb + 1]), ALU.mult)
                    link(stt(r_place[:, k, 0:NT], r_place[:, k, 0:NT], float(-P), r_slot[:, k, 0:NT], ALU.mult, ALU.add))
                for k in range(2):
                    ins = tt(at_place[:, k, 0:NT, :], placeno[:, None, :].to_broadcast([P, NT, P]),
                             r_place[:, k, 0:NT, None].to_broadcast([P, NT, P]), ALU.is_equal)
                ins.then_inc(S("tab_oh"), 1)
                dve.wait_ge(S("tab_ps"), at("tab_ps", l, 1))
                cp(tab_i[:, 0:nb + 1], psb(3)[:, 0:nb + 1]).then_inc(S("tab_i"), 1)

                def hidden(b, j, first=False):
                    dve.wait_ge(S("sil"), at("sil", l, b + 1))
                    if not first:
                        dve.wait_ge(S("aT_ps"), at("aT_ps", l, b - 1))
                    tt(act_a[j], sil[j], psb(1)[:, FF:2 * FF], ALU.mult).then_inc(S("a_sb"), 1)

                def rows_out(b, j, stored=None):
                    dve.wait_ge(S("y_ps"), at("y_ps", l, b + 1))
                    if stored is not None:
                        dve.wait_ge(S(f"y_st{j}"), at(f"y_st{j}", l, stored))
                    cp(ysb[j], psb(2 + j)).then_inc(S("y_sb"), 1)

                for b in range(3):
                    hidden(b, b % 2, b < 2)
                    if b:
                        rows_out(b - 1, (b - 1) % 2)
                with dve.Fori(0, (nb - 3) // 2) as i:
                    for j in range(2):
                        par = (3 + j) % 2
                        b = i * 2 + (3 + j)
                        hidden(b, par)
                        rows_out(b - 1, 1 - par, i * 16 + 16)
                rows_out(nb - 1, (nb - 1) % 2, 16 * ((nb - 1) // 2))

                dve.wait_ge(S("par_g2"), at("par_g2", l, 16))
                if l < DEPTH - 1:
                    scale_rows(l + 1)
                for t in range(NT + 3):
                    if t < NT:
                        v = 0 if t < LT else 1
                        y = ytmp[t % 2]
                        dve.wait_ge(S(f"yg{t % 3}"), at(f"yg{t % 3}", l, 32 * (t // 3 + 1)))
                        dve.wait_ge(S("y_w0"), at("y_w0", l, t + 1))
                        stt(y, yg[t % 3][1], gw[1][:, t:t + 1], y, ALU.mult, ALU.add).then_inc(S("yg_free"), 1)
                        dve.wait_ge(S("yg_free"), at("yg_free", l, t + 1))
                        link(tt(y, y, grow[:, v, :], ALU.mult))
                        tt(x_t[:, t, :], x_t[:, t, :], y, ALU.add).then_inc(S("x_new"), 1)
                    if l < DEPTH - 1:
                        to_h(l + 1, t)

        @block.gpsimd
        def _(pool):
            chain = [0]

            def link(ins):
                chain[0] += 1
                ins.then_inc(S("pool_chain"), 1)
                pool.wait_ge(S("pool_chain"), chain[0])

            pool.dma_start(T[0:KD, P:2 * P], A["c"][0].rearrange("(k p) -> k p", p=P)).then_inc(S("c_rows"), 16)
            pool.dma_start(T[KD:2 * KD, P:2 * P], A["c_ctx"].rearrange("(k p) -> k p", p=P)).then_inc(S("c_rows"), 16)
            link(pool.memset(ident[:, :], 0.0))
            pool.affine_select(out=ident[:, :], in_=ident[:, :], compare_op=ALU.not_equal, fill=1.0, base=0,
                               pattern=[[-1, P]], channel_multiplier=1).then_inc(S("const"), 1)
            link(pool.memset(ones[:, :], 1.0))
            pool.affine_select(out=tri[:, :], in_=ones[:, :], compare_op=ALU.is_gt, fill=0.0, base=0,
                               pattern=[[1, P]], channel_multiplier=-1).then_inc(S("const"), 1)
            for l in range(DEPTH):
                for v in range(2):
                    pool.dma_start(mod_sb[l][v:v + 1, :], A["mod_b"][l].rearrange("(a n) -> a n", a=1)).then_inc(S("mod_b"), 16)
            pool.dma_start(rwv, A["router_w"].rearrange("(k p) e -> p k e", p=P)).then_inc(S("const_dma"), 16)
            pool.dma_start(rbias[:, :], A["router_b"].rearrange("(a e) -> a e", a=1).partition_broadcast(P)).then_inc(S("const_dma"), 16)
            pool.dma_start(edge[:, :], A["edges"].rearrange("g e -> (g e)").rearrange("(a n) -> a n", a=1).partition_broadcast(P))\
                .then_inc(S("const_dma"), 16)

            def counter(dst, at_, n, base, step, channel):
                link(pool.iota(iint[:, at_:at_ + n], [[step, n]], base=base, channel_multiplier=channel))
                pool.tensor_copy(dst, iint[:, at_:at_ + n]).then_inc(S("const"), 1)

            counter(w4[:, :], 0, NG, NG, -1, 0)
            counter(w16[:, :], 4, NE, NE, -1, 0)
            counter(steps6[:, :], 20, 6, 0, P, 0)
            counter(blkno[:, :], 26, MAXB, 0, 1, 0)
            counter(tokf[:, :], 56, AT, 0, P, 1)
            counter(blk0[:, :], 64, MAXB + 2, 0, P, 0)
            counter(placeno[:, :], 96, P, 0, 1, 0)
            def row(a):
                return a.rearrange("(a n) -> a n", a=1).partition_broadcast(P)

            def norm_rows(l):
                for v in range(2):
                    pool.dma_start(MGZ[:, v * 2 * D:(v + 1) * 2 * D], row(mod_rows[l, v, 0:2 * D])).then_inc(S("par_n1"), 16)
                pool.dma_start(gain1, row(A["norm1_g"][l])).then_inc(S("par_n1"), 16)

            def parameters(l):
                pool.dma_start(g_qk[:, 0, :], row(A["k_norm_g"][l])).then_inc(S("par_g"), 16)
                pool.dma_start(g_qk[:, 1, :], row(A["q_norm_g"][l])).then_inc(S("par_g"), 16)
                for dst, src in ((g_kva, row(A["kv_a_norm_g"][l])), (g_qa, row(A["q_a_norm_g"][l])),
                                 (g_sgu, row(A["sgu_norm_g"][l])),
                                 (sguw, A["sgu_w"][l].rearrange("g p q -> p g q")),
                                 (crow[0:12, :], A["conv_w"][l].rearrange("k (c p) -> (k c) p", p=P)),
                                 (crow[12:16, :], A["pool_scale"][l].rearrange("(c p) -> c p", p=P)),
                                 (crow[16:24, :], mod_rows[l, 0, 2 * D:3 * D].rearrange("(c p) -> c p", p=P)),
                                 (crow[24:32, :], mod_rows[l, 1, 2 * D:3 * D].rearrange("(c p) -> c p", p=P))):
                    pool.dma_start(dst, src).then_inc(S("par_b"), 16)
                pool.dma_start(sgub, row(A["sgu_b"][l].rearrange("g q -> (g q)"))).then_inc(S("par_sb"), 16)
                pool.wait_ge(S("par_g"), at("par_g", l, 32))
                pool.tensor_scalar(g_qk[:, 1, :], g_qk[:, 1, :], SCALE, None, ALU.mult).then_inc(S("g_scaled"), 1)

            for l in range(DEPTH):
                pool.wait_ge(S("mod_row"), (l + 1) * MC // 2)
                pool.dma_start(mod_rows[l], mod_sb[l]).then_inc(S("mod_st"), 16)
                pool.wait_ge(S("mod_st"), 16 * (l + 1))
                if l == 0:
                    norm_rows(0)
            parameters(0)
            for l in range(DEPTH):
                NT = tiles(l)
                if l > 0:
                    pool.wait_ge(S("x_new"), at("x_new", l - 1, tiles(l - 1)))
                pool.dma_start(T[:, 1536:1792], A["rope"].rearrange("p s t e -> p (s t e)")).then_inc(S("par_r"), 16)
                pool.wait_ge(S("par_r"), 16 * (l + 1))

                def rotate(t):
                    pool.wait_ge(S("t_gain"), at("t_gain", l, t + 1))
                    if t >= LT:
                        pool.sem_inc(S("t_qk"), 1)
                        return
                    n = 2 * H
                    r = qk[:, t].rearrange("p s h e -> p (s h) e")[:, :, NOPE:QK]
                    free_ = raw[t % RB].rearrange("p s h e -> p (s h e)")
                    t1, t2 = (free_[:, j * n * ROPE:(j + 1) * n * ROPE].rearrange("p (h e) -> p h e", h=n) for j in range(2))
                    pool.tensor_tensor(t1, r, cosv[:, t:t + 1, :].to_broadcast([P, n, ROPE]), ALU.mult)
                    link(pool.tensor_tensor(t2, r, sinv[:, t:t + 1, :].to_broadcast([P, n, ROPE]), ALU.mult))
                    pool.tensor_tensor(r[:, :, 0:HALF], t1[:, :, 0:HALF], t2[:, :, HALF:ROPE], ALU.subtract)
                    pool.tensor_tensor(r[:, :, HALF:ROPE], t2[:, :, 0:HALF], t1[:, :, HALF:ROPE], ALU.add).then_inc(S("t_qk"), 1)

                for t in range(AT):
                    rotate(t)

                pool.wait_ge(S("o_sb"), at("o_sb", l, H * NT))
                pool.wait_ge(S("g_prod"), at("g_prod", l, 2 * KD))
                pool.dma_start(poolw, A["pool_w"][l].rearrange("g c d -> c g d")).then_inc(S("par_p"), 16)
                pool.wait_ge(S("prod"), done_no(l, S_WO - 1))
                for v in range(2):
                    pool.dma_start(HTF[:, v * 2 * D:(v + 1) * 2 * D], row(mod_rows[l, v, 3 * D:5 * D])).then_inc(S("par_n2"), 16)
                pool.dma_start(gain2, row(A["norm2_g"][l])).then_inc(S("par_n2"), 16)
                pool.wait_ge(S("w_tr"), at("w_tr", l, KD))
                pool.dma_start(T[:, 0:2 * D], mod_rows[l, :, 5 * D:6 * D].rearrange("(a v) d -> a v d", a=1).partition_broadcast(P))\
                    .then_inc(S("par_g2"), 16)

                pool.wait_ge(S("tab_i"), at("tab_i", l, 1))
                for t in range(3):
                    pool.wait_ge(S(f"h2_st{t}"), at(f"h2_st{t}", l, 16 * ((NT + 2 - t) // 3)))
                pool.wait_ge(S("h2_tr"), at("h2_tr", l, NT))
                nb = expert_blocks(W(l))

                def gather(b, j, n, dyn=False):
                    src = tab_i[:, bass.ds(b, 1)] if dyn else tab_i[:, b:b + 1]
                    pool.tensor_copy(idx_i[j][:, :], src).then_inc(S("idx"), 1)
                    pool.wait_ge(S("idx"), at("idx", l, n + 1))
                    pool.sem_inc(S("idx_seen"), 1)
                    pool.indirect_dma_start(out=xg[j], out_offset=None, in_=h2_rows,
                                            in_offset=bass.IndirectOffsetOnAxis(idx_i[j][:, :], 0)).then_inc(S(f"xg{j}"), 16)

                gather(0, 0, 0)
                gather(1, 1, 1)
                with pool.Fori(0, (nb - 1) // 2) as i:
                    for j in range(2):
                        pool.wait_ge(S("xT_ps"), at("xT_ps", l, i * 2 + (1 + j)))
                        gather(i * 2 + (2 + j), j, i * 2 + (2 + j), True)
                if l + 1 < DEPTH:
                    norm_rows(l + 1)
                    parameters(l + 1)
                for j in range(2):
                    pool.wait_ge(S(f"y_st{j}"), at(f"y_st{j}", l, 16 * ((nb + 1 - j) // 2)))
                for t in range(NT):
                    j = t % 3
                    if t >= 3:
                        pool.wait_ge(S("yg_free"), at("yg_free", l, t - 2))
                    for k in range(2):
                        c = k * AT + t
                        pool.indirect_dma_start(out=yg[j][k], out_offset=None, in_=y_rows[l],
                                                in_offset=bass.IndirectOffsetOnAxis(slot_i[:, c:c + 1], 0)).then_inc(S(f"yg{j}"), 16)
        return len(sems)


_INS = ["x", "c", "ctx", "c_ctx", "mod_w", "mod_b", "norm1_g", "norm2_g", "w_in", "kv_a_norm_g", "w_ukv", "k_norm_g",
        "q_a_norm_g", "w_uq", "q_norm_g", "conv_w", "pool_w", "pool_scale", "sgu_norm_g", "sgu_w", "sgu_b",
        "w_branch", "w_o", "router_w", "router_b", "moe_w1", "moe_w3", "moe_w2"]


def kernel(**inputs):
    import concourse.bacc as bacc
    from concourse.bass_utils import run_bass_kernel_spmd

    nc = bacc.Bacc("TRN2", target_bir_lowering=False, num_devices=1)
    arrays, aps = {}, {}
    tables = {"rope": rope_tables(), "edges": pool_edges()}
    for name in _INS + list(tables):
        a = np.ascontiguousarray(tables[name] if name in tables else inputs[name])
        arrays[f"in_{name}"] = a
        aps[name] = nc.dram_tensor(f"in_{name}", a.shape, mybir.dt.from_np(a.dtype), kind="ExternalInput").ap()
    out = nc.dram_tensor("out", [1, SEQ, D], F32, kind="ExternalOutput").ap()
    trunk(nc, aps, out)
    r = run_bass_kernel_spmd(nc, [arrays], core_ids=[0])
    return r.results[0]["out"]
```
